# Optimizing a Trainium2 kernel written in Bass

```python
import math
import jax
import jax.numpy as jnp
from jax import lax
import numpy as np
import jax, jax.numpy as jnp

D_MODEL = 1024
BATCH = 1
SEQ = 256
DEPTH = 2

MEM_LEN = 256
D_RG = 1024
RG_BLOCKS = 4
RG_BLOCK = D_RG // RG_BLOCKS
RG_C = 8.0
CONV_W = 4
D_ML = 1024
ML_HEADS = 4
ML_HEAD_DIM = D_ML // ML_HEADS
ML_CHUNK = 128
D_XA = 1024
XA_HEADS = 4
XA_HEAD_DIM = D_XA // XA_HEADS
N_BRANCH = 3
N_IN = 2 * D_RG + 2 * D_ML + 2 * ML_HEADS + D_XA + N_BRANCH * D_MODEL
D_FF = 3584
N_EXPERTS = 8
TOP_K = 2
MOE_BLOCK = 128
N_DENSE = (DEPTH + 1) // 2
N_MOE = DEPTH // 2
EPS = 1e-6


def rms_norm(x, g):
    xf = x.astype(jnp.float32)
    y = xf * lax.rsqrt(jnp.mean(xf * xf, axis=-1, keepdims=True) + EPS)
    return (y * g.astype(jnp.float32)).astype(x.dtype)

def causal_dwconv(x, w, b):
    C = x.shape[-1]
    y = lax.conv_general_dilated(
        x, w[:, None, :].astype(x.dtype), window_strides=(1,),
        padding=[(w.shape[0] - 1, 0)], dimension_numbers=("NWC", "WIO", "NWC"),
        feature_group_count=C)
    return y + b

def block_diag(x, w):
    G, bi, bo = w.shape
    xs = x.reshape(*x.shape[:-1], G, bi)
    return jnp.einsum("...gi,gio->...go", xs, w).reshape(*x.shape[:-1], G * bo)

def split_columns(z):
    sizes = [D_RG, D_RG, D_ML, D_ML, ML_HEADS, ML_HEADS, D_XA, N_BRANCH * D_MODEL]
    out = []
    off = 0
    for s in sizes:
        out.append(z[..., off:off + s])
        off += s
    return out

def rg_lru(x, w_a, b_a, w_x, b_x, lam):
    xf = x.astype(jnp.float32)
    r = jax.nn.sigmoid(block_diag(x, w_a).astype(jnp.float32) + b_a.astype(jnp.float32))
    i = jax.nn.sigmoid(block_diag(x, w_x).astype(jnp.float32) + b_x.astype(jnp.float32))
    log_a = -RG_C * r * jax.nn.softplus(-lam.astype(jnp.float32))
    a = jnp.exp(log_a)
    b_term = jnp.sqrt(-jnp.expm1(2.0 * log_a)) * (i * xf)

    def combine(left, right):
        a1, b1 = left
        a2, b2 = right
        return a1 * a2, a2 * b1 + b2

    _, h = lax.associative_scan(combine, (a, b_term), axis=1)
    return h.astype(x.dtype)

def mlstm_chunkwise(q, k, v, i_pre, f_pre):
    B, S, H, d = q.shape
    L = ML_CHUNK
    NC = S // L

    def to_chunks(t):
        t = t.reshape(B, NC, L, H, *t.shape[3:])
        return jnp.moveaxis(t, (1, 3), (0, 2))

    qc, kc, vc = to_chunks(q), to_chunks(k), to_chunks(v)
    ic = to_chunks(i_pre)
    lfc = to_chunks(jax.nn.log_sigmoid(f_pre))
    causal = jnp.tril(jnp.ones((L, L), dtype=bool))

    def step(carry, inp):
        C, n, m = carry
        qb, kb, vb, ib, lf = inp
        b = jnp.cumsum(lf, axis=-1)
        g = b + m[..., None]
        D = b[..., :, None] - b[..., None, :] + ib[..., None, :]
        D = jnp.where(causal, D, -jnp.inf)
        m_row = jnp.maximum(g, jnp.max(D, axis=-1))
        W = jnp.exp(D - m_row[..., None]) * jnp.einsum("bhjd,bhsd->bhjs", qb, kb)
        inter = jnp.exp(g - m_row)
        num = inter[..., None] * jnp.einsum("bhjk,bhkv->bhjv", qb, C) + jnp.einsum("bhjs,bhsv->bhjv", W, vb)
        den = inter * jnp.einsum("bhjk,bhk->bhj", qb, n) + jnp.sum(W, axis=-1)
        h = num / jnp.maximum(jnp.abs(den), jnp.exp(-m_row))[..., None]
        bL = b[..., -1]
        dL = bL[..., None] - b + ib
        m_new = jnp.maximum(bL + m, jnp.max(dL, axis=-1))
        decay = jnp.exp(bL + m - m_new)
        wL = jnp.exp(dL - m_new[..., None])
        C_new = decay[..., None, None] * C + jnp.einsum("bhs,bhsk,bhsv->bhkv", wL, kb, vb)
        n_new = decay[..., None] * n + jnp.einsum("bhs,bhsk->bhk", wL, kb)
        return (C_new, n_new, m_new), h

    init = (jnp.zeros((B, H, d, d), jnp.float32), jnp.zeros((B, H, d), jnp.float32),
            jnp.zeros((B, H), jnp.float32))
    _, hc = lax.scan(step, init, (qc, kc, vc, ic, lfc))
    return jnp.moveaxis(hc, (0, 2), (1, 3)).reshape(B, S, H, d)

def mlstm_branch(u, o_pre, i_pre, f_pre, conv_w, conv_b, w_q, w_k, w_v, b_i, b_f, norm_g):
    B, S, _ = u.shape
    c = jax.nn.silu(causal_dwconv(u, conv_w, conv_b))
    q = block_diag(c, w_q).reshape(B, S, ML_HEADS, ML_HEAD_DIM).astype(jnp.float32)
    k = block_diag(c, w_k).reshape(B, S, ML_HEADS, ML_HEAD_DIM).astype(jnp.float32) * (ML_HEAD_DIM ** -0.5)
    v = block_diag(u, w_v).reshape(B, S, ML_HEADS, ML_HEAD_DIM).astype(jnp.float32)
    ig = i_pre.astype(jnp.float32) + b_i.astype(jnp.float32)
    fg = f_pre.astype(jnp.float32) + b_f.astype(jnp.float32)
    h = mlstm_chunkwise(q, k, v, ig, fg)
    o = jax.nn.sigmoid(o_pre.astype(jnp.float32)).reshape(B, S, ML_HEADS, ML_HEAD_DIM)
    h = o * h
    h = h * lax.rsqrt(jnp.mean(h * h, axis=-1, keepdims=True) + EPS)
    return (h.reshape(B, S, D_ML) * norm_g.astype(jnp.float32)).astype(u.dtype)

def memory_attention(q, mem_n, w_kv):
    B, S, _ = q.shape
    M = mem_n.shape[1]
    kv = (mem_n @ w_kv).reshape(B, M, 2, XA_HEADS, XA_HEAD_DIM)
    k, v = kv[:, :, 0], kv[:, :, 1]
    qh = q.reshape(B, S, XA_HEADS, XA_HEAD_DIM)
    s = jnp.einsum("bshd,bmhd->bhsm", qh, k).astype(jnp.float32) * (XA_HEAD_DIM ** -0.5)
    p = jax.nn.softmax(s, axis=-1).astype(q.dtype)
    o = jnp.einsum("bhsm,bmhd->bshd", p, v)
    return o.reshape(B, S, D_XA)

def swiglu(x, w1, w3, w2):
    return (jax.nn.silu(x @ w1) * (x @ w3)) @ w2

def moe_swiglu(x2, router_w, router_b, w1, w3, w2):
    T, D = x2.shape
    logits = (x2 @ router_w).astype(jnp.float32) + router_b.astype(jnp.float32)
    top_val, top_idx = lax.top_k(logits, TOP_K)
    gates = jax.nn.softmax(top_val, axis=-1).astype(x2.dtype)
    A = T * TOP_K
    e_flat = top_idx.reshape(A).astype(jnp.int32)
    g_flat = gates.reshape(A)
    tok_flat = jnp.arange(A, dtype=jnp.int32) // TOP_K
    order = jnp.argsort(e_flat)
    e_sorted = e_flat[order]
    tok_sorted = tok_flat[order]
    g_sorted = g_flat[order]
    counts = jnp.bincount(e_flat, length=N_EXPERTS).astype(jnp.int32)
    padded = ((counts + MOE_BLOCK - 1) // MOE_BLOCK) * MOE_BLOCK
    start = jnp.cumsum(counts) - counts
    pend = jnp.cumsum(padded)
    pstart = pend - padded
    dest = pstart[e_sorted] + (jnp.arange(A, dtype=jnp.int32) - start[e_sorted])
    P = A + N_EXPERTS * MOE_BLOCK
    NB = P // MOE_BLOCK
    buf_tok = jnp.zeros((P,), jnp.int32).at[dest].set(tok_sorted)
    buf_g = jnp.zeros((P,), x2.dtype).at[dest].set(g_sorted)
    blk_start = jnp.arange(NB, dtype=jnp.int32) * MOE_BLOCK
    blk_e = jnp.minimum(jnp.searchsorted(pend, blk_start, side="right"), N_EXPERTS - 1).astype(jnp.int32)

    def expert_block(args):
        tok_b, e_b = args
        xb = x2[tok_b]
        return swiglu(xb, w1[e_b], w3[e_b], w2[e_b])

    y_blk = lax.map(expert_block, (buf_tok.reshape(NB, MOE_BLOCK), blk_e))
    y = y_blk.reshape(P, D) * buf_g[:, None]
    return jnp.zeros((T, D), x2.dtype).at[buf_tok].add(y)

def first_inputs(seed: int = 0) -> dict:
    key = jax.random.key(seed)
    ks = iter(jax.random.split(key, 48))
    f32 = jnp.float32

    def nrm(shape, scale):
        return jax.random.normal(next(ks), shape, f32) * scale

    def gain(shape):
        return 1.0 + nrm(shape, 0.05)

    res_scale = (2.0 * DEPTH) ** -0.5
    u = jax.random.uniform(next(ks), (DEPTH, D_RG), f32, minval=0.9, maxval=0.999)
    p = u ** (1.0 / RG_C)
    rg_lambda = jnp.log(p) - jnp.log1p(-p)
    ml_b_f = jnp.linspace(3.0, 6.0, ML_HEADS, dtype=f32)[None, :] + nrm((DEPTH, ML_HEADS), 0.1)
    return {
        "x": nrm((BATCH, SEQ, D_MODEL), 1.0),
        "mem": nrm((BATCH, MEM_LEN, D_MODEL), 1.0),
        "norm_mix_g": gain((DEPTH, D_MODEL)),
        "w_in": nrm((DEPTH, D_MODEL, N_IN), D_MODEL ** -0.5),
        "conv_rg_w": nrm((DEPTH, CONV_W, D_RG), CONV_W ** -0.5),
        "conv_rg_b": nrm((DEPTH, D_RG), 0.02),
        "rg_w_a": nrm((DEPTH, RG_BLOCKS, RG_BLOCK, RG_BLOCK), RG_BLOCK ** -0.5),
        "rg_b_a": nrm((DEPTH, D_RG), 0.1),
        "rg_w_x": nrm((DEPTH, RG_BLOCKS, RG_BLOCK, RG_BLOCK), RG_BLOCK ** -0.5),
        "rg_b_x": nrm((DEPTH, D_RG), 0.1),
        "rg_lambda": rg_lambda,
        "conv_ml_w": nrm((DEPTH, CONV_W, D_ML), CONV_W ** -0.5),
        "conv_ml_b": nrm((DEPTH, D_ML), 0.02),
        "ml_w_q": nrm((DEPTH, ML_HEADS, ML_HEAD_DIM, ML_HEAD_DIM), ML_HEAD_DIM ** -0.5),
        "ml_w_k": nrm((DEPTH, ML_HEADS, ML_HEAD_DIM, ML_HEAD_DIM), ML_HEAD_DIM ** -0.5),
        "ml_w_v": nrm((DEPTH, ML_HEADS, ML_HEAD_DIM, ML_HEAD_DIM), ML_HEAD_DIM ** -0.5),
        "ml_b_i": nrm((DEPTH, ML_HEADS), 0.1),
        "ml_b_f": ml_b_f,
        "ml_norm_g": gain((DEPTH, D_ML)),
        "mem_norm_g": gain((DEPTH, D_MODEL)),
        "w_kv": nrm((DEPTH, D_MODEL, 2 * D_XA), D_MODEL ** -0.5),
        "w_br_rg": nrm((DEPTH, D_RG, D_MODEL), D_RG ** -0.5),
        "w_br_ml": nrm((DEPTH, D_ML, D_MODEL), D_ML ** -0.5),
        "w_br_xa": nrm((DEPTH, D_XA, D_MODEL), D_XA ** -0.5),
        "b_merge": nrm((DEPTH, N_BRANCH * D_MODEL), 0.1),
        "w_out": nrm((DEPTH, D_MODEL, D_MODEL), D_MODEL ** -0.5 * res_scale),
        "norm_ffn_g": gain((DEPTH, D_MODEL)),
        "ffn_w1": nrm((N_DENSE, D_MODEL, D_FF), D_MODEL ** -0.5),
        "ffn_w3": nrm((N_DENSE, D_MODEL, D_FF), D_MODEL ** -0.5),
        "ffn_w2": nrm((N_DENSE, D_FF, D_MODEL), D_FF ** -0.5 * res_scale),
        "router_w": nrm((N_MOE, D_MODEL, N_EXPERTS), D_MODEL ** -0.5),
        "router_b": nrm((N_MOE, N_EXPERTS), 0.01),
        "moe_w1": nrm((N_MOE, N_EXPERTS, D_MODEL, D_FF), D_MODEL ** -0.5),
        "moe_w3": nrm((N_MOE, N_EXPERTS, D_MODEL, D_FF), D_MODEL ** -0.5),
        "moe_w2": nrm((N_MOE, N_EXPERTS, D_FF, D_MODEL), D_FF ** -0.5 * res_scale),
        "final_norm_g": gain((D_MODEL,)),
    }

def first_block(x, mem, norm_mix_g, w_in, conv_rg_w, conv_rg_b, rg_w_a, rg_b_a, rg_w_x, rg_b_x,
              rg_lambda, conv_ml_w, conv_ml_b, ml_w_q, ml_w_k, ml_w_v, ml_b_i, ml_b_f, ml_norm_g,
              mem_norm_g, w_kv, w_br_rg, w_br_ml, w_br_xa, b_merge, w_out, norm_ffn_g,
              ffn_w1, ffn_w3, ffn_w2, router_w, router_b, moe_w1, moe_w3, moe_w2, final_norm_g):
    B, S, D = x.shape
    for l in range(DEPTH):
        h = rms_norm(x, norm_mix_g[l])
        z = h @ w_in[l]
        a_x, a_y, m_u, m_o, m_i, m_f, xa_q, gate_pre = split_columns(z)
        xa_c = causal_dwconv(a_x, conv_rg_w[l], conv_rg_b[l])
        y_rg = rg_lru(xa_c, rg_w_a[l], rg_b_a[l], rg_w_x[l], rg_b_x[l], rg_lambda[l]) * jax.nn.gelu(a_y)
        y_ml = mlstm_branch(m_u, m_o, m_i, m_f, conv_ml_w[l], conv_ml_b[l], ml_w_q[l], ml_w_k[l],
                            ml_w_v[l], ml_b_i[l], ml_b_f[l], ml_norm_g[l])
        mem_n = rms_norm(mem, mem_norm_g[l])
        y_xa = memory_attention(xa_q, mem_n, w_kv[l])
        gates = jax.nn.sigmoid((gate_pre + b_merge[l]).astype(jnp.float32)).astype(x.dtype)
        gates = gates.reshape(B, S, N_BRANCH, D)
        merged = (gates[:, :, 0] * (y_rg @ w_br_rg[l])
                  + gates[:, :, 1] * (y_ml @ w_br_ml[l])
                  + gates[:, :, 2] * (y_xa @ w_br_xa[l]))
        x = x + merged @ w_out[l]
        h2 = rms_norm(x, norm_ffn_g[l])
        j = l // 2
        if l % 2 == 0:
            f = swiglu(h2, ffn_w1[j], ffn_w3[j], ffn_w2[j])
        else:
            f = moe_swiglu(h2.reshape(B * S, D), router_w[j], router_b[j],
                           moe_w1[j], moe_w3[j], moe_w2[j]).reshape(B, S, D)
        x = x + f
    return rms_norm(x, final_norm_g)


DEPTH_2 = 1

GRID_W = 64
DILATED_GROUPS = ((128, 1), (512, 4), (2048, 16))
N_GROUPS_A = len(DILATED_GROUPS)
HEADS_PER_GROUP_A = 8
HEAD_DIM_A = 64
N_HEADS_A = N_GROUPS_A * HEADS_PER_GROUP_A
GROUP_WIDTH_A = HEADS_PER_GROUP_A * HEAD_DIM_A
A_QKV_WIDTH = 3 * N_HEADS_A * HEAD_DIM_A
BAND_BLK = 64
N_HEADS_B = 8
N_KV_B = 2
GQA_GROUP_B = N_HEADS_B // N_KV_B
HEAD_DIM_B = 128
B_Q_WIDTH = N_HEADS_B * HEAD_DIM_B
B_KV_WIDTH = N_KV_B * HEAD_DIM_B
ROPE_THETA = 10000.0
Q_BLOCK = 128
N_BRANCHES = 2
GATE_WIDTH = N_BRANCHES * D_MODEL
IN_WIDTH = A_QKV_WIDTH + B_Q_WIDTH + 2 * B_KV_WIDTH + GATE_WIDTH
N_BUCKETS = 32
MAX_DISTANCE = 1024
D_FF_2 = 2816
NEG_INF = -1e30


def rmsnorm(x, g):
    xf = x.astype(jnp.float32)
    y = xf * lax.rsqrt(jnp.mean(xf * xf, axis=-1, keepdims=True) + EPS)
    return (y * g.astype(jnp.float32)).astype(x.dtype)

def swiglu_2(x, w1, w3, w2):
    return (jax.nn.silu(x @ w1) * (x @ w3)) @ w2

def t5_bucket(rel):
    n = N_BUCKETS // 2
    max_exact = n // 2
    ret = jnp.where(rel > 0, n, 0)
    a = jnp.abs(rel)
    af = jnp.maximum(a, 1).astype(jnp.float32)
    large = max_exact + (jnp.log(af / max_exact) / math.log(MAX_DISTANCE / max_exact)
                         * (n - max_exact)).astype(jnp.int32)
    large = jnp.minimum(large, n - 1)
    return ret + jnp.where(a < max_exact, a, large)

def dilated_group_attention(q, k, v, bias_tab, dilation, half):
    B, S, H, hd = q.shape
    L = S // dilation
    nblk = -(-L // BAND_BLK)
    Lp = nblk * BAND_BLK

    def to_sub(a):
        a = a.reshape(B, L, dilation, H, hd).transpose(0, 2, 1, 3, 4)
        return jnp.pad(a, ((0, 0), (0, 0), (0, Lp - L), (0, 0), (0, 0)))

    def band(a):
        a = jnp.pad(a, ((0, 0), (0, 0), (BAND_BLK, BAND_BLK), (0, 0), (0, 0)))
        blocks = a.reshape(B, dilation, nblk + 2, BAND_BLK, H, hd)
        return jnp.concatenate([blocks[:, :, :-2], blocks[:, :, 1:-1], blocks[:, :, 2:]], axis=3)

    qs = to_sub(q).reshape(B, dilation, nblk, BAND_BLK, H, hd)
    kb = band(to_sub(k))
    vb = band(to_sub(v))

    scores = jnp.einsum('brnqhd,brnkhd->brnhqk', qs, kb,
                        preferred_element_type=jnp.float32) * (hd ** -0.5)
    qi = jnp.arange(BAND_BLK, dtype=jnp.int32)
    ki = jnp.arange(3 * BAND_BLK, dtype=jnp.int32) - BAND_BLK
    rel_steps = ki[None, :] - qi[:, None]
    key_m = jnp.arange(nblk, dtype=jnp.int32)[:, None] * BAND_BLK + ki[None, :]
    valid = ((jnp.abs(rel_steps) <= half)[None]
             & ((key_m >= 0) & (key_m < L))[:, None, :])
    bias = bias_tab[t5_bucket(rel_steps * dilation)].transpose(2, 0, 1)
    scores = scores + bias.astype(jnp.float32)
    scores = jnp.where(valid[None, None, :, None], scores, NEG_INF)
    lse = jax.nn.logsumexp(scores, axis=-1)
    p = jnp.exp(scores - lse[..., None])
    out = jnp.einsum('brnhqk,brnkhd->brnqhd', p.astype(v.dtype), vb)
    out = out.reshape(B, dilation, Lp, H, hd)[:, :, :L]
    out = out.transpose(0, 2, 1, 3, 4).reshape(B, S, H, hd)
    lse = lse.transpose(0, 1, 2, 4, 3).reshape(B, dilation, Lp, H)[:, :, :L]
    lse = lse.transpose(0, 2, 1, 3).reshape(B, S, H)
    return out, lse

def axial_rope_tables(rows):
    row = jnp.repeat(jnp.arange(rows, dtype=jnp.float32), GRID_W)
    col = jnp.tile(jnp.arange(GRID_W, dtype=jnp.float32), rows)
    n_freq = HEAD_DIM_B // 4
    freq = ROPE_THETA ** (-jnp.arange(n_freq, dtype=jnp.float32) / n_freq)
    ang = jnp.concatenate([row[:, None] * freq, col[:, None] * freq], axis=-1)
    return jnp.cos(ang), jnp.sin(ang)

def apply_rope(x, cos, sin):
    xf = x.astype(jnp.float32).reshape(*x.shape[:-1], x.shape[-1] // 2, 2)
    x0, x1 = xf[..., 0], xf[..., 1]
    c = cos[None, :, None, :]
    s = sin[None, :, None, :]
    out = jnp.stack([x0 * c - x1 * s, x0 * s + x1 * c], axis=-1)
    return out.reshape(x.shape).astype(x.dtype)

def gqa_axial_attention(q, k, v, q_norm, k_norm, cos, sin):
    B, S = q.shape[0], q.shape[1]
    q = apply_rope(rmsnorm(q, q_norm), cos, sin)
    k = apply_rope(rmsnorm(k, k_norm), cos, sin)
    scale = HEAD_DIM_B ** -0.5
    qblocks = q.reshape(B, S // Q_BLOCK, Q_BLOCK, N_KV_B, GQA_GROUP_B, HEAD_DIM_B).swapaxes(0, 1)

    def attn_block(qb):
        s = jnp.einsum('bqkgd,bskd->bkgqs', qb, k, preferred_element_type=jnp.float32) * scale
        p = jax.nn.softmax(s, axis=-1)
        return jnp.einsum('bkgqs,bskd->bqkgd', p.astype(v.dtype), v)

    ob = lax.map(attn_block, qblocks)
    return ob.swapaxes(0, 1).reshape(B, S, B_Q_WIDTH)

def hybrid_mixer(h, w_in, b_gate, q_norm, k_norm, rel_bias, w_branch_a, w_branch_b, w_out, cos, sin):
    B, S, D = h.shape
    proj = h @ w_in
    o1 = A_QKV_WIDTH
    o2 = o1 + B_Q_WIDTH
    o3 = o2 + B_KV_WIDTH
    o4 = o3 + B_KV_WIDTH
    pa, pq, pk, pv, pg = proj[..., :o1], proj[..., o1:o2], proj[..., o2:o3], proj[..., o3:o4], proj[..., o4:]

    a = pa.reshape(B, S, 3, N_GROUPS_A, HEADS_PER_GROUP_A, HEAD_DIM_A)
    bias_groups = rel_bias.reshape(N_BUCKETS, N_GROUPS_A, HEADS_PER_GROUP_A)
    outs, lses = [], []
    for g, (window, dil) in enumerate(DILATED_GROUPS):
        o, lse = dilated_group_attention(a[:, :, 0, g], a[:, :, 1, g], a[:, :, 2, g],
                                         bias_groups[:, g], dil, window // (2 * dil))
        outs.append(o)
        lses.append(lse)
    wgt = jax.nn.softmax(jnp.stack(lses, axis=0), axis=0)
    o_a = jnp.sum(wgt[..., None] * jnp.stack(outs, axis=0).astype(jnp.float32), axis=0)
    o_a = o_a.astype(h.dtype).reshape(B, S, GROUP_WIDTH_A)

    o_b = gqa_axial_attention(pq.reshape(B, S, N_HEADS_B, HEAD_DIM_B),
                              pk.reshape(B, S, N_KV_B, HEAD_DIM_B),
                              pv.reshape(B, S, N_KV_B, HEAD_DIM_B),
                              q_norm, k_norm, cos, sin)

    gates = jax.nn.sigmoid((pg + b_gate).reshape(B, S, N_BRANCHES, D))
    merged = gates[:, :, 0] * (o_a @ w_branch_a) + gates[:, :, 1] * (o_b @ w_branch_b)
    return merged @ w_out

def second_inputs(seed: int = 0) -> dict:
    key = jax.random.key(seed)
    ks = jax.random.split(key, 24)
    f32 = jnp.float32

    def w(k, shape, fan_in):
        return jax.random.normal(k, shape, f32) * (fan_in ** -0.5)

    def gain(k, shape):
        return 1.0 + 0.05 * jax.random.normal(k, shape, f32)

    L, D = DEPTH_2, D_MODEL
    return {
        'x': jax.random.normal(ks[0], (BATCH, SEQ, D), f32),
        'ffn1_norm': gain(ks[1], (L, D)),
        'ffn1_w1': w(ks[2], (L, D, D_FF_2), D),
        'ffn1_w3': w(ks[3], (L, D, D_FF_2), D),
        'ffn1_w2': w(ks[4], (L, D_FF_2, D), D_FF_2),
        'mix_norm': gain(ks[5], (L, D)),
        'w_in': w(ks[6], (L, D, IN_WIDTH), D),
        'b_gate': 0.02 * jax.random.normal(ks[7], (L, GATE_WIDTH), f32),
        'q_norm': gain(ks[8], (L, HEAD_DIM_B)),
        'k_norm': gain(ks[9], (L, HEAD_DIM_B)),
        'rel_bias': 0.5 * jax.random.normal(ks[10], (N_BUCKETS, N_HEADS_A), f32),
        'w_branch_a': w(ks[11], (L, GROUP_WIDTH_A, D), GROUP_WIDTH_A),
        'w_branch_b': w(ks[12], (L, B_Q_WIDTH, D), B_Q_WIDTH),
        'w_out': w(ks[13], (L, D, D), D),
        'ffn2_norm': gain(ks[14], (L, D)),
        'ffn2_w1': w(ks[15], (L, D, D_FF_2), D),
        'ffn2_w3': w(ks[16], (L, D, D_FF_2), D),
        'ffn2_w2': w(ks[17], (L, D_FF_2, D), D_FF_2),
        'final_norm': gain(ks[18], (D,)),
    }

def second_block(x, ffn1_norm, ffn1_w1, ffn1_w3, ffn1_w2, mix_norm, w_in, b_gate, q_norm, k_norm,
              rel_bias, w_branch_a, w_branch_b, w_out, ffn2_norm, ffn2_w1, ffn2_w3, ffn2_w2,
              final_norm):
    S = x.shape[1]
    rows = S // GRID_W
    cos, sin = axial_rope_tables(rows)
    for l in range(DEPTH_2):
        x = x + 0.5 * swiglu_2(rmsnorm(x, ffn1_norm[l]), ffn1_w1[l], ffn1_w3[l], ffn1_w2[l])
        h = rmsnorm(x, mix_norm[l])
        x = x + hybrid_mixer(h, w_in[l], b_gate[l], q_norm[l], k_norm[l], rel_bias,
                             w_branch_a[l], w_branch_b[l], w_out[l], cos, sin)
        x = x + 0.5 * swiglu_2(rmsnorm(x, ffn2_norm[l]), ffn2_w1[l], ffn2_w3[l], ffn2_w2[l])
    return rmsnorm(x, final_norm)


def setup_inputs(seed=0):
    out = dict(first_inputs(seed))
    for name, value in second_inputs(seed + 1).items():
        if name != "x":
            out[name + "_2"] = value
    return out


def reference(
    x, mem, norm_mix_g, w_in, conv_rg_w, conv_rg_b, rg_w_a, rg_b_a, rg_w_x, rg_b_x, rg_lambda,
    conv_ml_w, conv_ml_b, ml_w_q, ml_w_k, ml_w_v, ml_b_i, ml_b_f, ml_norm_g, mem_norm_g, w_kv,
    w_br_rg, w_br_ml, w_br_xa, b_merge, w_out, norm_ffn_g, ffn_w1, ffn_w3, ffn_w2, router_w,
    router_b, moe_w1, moe_w3, moe_w2, final_norm_g, ffn1_norm_2, ffn1_w1_2, ffn1_w3_2,
    ffn1_w2_2, mix_norm_2, w_in_2, b_gate_2, q_norm_2, k_norm_2, rel_bias_2, w_branch_a_2,
    w_branch_b_2, w_out_2, ffn2_norm_2, ffn2_w1_2, ffn2_w3_2, ffn2_w2_2, final_norm_2,
):
    x = first_block(
        x, mem, norm_mix_g, w_in, conv_rg_w, conv_rg_b, rg_w_a, rg_b_a, rg_w_x, rg_b_x,
        rg_lambda, conv_ml_w, conv_ml_b, ml_w_q, ml_w_k, ml_w_v, ml_b_i, ml_b_f, ml_norm_g,
        mem_norm_g, w_kv, w_br_rg, w_br_ml, w_br_xa, b_merge, w_out, norm_ffn_g, ffn_w1, ffn_w3,
        ffn_w2, router_w, router_b, moe_w1, moe_w3, moe_w2, final_norm_g,
    )
    return second_block(
        x, ffn1_norm_2, ffn1_w1_2, ffn1_w3_2, ffn1_w2_2, mix_norm_2, w_in_2, b_gate_2, q_norm_2,
        k_norm_2, rel_bias_2, w_branch_a_2, w_branch_b_2, w_out_2, ffn2_norm_2, ffn2_w1_2,
        ffn2_w3_2, ffn2_w2_2, final_norm_2,
    )


_drawn_inputs = setup_inputs


def setup_inputs(seed=0):
    import zlib

    import numpy as np

    out = dict(_drawn_inputs(seed))
    spreads = {}
    factors = {'rg_b_a': 8.0,
     'rg_b_x': 4.617,
     'ml_b_i': 64.0,
     'mem_norm_g': 7.066,
     'mix_norm_2': 6.999,
     'b_gate_2': 8.0,
     'q_norm_2': 8.0,
     'k_norm_2': 8.0,
     'ffn2_norm_2': 2.901}
    for name, (base, spread) in spreads.items():
        noise = np.random.default_rng([zlib.crc32(name.encode()), seed]).standard_normal(out[name].shape)
        drawn = base * np.exp(spread * noise) if base else spread * noise
        out[name] = jnp.asarray(drawn.astype(out[name].dtype))
    for name, factor in factors.items():
        out[name] = (out[name] * factor).astype(out[name].dtype)
    return out
```

```python
import concourse.bass as bass
from concourse import mybir
from concourse.alu_op_type import AluOpType as ALU
from contextlib import ExitStack
import math
import numpy as np

F32 = mybir.dt.float32
I32 = mybir.dt.int32
ACT = mybir.ActivationFunctionType
AXX = mybir.AxisListType.X

P = 128
T = 256
TT = T // P
D = 1024
KD = D // P
HEADS = 4
UC = 256
NS = 6
NB = 4
EPS = 1e-6
FF1 = 3584 // UC
FF2 = 2816 // UC
EXPERTS = 8
CAP = P
PAD = 3
SERIES = 8
GROUPS = 3
DIL = (1, 4, 16)
HA = 8
DA = 64
HB = 8
NEG = -1e30
RG_C = 8.0

VEC = {}


def _columns():
    at = 0
    for l in range(2):
        for name, n in (("norm_mix_g", 8), ("mem_norm_g", 8), ("norm_ffn_g", 8), ("conv_rg_w", 32),
                        ("conv_rg_b", 8), ("rg_b_a", 8), ("rg_b_x", 8), ("rg_lambda", 8), ("conv_ml_w", 32),
                        ("conv_ml_b", 8), ("ml_norm_g", 8), ("b_merge", 24), ("ml_b_i", 1), ("ml_b_f", 1)):
            VEC[name, l] = at
            at += n
    for name, n in (("final_norm_g", 8), ("ffn1_norm_2", 8), ("mix_norm_2", 8), ("b_gate_2", 16),
                    ("q_norm_2", 1), ("k_norm_2", 1), ("ffn2_norm_2", 8), ("final_norm_2", 8), ("router_b", 8)):
        VEC[name] = at
        at += n
    return at


NV = _columns()


class Plan:

    def __init__(self):
        self.units = []
        self.u = {}
        self.o = {}
        self.released = []
        self.n_o = 0
        self.n_acc = 0

    def out(self, *name):
        self.o[name] = self.n_o
        self.n_o += 1

    def unit(self, array, index, *name, outs=1):
        self.u[name] = len(self.units)
        self.units.append((array, index))
        if outs == 1:
            self.out(*name)
        else:
            for g in range(outs):
                self.out(*name, g)
        self.released.append(("bank", self.n_o))

    def acc(self, array, index, *name):
        self.u[name] = len(self.units)
        self.units.append((array, index))
        self.n_acc += 1
        self.released.append(("acc", self.n_acc))


N_MIX0, N_FFN0, N_MIX1, N_MOE, N_FINAL1, N_FFN1B, N_MIXB, N_FFN2B, N_FINALB = range(9)

SUMMED = (N_MIX0, N_FFN0, N_MIX1, N_MOE, N_MIXB, N_FFN2B, N_FINALB)

BIAS_NORM = 10
KV_NORM = 6
ML_FIRST = 3
MEM_SLOTS = [("o", j) for j in range(4)] + [("ay", j) for j in range(4)]
DIL_STEPS = [("dil", h, tt) for h in range(HA) for tt in range(TT)]
GQA_STEPS = [("gqa", h) for h in range(HB)]
SLOTS_B = [("qb", 0), ("qb", 1), ("qb", 2), ("qb", 3), ("kb", 0), ("vb", 0)] + [("gate", j) for j in range(8)]


def attention_steps():
    steps = [("mem", 0, h) for h in range(HEADS)] + [("mem", 1, h) for h in range(HEADS)]
    return steps + DIL_STEPS + GQA_STEPS


STEP = {s: n for n, s in enumerate(attention_steps())}


def slots_b():
    halves = [(unit, m) for unit in SLOTS_B for m in range(2)]
    steps = DIL_STEPS + GQA_STEPS
    out = []
    for n in range(len(steps) + 2):
        count = 2 if n in (18, 21) else 1
        out.append(([halves.pop(0) for _ in range(count)],
                    n // 2 - 1 if n in (2, 4, 6, 8, 10) else None,
                    n // 2 - 2 if n in (5, 7, 9, 11, 13) else None,
                    steps[n] if n < len(steps) else None,
                    steps[n - 1] if 1 <= n <= len(steps) else None,
                    steps[n - 2] if n >= 2 else None))
    assert not halves
    return out


def make_plan():
    p = Plan()
    p.out("msum")
    for l in range(2):
        for j in range(8):
            if j == KV_NORM:
                p.out("nsum", 2 * l)
            p.unit("w_kv", l * 8 + j, "kv", l, j)
        for j in range(4):
            p.unit("w_in", l * 32 + j, "ax", l, j)
        for j in range(4):
            p.unit("w_in", l * 32 + 8 + j, "mu", l, j)
        p.out("if", l)
        for j in range(4):
            p.unit("w_in", l * 32 + 16 + j, "qa", l, j)
        for n, (kind, j) in enumerate(MEM_SLOTS):
            p.unit("w_in", l * 32 + {"o": 12, "ay": 4}[kind] + j, kind, l, j)
            if 2 <= n < 2 + HEADS:
                p.out("pv", STEP["mem", l, n - 2])
        for w in ("rga", "rgx", "mlq", "mlk", "mlv"):
            p.unit(w, l, w, l, outs=4)
        p.out("acol", l)
        for j in range(12):
            p.unit("w_in", l * 32 + 20 + j, "gt", l, j)
        for j in range(4):
            p.unit("w_br_rg", l * 4 + j, "br", l, j)
        for j in range(2):
            p.out("mlsum", l, j)
        for j in range(4):
            p.unit("w_br_xa", l * 4 + j, "br", l, 8 + j)
        for j in range(4):
            p.unit("w_br_ml", l * 4 + j, "br", l, 4 + j)
        for j in range(4):
            p.unit("w_out", l * 4 + j, "wout", l, j)
        p.out("nsum", 2 * l + 1)
        if l == 0:
            for j in range(FF1):
                p.unit("ffn_w1", j, "w1", "a", j)
                p.unit("ffn_w3", j, "w3", "a", j)
            for j in range(FF1):
                p.acc("ffn_w2", j, "w2", "a", j)
    p.out("logit")
    for j in range(4):
        p.out("htok", j)
    p.out("rank")
    for j in range(4):
        p.out("gtr", j)
    p.moe_u, p.moe_o, p.moe_acc = len(p.units), p.n_o, p.n_acc
    for _ in range(EXPERTS):
        p.units += [None] * (3 * FF1)
        p.released += [None] * (3 * FF1)
    for j in range(FF1):
        p.released[len(p.units) - FF1 + j] = ("acc", p.moe_acc + (EXPERTS - 1) * FF1 + j + 1)
    p.n_o += EXPERTS * MOE_OUTS
    p.n_acc += EXPERTS * FF1
    for j in range(4):
        p.out("comb", j)
    p.out("nsum", N_FINAL1)
    p.out("nsum", N_FFN1B)
    for g in range(GROUPS):
        p.out("brow", g)

    def ffn_b(f):
        for j in range(FF2):
            p.unit(f"ffn{f}_w1_2", j, "w1", f, j)
            p.unit(f"ffn{f}_w3_2", j, "w3", f, j)
        for j in range(FF2):
            p.acc(f"ffn{f}_w2_2", j, "w2", f, j)

    ffn_b(1)
    for h in range(GROUPS * HA):
        if h == BIAS_NORM:
            p.out("nsum", N_MIXB)
        p.out("bias", h)
    for kind, n, at in (("qd", 6, 0), ("kd", 6, 6), ("vd", 6, 12)):
        for j in range(n):
            p.unit("w_in_2", at + j, kind, j)
    col = {"qb": 18, "kb": 22, "vb": 23, "gate": 24}
    for halves, normed, turned, score, trans, value in slots_b():
        for unit, m in halves:
            if m == 1:
                p.unit("w_in_2", col[unit[0]] + unit[1], *unit)
        if normed is not None:
            p.out("qksum", normed)
        if turned is not None:
            p.out("rot", turned)
        if value:
            p.out("pv", STEP[value])
    for j in range(2):
        p.acc("w_branch_a", j, "bra", j)
    for j in range(4):
        p.unit("w_branch_b", j, "brb", j)
    for j in range(4):
        p.unit("w_out_2", j, "wout", 2, j)
    p.out("nsum", N_FFN2B)
    ffn_b(2)
    p.out("nsum", N_FINALB)
    return p


MOE_OUTS = 2 * FF1 + 4


class Experts:

    def __init__(self, sem, tag, loaded, bank_full, bank_free, acc_units, u, o, acc):
        self.loaded, self.bank_full, self.bank_free, self.acc_units = loaded, bank_full, bank_free, acc_units
        self.u, self.o, self.acc = u, o, acc
        self.gathered = sem(f"gathered{tag}")
        self.xg_ready = sem(f"xg_ready{tag}")
        self.y_ready = sem(f"y_ready{tag}")

    def comb(self, j):
        return self.o + 2 + j

    def w(self, which, j):
        return self.o + (which if j == 0 else 4 + 2 * j + which)


def build(nc, a, out):
    with ExitStack() as ctx:
        def sb(name, shape, dt=F32):
            return ctx.enter_context(nc.sbuf_tensor(name, shape, dt))

        def sem(name):
            return ctx.enter_context(nc.semaphore(name))

        plan = make_plan()

        ring = sb("ring", [P, NS, 2048])
        arena = sb("arena", [P, 18 * 2048 + 48])
        at = [0]

        def page(n):
            at[0] += n
            return arena[:, at[0] - n:at[0]]

        def tiles(v, k=KD):
            return v.rearrange("p (k t) -> p k t", k=k)

        pages = [page(2048) for _ in range(6)]
        ax_pad = tiles(page(KD * (T + PAD)))
        mu_pad = tiles(page(KD * (T + PAD)))
        pages += [None, None] + [page(2048) for _ in range(10)]
        xT, hT, memT, memn = [tiles(pages[n]) for n in range(4)]
        yxa = memn
        kmem, vmem = tiles(pages[4]), pages[5].rearrange("p (m c) -> p m c", m=TT)
        qml, kml = tiles(pages[4]), tiles(pages[5])
        qxa, vml = tiles(pages[8]), pages[8].rearrange("p (m c) -> p m c", m=TT)
        ogate, ygelu, xc, cml = [tiles(pages[n]) for n in (9, 10, 11, 12)]
        hn = cml
        ml_root = arena[:, 6 * 2048:6 * 2048 + HEADS * T]
        ra, ib, g0, g1, g2 = [tiles(pages[n]) for n in (13, 14, 15, 16, 17)]
        gates = (g0, g1, g2)
        tanh_v = arena[:, 6 * 2048:7 * 2048]
        tanh_t = tiles(tanh_v)
        sq = ib
        sq_mem = g0
        merged = ra
        hid = arena[:, at[0] - 8192:at[0] - 8192 + 2 * FF1 * T].rearrange("p (f t) -> p f t", f=2 * FF1)
        silu_tmp = pages[13].rearrange("p (b c) -> p b c", b=4)
        hid_e = arena[:, at[0] - 8192:at[0] - 8192 + 2 * FF1 * CAP].rearrange("p (f t) -> p f t", f=2 * FF1)
        xg = pages[12][:, 0:KD * CAP].rearrange("p (k t) -> p k t", k=KD)
        y_tok = pages[12][:, 1024:2048]
        htok = pages[5].rearrange("p (m c) -> p m c", m=TT)
        Pg = pages[4].rearrange("p (m e s) -> p m e s", m=TT, e=EXPERTS)
        blk = arena[:, 6 * 2048:6 * 2048 + 4144 + 2048]
        Pall = blk[:, 0:TT * (EXPERTS + 1) * CAP].rearrange("p (m s) -> p m s", m=TT)
        GT = blk[:, 2304:2304 + (EXPERTS + 1) * T]
        b0 = 2 * 2048

        def area(n):
            nonlocal b0
            b0 += n
            return arena[:, b0 - n:b0]

        qd, kd = tiles(area(12 * T), 12), tiles(area(12 * T), 12)
        vd = area(TT * 12 * P).rearrange("p (m c) -> p m c", m=TT)
        bias = area(24 * 384).rearrange("p (h m) -> p h m", h=24)
        b_qk = b0
        qk = area(10 * T)
        scr = area(10 * T)
        vb = area(TT * 256).rearrange("p (m c) -> p m c", m=TT)
        gate2 = area(16 * T)
        o_a, o_b = tiles(area(4 * T), 4), tiles(area(8 * T))
        onehot = vd.rearrange("p m c -> p (m c)")[0:33, 0:GROUPS * 512].rearrange("p (g m) -> p g m", g=GROUPS)
        brow = scr[0:HA, 0:GROUPS * 512].rearrange("p (g m) -> p g m", g=GROUPS)
        brevs = [v.rearrange("p (h m) -> p h m", h=HA)
                 for v in (kd.rearrange("p k t -> p (k t)"), vd.rearrange("p m c -> p (m c)"),
                           arena[:, b_qk:b_qk + HA * 384])]
        sq_b = qd[:, 0:KD, :]
        assert b0 <= 18 * 2048 + 48, b0
        hid2 = arena[:, at[0] - 8192:at[0] - 8192 + 2 * FF2 * T].rearrange("p (f t) -> p f t", f=2 * FF2)

        ones_row = sb("ones_row", [P, T])
        vecs = sb("vecs", [P, NV])
        mats = sb("mats", [P, 6 * P])
        ident, ones, flip, rotm, tri, iota = [mats[:, n * P:(n + 1) * P] for n in range(6)]
        sel = sb("sel", [4, HEADS * P])
        wif = sb("wif", [P, 2, KD, 8])
        wr = sb("wr", [P, KD, 8])
        rope = sb("rope", [P, 2, T])
        btab = sb("btab", [33, 24])
        softp = sb("softp", [P, 4, 16])
        eps_t = sb("eps_t", [P, 1])
        warm = sb("warm", [P, 1])
        root = sb("root", [P, T])
        mem_rstd = sb("mem_rstd", [P, T])
        probs = sb("probs", [P, 2, 768])
        probsT = sb("probsT", [P, 2, 768])
        work = sb("work", [P, 768])
        smax = sb("smax", [P, 2, 2, 2])
        ssum = sb("ssum", [P, 2, 2, 2])
        mrow = probs[0:4, :, 512:768]
        arow = probsT[0:4, 0, 512:768]
        acol = sb("acol", [P, TT, HEADS])
        lg = sb("lg", [P, 14, TT, EXPERTS])
        gv = sb("gv", [P, TT, 8])
        flag = sb("flag", [P, 1], I32)
        cnt = sb("cnt", [P, 2])
        rows = [pages[15][0:4, n * T:(n + 1) * T] for n in range(8)]

        O = [ctx.enter_context(nc.psum_tensor(f"O{n}", [P, 512], F32)) for n in range(NB)]
        S = ctx.enter_context(nc.psum_tensor("S", [P, 4, 512], F32))
        S2 = S[:, :, :].rearrange("p b c -> p (b c)")
        brow_dram = nc.dram_tensor("bias_rows", [GROUPS * HA, 512], F32, kind="Internal").ap()

        loaded = [sem(f"slot{n}_loaded") for n in range(NS)]
        first_loaded = sem("first_loaded")
        small_loaded = sem("small_loaded")
        bank_full = sem("bank_full")
        bank_free = [sem(f"bank{n}_free") for n in range(NB)]
        acc_units = sem("acc_units")
        acc_quarter = sem("acc_quarter")
        squares = sem("squares")
        sq_sum = sem("sq_sum")
        memsq = sem("memsq")
        h_ready = sem("h_ready")
        memn_ready = sem("memn_ready")
        x_added = sem("x_added")
        dve_step = sem("dve_step")
        act_step = sem("act_step")
        init_done = sem("init_done")
        conv_rg = sem("conv_rg")
        conv_ml = sem("conv_ml")
        silu_ml = sem("silu_ml")
        exp_f = sem("exp_f")
        abs_f = sem("abs_f")
        a_ready = sem("a_ready")
        decay = sem("decay")
        rg_s = sem("rg_s")
        rg_root = sem("rg_root")
        rg_done = sem("rg_done")
        lam_abs = sem("lam_abs")
        lam_exp = sem("lam_exp")
        lam_done = sem("lam_done")
        scores = sem("scores")
        scores_free = sem("scores_free")
        maxed = sem("maxed")
        exped = sem("exped")
        probs_ready = sem("probs_ready")
        transposed = sem("transposed")
        probsT_ready = sem("probsT_ready")
        ml_scores = sem("ml_scores")
        ml_arg = sem("ml_arg")
        ml_exp = sem("ml_exp")
        ml_em = sem("ml_em")
        ml_mask = sem("ml_mask")
        ml_w = sem("ml_w")
        ml_num = sem("ml_num")
        ml_abs = sem("ml_abs")
        ml_head = sem("ml_head")
        ml_sq = sem("ml_sq")
        ml_done = sem("ml_done")
        merged_ready = sem("merged_ready")
        routed = sem("routed")
        gate_exp = sem("gate_exp")
        gate_arg = sem("gate_arg")
        sel_ready = sem("sel_ready")
        picks = sem("picks")
        ranks_moved = sem("ranks_moved")
        moe_done = sem("moe_done")
        table_loaded = sem("table_loaded")
        rows_stored = sem("rows_stored")
        rows_loaded = [sem(f"rows_loaded{g}") for g in range(GROUPS)]
        qk_sq = sem("qk_sq")
        qk_norm = sem("qk_norm")
        qk_ready = sem("qk_ready")
        bra_free = sem("bra_free")
        stored = sem("stored")

        main = Experts(sem, "", loaded, bank_full, bank_free, acc_units, plan.moe_u, plan.moe_o, plan.moe_acc)
        again = Experts(sem, "_again", [sem(f"slot{n}_loaded_again") for n in range(NS)], sem("bank_full_again"),
                        [sem(f"bank{n}_free_again") for n in range(NB)], sem("acc_units_again"), 0, 4, 0)

        def vec(name, l=None, n=8):
            c = VEC[name] if l is None else VEC[name, l]
            return vecs[:, c:c + n]

        def filled(eng, *name):
            o = plan.o[name]
            eng.wait_ge(bank_full, o + 1)
            return O[o % NB]

        def freed(*name):
            return bank_free[plan.o[name] % NB]

        def evacuated(eng, *name):
            o = plan.o[name]
            eng.wait_ge(bank_free[o % NB], o // NB + 1)

        MIXER_BEFORE = {N_FFN0: 0, N_MOE: 1, N_FFN2B: 2}
        FFN_BEFORE = {N_MIX1: 0, N_MIXB: 1, N_FINALB: 2}

        def x_ready(eng, n, quarter):
            if n == N_MIX0:
                eng.wait_ge(small_loaded, SMALL * 16)
            elif n == N_FINAL1:
                eng.wait_ge(moe_done, 1)
            elif n == N_FFN1B:
                eng.wait_ge(h_ready, 8 * N_FINAL1 + 2 * quarter + 2)
            elif n in MIXER_BEFORE:
                evacuated(eng, "wout", MIXER_BEFORE[n], quarter)
            else:
                eng.wait_ge(x_added, 4 * FFN_BEFORE[n] + quarter + 1)

        NORM_G = {N_MIX0: ("norm_mix_g", 0), N_FFN0: ("norm_ffn_g", 0), N_MIX1: ("norm_mix_g", 1),
                  N_MOE: ("norm_ffn_g", 1), N_FINAL1: ("final_norm_g",), N_FFN1B: ("ffn1_norm_2",),
                  N_MIXB: ("mix_norm_2",), N_FFN2B: ("ffn2_norm_2",), N_FINALB: ("final_norm_2",)}

        FIRST_LOADS = [(memT, a["memT"]), (mats[:, :], a["mats"]), (vecs[:, :], a["vecs"])]
        SMALL_LOADS = [(xT, a["xT"]), (sel[:, :], a["sel"]), (wif[:, :, :, :], a["wif"]), (wr[:, :, :], a["wr"]),
                       (rope[:, :, :], a["rope"]), (btab[:, :], a["btab"])]
        SMALL = len(SMALL_LOADS)

        block = ctx.enter_context(nc.Block())

        @block.sync
        def _(sp):
            def bring(first, last):
                for u in range(first, last):
                    array, index = plan.units[u]
                    if u >= NS:
                        how, count = plan.released[u - NS]
                        sp.wait_ge(bank_full if how == "bank" else acc_units, count)
                    sp.dma_start(ring[:, u % NS, :], a[array][index]).then_inc(loaded[u % NS], 16)

            def expert_unit(x, e, i):
                slot = (x.u + i) % NS
                array, index = (("moe_w1", "moe_w3")[i % 2], i // 2) if i < 2 * FF1 else ("moe_w2", i - 2 * FF1)
                sp.dma_start(ring[:, slot, :], a[array][e, index]).then_inc(x.loaded[slot], 16)

            def used(x, e, i):
                if i < 2 * FF1:
                    sp.wait_ge(x.bank_full, e * MOE_OUTS + x.w(i % 2, i // 2) + 1)
                else:
                    sp.wait_ge(x.acc_units, e * FF1 + x.acc + i - 2 * FF1 + 1)

            def experts(x):
                with sp.Fori(0, EXPERTS - 1) as e:
                    for i in range(NS, 3 * FF1):
                        if i == 2 * FF1 - 1:
                            used(x, e, i + 1 - NS)
                        elif i != 2 * FF1:
                            used(x, e, i - NS)
                        expert_unit(x, e, i)
                    for i in range(NS):
                        used(x, e, 3 * FF1 - NS + i)
                        expert_unit(x, e + 1, i)
                for i in range(NS, 3 * FF1):
                    used(x, EXPERTS - 1, i - NS)
                    expert_unit(x, EXPERTS - 1, i)

            for to, of in FIRST_LOADS:
                sp.dma_start(to, of).then_inc(first_loaded, 16)
            bring(0, plan.moe_u)
            for i in range(NS):
                how, count = plan.released[plan.moe_u - NS + i]
                sp.wait_ge(bank_full if how == "bank" else acc_units, count)
                expert_unit(main, 0, i)
            experts(main)
            sp.wait_ge(routed, 1)
            with sp.If(sp.value_load(flag[0:1, 0:1], min_val=0, max_val=1) != 0):
                sp.wait_ge(acc_units, plan.moe_acc + EXPERTS * FF1)
                for i in range(NS):
                    expert_unit(again, 0, i)
                experts(again)
                sp.wait_ge(again.acc_units, EXPERTS * FF1)
            bring(plan.moe_u + EXPERTS * 3 * FF1, len(plan.units))

        @block.tensor
        def _(pe):
            seen = [0]

            def take(*name):
                u = plan.u[name]
                pe.wait_ge(loaded[u % NS], 16 * (u // NS + 1))
                return ring[:, u % NS, :]

            def bank(*name):
                o = plan.o[name]
                assert o == seen[0], (name, o, seen[0])
                seen[0] += 1
                if o >= NB:
                    pe.wait_ge(bank_free[o % NB], o // NB)
                return O[o % NB]

            def columns(w, rhs, name, kt=KD, tile_ready=None):
                b = bank(*name)
                w = w.rearrange("p (k c) -> p k c", k=kt)
                for m in range(2):
                    for k in range(kt):
                        if m == 0 and tile_ready:
                            tile_ready(k)
                        mm = pe.matmul(b[:, m * T:(m + 1) * T], w[:, k, m * P:(m + 1) * P], rhs(k),
                                       start=(k == 0), stop=(k == kt - 1))
                mm.then_inc(bank_full, 1)

            def normed(n):
                return lambda k: pe.wait_ge(h_ready, 8 * n + k + 1)

            def merged_tiles(n):
                return lambda k: pe.wait_ge(merged_ready, 4 * n + k // 2 + 1)

            def token_rows(w, lhs, name):
                b = bank(*name)
                w = w.rearrange("p (k c) -> p k c", k=KD)
                for m in range(TT):
                    for k in range(KD):
                        mm = pe.matmul(b[:, m * UC:(m + 1) * UC], lhs(k, m), w[:, k, :],
                                       start=(k == 0), stop=(k == KD - 1))
                mm.then_inc(bank_full, 1)

            def half(unit, m):
                w = take(*unit).rearrange("p (k c) -> p k c", k=KD)
                if m == 1:
                    b = bank(*unit)
                else:
                    o = plan.o[unit]
                    pe.wait_ge(bank_free[o % NB], o // NB)
                    b = O[o % NB]
                for k in range(KD):
                    if unit[0] == "vb":
                        lhs, rhs = hT[:, k, m * P:(m + 1) * P], w[:, k, :]
                    else:
                        lhs, rhs = w[:, k, m * P:(m + 1) * P], hT[:, k, :]
                    mm = pe.matmul(b[:, m * 256:(m + 1) * 256], lhs, rhs, start=(k == 0), stop=(k == KD - 1))
                if m == 1:
                    mm.then_inc(bank_full, 1)

            def norm_sum(n):
                b = bank("nsum", n)
                s = sq if n <= N_FINAL1 else sq_b
                if n in SUMMED:
                    pe.wait_ge(sq_sum, SUMMED.index(n) + 1)
                for k in (0, 1, 6, 7) if n in SUMMED else range(KD):
                    if k == 6 or k % 2 == 0 and n not in SUMMED:
                        pe.wait_ge(squares, 4 * n + k // 2 + 1)
                    mm = pe.matmul(b[:, 0:T], ones, s[:, k, :], start=(k == 0), stop=(k == 7))
                mm.then_inc(bank_full, 1)

            def hidden(f, ff, n):
                for j in range(ff):
                    for which in ("w1", "w3"):
                        w = take(which, f, j)
                        columns(w, lambda k: hT[:, k, :], (which, f, j),
                                tile_ready=normed(n) if j == 0 and which == "w1" else None)

            def second(f, ff, h):
                for j in range(ff):
                    w = take("w2", f, j).rearrange("p (k c) -> p k c", k=2)
                    evacuated(pe, "w3", f, j)
                    order = [(k, m) for k in range(2) for m in range(KD)]
                    if j == ff - 1:
                        order.sort(key=lambda km: (km[1] // 2, km[0]))
                    for n, (k, m) in enumerate(order):
                        mm = pe.matmul(S[:, m // 2, (m % 2) * T:(m % 2 + 1) * T], w[:, k, m * P:(m + 1) * P],
                                       h[:, 2 * j + k, :], start=(j == 0 and k == 0 and m % 2 == 0),
                                       stop=(j == ff - 1 and k == 1), skip_group_check=True)
                        if j == ff - 1 and n in (3, 7, 11):
                            mm.then_inc(acc_quarter, 1)
                    mm.then_inc(acc_units, 1)

            def score(step):
                n = STEP[step]
                if n == 0:
                    pass
                else:
                    pe.wait_ge(scores_free, n)
                if step[0] == "mem":
                    h = step[2]
                    if h == 0:
                        evacuated(pe, "kv", step[1], 3)
                    evacuated(pe, "qa", step[1], h)
                    for m in range(TT):
                        for k in range(2):
                            mm = pe.matmul(S[:, 0, m * T:(m + 1) * T], qxa[:, 2 * h + k, m * P:(m + 1) * P],
                                           kmem[:, 2 * h + k, :], start=(k == 0), stop=(k == 1))
                elif step[0] == "dil":
                    h, m = step[1:]
                    if (h, m) == (0, 0):
                        evacuated(pe, "kd", 5)
                        evacuated(pe, "qd", 5)
                    r = DA * (h % 2)
                    for g in range(GROUPS):
                        t = (g * HA + h) // 2
                        mm = pe.matmul(S2[:, g * T:(g + 1) * T], qd[r:r + DA, t, m * P:(m + 1) * P],
                                       kd[r:r + DA, t, :], start=True, stop=True)
                else:
                    h = step[1]
                    if h == 0:
                        pe.wait_ge(qk_ready, 5)
                    q4 = qk.rearrange("p (k t) -> p k t", k=10)
                    for m in range(TT):
                        mm = pe.matmul(S[:, 0, m * T:(m + 1) * T], q4[:, h, m * P:(m + 1) * P],
                                       q4[:, HB + h // 4, :], start=True, stop=True)
                mm.then_inc(scores, 1)

            def transpose(step):
                n = STEP[step]
                pe.wait_ge(probs_ready, n + 1)
                if n:
                    pe.wait_ge(probsT_ready, n)
                p = probs[:, n % 2, :]
                if step[0] == "dil":
                    for c in range(6):
                        mm = pe.transpose(S2[:, 1024 + c * P:1024 + (c + 1) * P], p[:, c * P:(c + 1) * P], ident)
                else:
                    for m in range(TT):
                        for c in range(2):
                            mm = pe.transpose(S2[:, 1024 + c * T + m * P:1024 + c * T + (m + 1) * P],
                                              p[:, m * T + c * P:m * T + (c + 1) * P], ident)
                mm.then_inc(transposed, 1)

            def value(step):
                n = STEP[step]
                b = bank("pv", n)
                pe.wait_ge(probsT_ready, n + 1)
                p = probsT[:, n % 2, :]
                if step[0] == "mem":
                    h = step[2]
                    evacuated(pe, "kv", step[1], 4 + h)
                    for m in range(2):
                        for c in range(2):
                            mm = pe.matmul(b[:, m * T:(m + 1) * T], vmem[:, c, h * 256 + m * P:h * 256 + (m + 1) * P],
                                           p[:, c * T:(c + 1) * T], start=(c == 0), stop=(c == 1))
                elif step[0] == "dil":
                    h, m = step[1:]
                    if (h, m) == (0, 0):
                        evacuated(pe, "vd", 5)
                    r = DA * (h % 2)
                    for c in range(6):
                        g, t = c // 2, c % 2
                        mm = pe.matmul(b[r:r + DA, 0:P], vd[:, t, g * 512 + h * DA:g * 512 + (h + 1) * DA],
                                       p[:, c * P:(c + 1) * P], start=(c == 0), stop=(c == 5))
                else:
                    h = step[1]
                    if h == 0:
                        evacuated(pe, "vb", 0)
                    for c in range(2):
                        mm = pe.matmul(b[:, 0:T], vb[:, c, (h // 4) * P:(h // 4 + 1) * P], p[:, c * T:(c + 1) * T],
                                       start=(c == 0), stop=(c == 1))
                mm.then_inc(bank_full, 1)

            def blocks(w, rhs, name):
                w = w.rearrange("p (k c) -> p k c", k=KD)
                for g in range(4):
                    b = bank(*name, g)
                    for m in range(2):
                        for k in range(2):
                            mm = pe.matmul(b[:, m * T:(m + 1) * T], w[:, 2 * g + k, m * P:(m + 1) * P],
                                           rhs(2 * g + k), start=(k == 0), stop=(k == 1))
                    mm.then_inc(bank_full, 1)

            def ml_score(l, h):
                n = HEADS * l + h
                if n:
                    pe.wait_ge(ml_w, n)
                    pe.wait_ge(ml_em, n)
                if h == 0:
                    pe.wait_ge(scores_free, STEP["mem", l, 3] + 1)
                    pe.wait_ge(a_ready, l + 1)
                    evacuated(pe, "mlq", l, 3)
                    evacuated(pe, "mlk", l, 3)
                for s in range(TT):
                    to = S[:, 0, 0:T] if s == 0 else S[:, 0, T:T + P]
                    for k in range(2):
                        pe.matmul(to, kml[:, 2 * h + k, s * P:(s + 1) * P], qml[:, 2 * h + k, s * P:T],
                                  start=(k == 0), stop=(k == 1))
                pe.matmul(S[:, 1, :], sel[:, h * P:(h + 1) * P], mrow, start=True, stop=True)\
                  .then_inc(ml_scores, 1)

            def ml_value(l, h):
                n = HEADS * l + h
                pe.wait_ge(ml_w, n + 1)
                if n:
                    pe.wait_ge(ml_head, n)
                if h == 0:
                    pe.wait_ge(probsT_ready, STEP["mem", l, 3] + 1)
                    evacuated(pe, "mlv", l, 3)
                w = probs[:, n % 2, :]
                pe.matmul(S[:, 3, 0:T], ones, w[:, 0:T], start=True, stop=False, skip_group_check=True)
                pe.matmul(S[:, 3, P:T], ones, w[:, T:T + P], start=False, stop=True, skip_group_check=True)
                for m in range(2):
                    c = h * 256 + m * P
                    pe.matmul(S[:, 2, m * T:(m + 1) * T], vml[:, 0, c:c + P], w[:, 0:T], start=True, stop=False,
                              skip_group_check=True)
                    mm = pe.matmul(S[:, 2, m * T + P:(m + 1) * T], vml[:, 1, c:c + P], w[:, T:T + P], start=False,
                                   stop=True, skip_group_check=True)
                mm.then_inc(ml_num, 1)

            def mixer(l):
                for j in range(8):
                    if j == KV_NORM:
                        norm_sum(2 * l)
                    w = take("kv", l, j)
                    if j < 4:
                        columns(w, lambda k: memn[:, k, :], ("kv", l, j),
                                tile_ready=(lambda k: pe.wait_ge(memn_ready, 8 * l + k + 1)) if j == 0 else None)
                    else:
                        token_rows(w, lambda k, m: memn[:, k, m * P:(m + 1) * P], ("kv", l, j))
                for kind in ("ax", "mu"):
                    for j in range(4):
                        columns(take(kind, l, j), lambda k: hT[:, k, :], (kind, l, j),
                                tile_ready=normed(2 * l) if (kind, j) == ("ax", 0) else None)
                b = bank("if", l)
                for m in range(2):
                    for k in range(KD):
                        mm = pe.matmul(b[0:4, m * T:(m + 1) * T], wif[:, l, k, 4 * m:4 * m + 4], hT[:, k, :],
                                       start=(k == 0), stop=(k == KD - 1))
                mm.then_inc(bank_full, 1)
                for j in range(4):
                    columns(take("qa", l, j), lambda k: hT[:, k, :], ("qa", l, j))
                for n, (kind, j) in enumerate(MEM_SLOTS):
                    columns(take(kind, l, j), lambda k: hT[:, k, :], (kind, l, j))
                    if n < HEADS:
                        score(("mem", l, n))
                    if 1 <= n < 1 + HEADS:
                        transpose(("mem", l, n - 1))
                    if 2 <= n < 2 + HEADS:
                        value(("mem", l, n - 2))
                for name in ("rga", "rgx"):
                    w = take(name, l)
                    pe.wait_ge(conv_rg, l + 1)
                    blocks(w, lambda k: xc[:, k, :], (name, l))
                for name in ("mlq", "mlk"):
                    w = take(name, l)
                    pe.wait_ge(silu_ml, l + 1)
                    blocks(w, lambda k: cml[:, k, :], (name, l))
                w = take("mlv", l).rearrange("p (k c) -> p k c", k=KD)
                evacuated(pe, "mu", l, 3)
                for g in range(4):
                    b = bank("mlv", l, g)
                    for m in range(TT):
                        for k in range(2):
                            mm = pe.matmul(b[:, m * UC:(m + 1) * UC],
                                           mu_pad[:, 2 * g + k, PAD + m * P:PAD + (m + 1) * P], w[:, 2 * g + k, :],
                                           start=(k == 0), stop=(k == 1))
                    mm.then_inc(bank_full, 1)
                b = bank("acol", l)
                pe.wait_ge(a_ready, l + 1)
                for m in range(TT):
                    mm = pe.matmul(b[:, 4 * m:4 * m + 4], arow[:, m * P:(m + 1) * P], ident[0:4, 0:4],
                                   start=True, stop=True)
                mm.then_inc(bank_full, 1)
                for j in range(12):
                    columns(take("gt", l, j), lambda k: hT[:, k, :], ("gt", l, j))
                    if ML_FIRST <= j < ML_FIRST + HEADS:
                        ml_score(l, j - ML_FIRST)
                    if ML_FIRST + 2 <= j < ML_FIRST + 2 + HEADS:
                        ml_value(l, j - ML_FIRST - 2)
                for j in range(4):
                    w = take("br", l, j)
                    if j == 0:
                        pe.wait_ge(rg_done, l + 1)
                    columns(w, lambda k: ygelu[:, k, :], ("br", l, j))
                pe.wait_ge(ml_sq, l + 1)
                for j in range(2):
                    b = bank("mlsum", l, j)
                    for h in range(2):
                        for k in range(2):
                            mm = pe.matmul(b[:, h * T:(h + 1) * T], ones, sq[:, 4 * j + 2 * h + k, :],
                                           start=(k == 0), stop=(k == 1))
                    mm.then_inc(bank_full, 1)
                for j in range(8, 12):
                    w = take("br", l, j)
                    if j == 8:
                        evacuated(pe, "pv", STEP["mem", l, 3])
                    columns(w, lambda k: yxa[:, k, :], ("br", l, j))
                for j in range(4, 8):
                    w = take("br", l, j)
                    if j == 4:
                        pe.wait_ge(ml_done, l + 1)
                    columns(w, lambda k: hn[:, k, :], ("br", l, j))
                for j in range(4):
                    columns(take("wout", l, j), lambda k: merged[:, k, :], ("wout", l, j),
                            tile_ready=merged_tiles(l) if j == 0 else None)
                norm_sum(2 * l + 1)

            b = bank("msum")
            pe.wait_ge(first_loaded, 16 * len(FIRST_LOADS))
            for k in range(KD):
                if k % 2 == 0:
                    pe.wait_ge(memsq, k // 2 + 1)
                mm = pe.matmul(b[:, 0:T], ones, sq_mem[:, k, :], start=(k == 0), stop=(k == KD - 1))
            mm.then_inc(bank_full, 1)
            mixer(0)
            hidden("a", FF1, N_FFN0)
            second("a", FF1, hid)
            mixer(1)

            b = bank("logit")
            for m in range(TT):
                for k in range(KD):
                    if m == 0:
                        normed(N_MOE)(k)
                    mm = pe.matmul(b[:, 8 * m:8 * m + 8], hT[:, k, m * P:(m + 1) * P], wr[:, k, :],
                                   start=(k == 0), stop=(k == KD - 1))
            mm.then_inc(bank_full, 1)
            for j in range(4):
                b = bank("htok", j)
                for c in range(4):
                    m, k = j // 2, 4 * (j % 2) + c
                    mm = pe.transpose(b[:, c * P:(c + 1) * P], hT[:, k, m * P:(m + 1) * P], ident)
                mm.then_inc(bank_full, 1)
            b = bank("rank")
            pe.wait_ge(sel_ready, 1)
            picked = lg[:, 6, :, :]
            pe.matmul(b[:, 0:8], tri, picked[:, 0, :], start=True, stop=True)
            pe.matmul(b[:, 8:16], tri, picked[:, 1, :], start=True, stop=False)
            pe.matmul(b[:, 8:16], ones, picked[:, 0, :], start=False, stop=True)
            pe.matmul(b[:, 16:24], ones, picked[:, 0, :], start=True, stop=False)
            pe.matmul(b[:, 16:24], ones, picked[:, 1, :], start=False, stop=True).then_inc(bank_full, 1)

            def gate_rows(x, o, n_pass):
                pe.wait_ge(picks, 3 * n_pass - 1)
                for j in range(4):
                    if o + j >= NB:
                        pe.wait_ge(x.bank_free[(o + j) % NB], (o + j) // NB)
                    b = O[(o + j) % NB]
                    for c in range(4):
                        e, m = 2 * j + c // 2, c % 2
                        mm = pe.transpose(b[:, c * P:(c + 1) * P], Pg[:, m, e, :], ident)
                    mm.then_inc(x.bank_full, 1)

            def gather(x, e):
                for k in range(KD):
                    for m in range(TT):
                        mm = pe.matmul(S2[:, 1024 + k * CAP:1024 + (k + 1) * CAP], htok[:, m, k * P:(k + 1) * P],
                                       Pall[:, m, bass.ts(e, CAP)], start=(m == 0), stop=(m == 1))
                mm.then_inc(x.gathered, 1)

            def combine(x, o, e):
                for j in range(4):
                    pe.wait_ge(x.bank_free[(o + j) % NB], (o + j) // NB + e * (MOE_OUTS // NB))
                    b = O[(o + j) % NB]
                    for m in range(2):
                        c = (2 * j + m) * P
                        mm = pe.matmul(b[:, m * T:(m + 1) * T], y_tok[:, c:c + P], GT[:, bass.ts(e, T)],
                                       start=True, stop=True)
                    mm.then_inc(x.bank_full, 1)

            def first_gather(x, n_pass):
                pe.wait_ge(picks, 3 * n_pass - 2)
                gather(x, 0)

            def experts(x, n_pass):
                with pe.Fori(0, EXPERTS) as e:
                    pe.wait_ge(x.xg_ready, e * 2 + 2)
                    for i in range(2 * FF1):
                        o = x.w(i % 2, i // 2)
                        slot = (x.u + i) % NS
                        pe.wait_ge(x.loaded[slot], e * (16 * 3 * FF1 // NS) + 16 * ((x.u + i) // NS + 1))
                        pe.wait_ge(x.bank_free[o % NB], e * (MOE_OUTS // NB) + o // NB)
                        b = O[o % NB]
                        w = ring[:, slot, :].rearrange("p (k c) -> p k c", k=KD)
                        for m in range(2):
                            for k in range(KD):
                                mm = pe.matmul(b[:, m * CAP:(m + 1) * CAP], w[:, k, m * P:(m + 1) * P], xg[:, k, :],
                                               start=(k == 0), stop=(k == KD - 1))
                        mm.then_inc(x.bank_full, 1)
                        if i == 1:
                            pe.wait_ge(x.y_ready, e * 2 + 2)
                            combine(x, x.comb(0), e)
                    pe.wait_ge(picks, 3 * n_pass)
                    gather(x, e + 1)
                    for j in range(FF1):
                        slot = (x.u + 2 * FF1 + j) % NS
                        pe.wait_ge(x.loaded[slot], e * (16 * 3 * FF1 // NS) + 16 * ((x.u + 2 * FF1 + j) // NS + 1))
                        o = x.w(1, j)
                        pe.wait_ge(x.bank_free[o % NB], e * (MOE_OUTS // NB) + o // NB + 1)
                        w = ring[:, slot, :].rearrange("p (k c) -> p k c", k=2)
                        for k in range(2):
                            for c in range(2):
                                mm = pe.matmul(S[:, c, :], hid_e[:, 2 * j + k, :], w[:, k, c * 512:(c + 1) * 512],
                                               start=(j == 0 and k == 0), stop=(j == FF1 - 1 and k == 1))
                        mm.then_inc(x.acc_units, 1)
                pe.wait_ge(x.y_ready, 2 * EXPERTS + 2)
                last_combine(x)

            def last_combine(x):
                o = x.o + EXPERTS * MOE_OUTS
                for j in range(4):
                    pe.wait_ge(x.bank_free[(o + j) % NB], (o + j) // NB)
                    b = O[(o + j) % NB]
                    for m in range(2):
                        c = (2 * j + m) * P
                        mm = pe.matmul(b[:, m * T:(m + 1) * T], y_tok[:, c:c + P], GT[:, EXPERTS * T:(EXPERTS + 1) * T],
                                       start=True, stop=True)
                    mm.then_inc(x.bank_full, 1)

            def combined(x):
                o = x.o + EXPERTS * MOE_OUTS
                for q in range(4):
                    pe.wait_ge(x.bank_free[(o + q) % NB], (o + q) // NB + 1)

            for j in range(4):
                evacuated(pe, "htok", j)
            first_gather(main, 1)
            gate_rows(main, plan.o["gtr", 0], 1)
            seen[0] = plan.moe_o
            experts(main, 1)
            seen[0] = plan.o["comb", 3] + 1
            pe.wait_ge(routed, 1)
            with pe.If(pe.value_load(flag[0:1, 0:1], min_val=0, max_val=1) != 0):
                combined(main)
                first_gather(again, 2)
                gate_rows(again, 0, 2)
                experts(again, 2)
                combined(again)
            norm_sum(N_FINAL1)
            norm_sum(N_FFN1B)

            pe.wait_ge(table_loaded, 16)
            for g in range(GROUPS):
                bank("brow", g)
                pe.matmul(O[plan.o["brow", g] % NB][0:HA, :], btab[:, g * HA:(g + 1) * HA], onehot[:, g, :],
                          start=True, stop=True).then_inc(bank_full, 1)
            hidden(1, FF2, N_FFN1B)
            second(1, FF2, hid2)
            for h in range(GROUPS * HA):
                if h == BIAS_NORM:
                    norm_sum(N_MIXB)
                b = bank("bias", h)
                if h % HA == 0:
                    pe.wait_ge(rows_loaded[h // HA], 16)
                pe.matmul(b[:, 0:384], flip, brevs[h // HA][:, h % HA, :], start=True, stop=True).then_inc(bank_full, 1)
            for kind in ("qd", "kd", "vd"):
                for j in range(6):
                    w = take(kind, j)
                    if kind == "vd":
                        token_rows(w, lambda k, m: hT[:, k, m * P:(m + 1) * P], (kind, j))
                    else:
                        columns(w, lambda k: hT[:, k, :], (kind, j),
                                tile_ready=normed(N_MIXB) if (kind, j) == ("qd", 0) else None)
            for halves, summed, turned, s, t, v in slots_b():
                for unit, m in halves:
                    half(unit, m)
                if summed is not None:
                    b = bank("qksum", summed)
                    pe.wait_ge(qk_sq, summed + 1)
                    pe.matmul(b[:, :], ones, scr[:, summed * 512:(summed + 1) * 512], start=True, stop=True)\
                      .then_inc(bank_full, 1)
                if turned is not None:
                    b = bank("rot", turned)
                    pe.wait_ge(qk_norm, turned + 1)
                    pe.matmul(b[:, :], rotm, qk[:, turned * 512:(turned + 1) * 512], start=True, stop=True)\
                      .then_inc(bank_full, 1)
                if s:
                    score(s)
                if t:
                    transpose(t)
                if v:
                    value(v)
            pe.wait_ge(scores_free, len(STEP))
            pe.wait_ge(probsT_ready, len(STEP))
            for j in range(2):
                w = take("bra", j).rearrange("p (k c) -> p k c", k=2)
                if j == 0:
                    evacuated(pe, "pv", STEP["dil", HA - 1, 1])
                for k in range(2):
                    for m in range(KD):
                        mm = pe.matmul(S[:, m // 2, (m % 2) * T:(m % 2 + 1) * T], w[:, k, m * P:(m + 1) * P],
                                       o_a[:, 2 * j + k, :], start=(j == 0 and k == 0 and m % 2 == 0),
                                       stop=(j == 1 and k == 1), skip_group_check=True)
                mm.then_inc(acc_units, 1)
            for j in range(4):
                w = take("brb", j)
                if j == 0:
                    evacuated(pe, "pv", STEP["gqa", HB - 1])
                columns(w, lambda k: o_b[:, k, :], ("brb", j))
            for j in range(4):
                columns(take("wout", 2, j), lambda k: tiles(gate2[:, 0:2048])[:, k, :], ("wout", 2, j),
                        tile_ready=merged_tiles(2) if j == 0 else None)
            norm_sum(N_FFN2B)
            hidden(2, FF2, N_FFN2B)
            second(2, FF2, hid2)
            norm_sum(N_FINALB)
            assert seen[0] == plan.n_o

        @block.scalar
        def _(act):
            steps = [0]

            def step(ins):
                steps[0] += 1
                ins.then_inc(act_step, 1)
                act.wait_ge(act_step, steps[0])

            def copy(to, of, *name):
                b = filled(act, *name)
                act.activation(to, b[:, :] if of is None else of(b), ACT.Copy).then_inc(freed(*name), 1)

            def square(n):
                s = sq if n <= N_FINAL1 else sq_b
                act.activation(warm[:, :], eps_t[:, :], ACT.Sqrt)
                for q in range(4):
                    x_ready(act, n, q)
                    act.activation(s[:, 2 * q:2 * q + 2, :], xT[:, 2 * q:2 * q + 2, :], ACT.Square)\
                       .then_inc(squares, 1)

            def root_mean(n):
                b = filled(act, "nsum", n)
                if n:
                    act.wait_ge(h_ready, 8 * n)
                act.activation(root[:, :], b[:, 0:T], ACT.Sqrt, bias=eps_t[:, :], scale=1.0 / D)\
                   .then_inc(freed("nsum", n), 1)

            def hidden(f, ff):
                for j in range(ff):
                    if j >= 4:
                        evacuated(act, "w3", f, j - 4)
                    b = filled(act, "w1", f, j)
                    act.activation(silu_tmp[:, j % 4, :], b[:, :], ACT.Silu).then_inc(freed("w1", f, j), 1)

            def exps(s):
                n = STEP[s]
                par = n % 2
                act.wait_ge(maxed, n + 1)
                if n >= 2:
                    act.wait_ge(transposed, n - 1)
                if s[0] == "dil":
                    act.activation(probs[:, par, :], work[:, :], ACT.Exp, bias=smax[:, par, 1, 0:1],
                                   accum_out=ssum[:, par, 0, 0:1]).then_inc(exped, 1)
                    return
                scale = 256 ** -0.5 if s[0] == "mem" else P ** -0.5
                for m in range(TT):
                    last = act.activation(probs[:, par, m * T:(m + 1) * T], S[:, 0, m * T:(m + 1) * T], ACT.Exp,
                                          bias=smax[:, par, 1, m:m + 1], scale=scale,
                                          accum_out=ssum[:, par, 0, m:m + 1])
                last.then_inc(exped, 1)

            def take_over(s):
                n = STEP[s]
                act.wait_ge(transposed, n + 1)
                if n >= 2:
                    act.wait_ge(bank_full, plan.o["pv", n - 2] + 1)
                w = 768 if s[0] == "dil" else 512
                act.activation(probsT[:, n % 2, 0:w], S2[:, 1024:1024 + w], ACT.Copy).then_inc(probsT_ready, 1)

            def gated(l, kind, j, func, to):
                b = filled(act, kind, l, j)
                act.activation(to, b[:, :], func).then_inc(freed(kind, l, j), 1)

            def two_biased(to, name, func, bias_of):
                b = filled(act, *name)
                act.activation(to(0), b[:, 0:T], func, bias=bias_of(0))
                act.activation(to(1), b[:, T:2 * T], func, bias=bias_of(1)).then_inc(freed(*name), 1)

            def ml_exps(l, h):
                n = HEADS * l + h
                e = probs[:, n % 2, 0:3 * P]
                act.wait_ge(ml_arg, n + 1)
                act.activation(e, e, ACT.Exp, scale=-1.0).then_inc(ml_exp, 1)
                if n >= 2:
                    act.wait_ge(ml_head, n - 1)
                act.activation(work[:, (n % 2) * T:(n % 2 + 1) * T], S[:, 1, T:2 * T], ACT.Exp, scale=-1.0)\
                   .then_inc(ml_em, 1)

            def ml_den(l, h):
                n = HEADS * l + h
                act.wait_ge(ml_num, n + 1)
                act.activation(work[:, 2 * T:3 * T], S[:, 3, 0:T], ACT.Abs).then_inc(ml_abs, 1)

            def mixer(l):
                square(2 * l)
                for j in range(4):
                    copy(kmem[:, 2 * j:2 * j + 2, :], None, "kv", l, j)
                root_mean(2 * l)
                for j in range(4):
                    b = filled(act, "ax", l, j)
                    act.activation(ax_pad[:, 2 * j:2 * j + 2, PAD:PAD + T], b[:, :].rearrange("p (k t) -> p k t", k=2),
                                   ACT.Copy).then_inc(freed("ax", l, j), 1)
                act.wait_ge(abs_f, l + 1)
                act.activation(rows[3], rows[2], ACT.Exp, scale=-1.0).then_inc(exp_f, 1)
                for j in range(4):
                    copy(qxa[:, 2 * j:2 * j + 2, :], None, "qa", l, j)
                for n, (kind, j) in enumerate(MEM_SLOTS):
                    if kind == "o":
                        gated(l, kind, j, ACT.Sigmoid, ogate[:, 2 * j:2 * j + 2, :])
                    else:
                        gated(l, kind, j, ACT.Gelu_apprx_tanh, ygelu[:, 2 * j:2 * j + 2, :])
                    if 1 <= n < 1 + HEADS:
                        take_over(("mem", l, n - 1))
                    if n < HEADS:
                        exps(("mem", l, n))
                act.wait_ge(conv_ml, l + 1)
                act.activation(cml, cml, ACT.Silu).then_inc(silu_ml, 1)
                for name, to, bias_name in (("rga", ra, "rg_b_a"), ("rgx", ib, "rg_b_x")):
                    for g in range(4):
                        two_biased(lambda m: to[:, 2 * g + m, :], (name, l, g), ACT.Sigmoid,
                                   lambda m: vec(bias_name, l)[:, 2 * g + m:2 * g + m + 1])
                if l == 0:
                    act.wait_ge(lam_done, 1)
                evacuated(act, "rga", l, 3)
                act.wait_ge(conv_rg, l + 1)
                for k in range(KD):
                    c = 8 * l + k
                    act.activation(tanh_t[:, k, :], ra[:, k, :], ACT.Tanh, scale=softp[:, 0, c:c + 1])
                for k in range(KD):
                    c = 8 * l + k
                    last = act.activation(ra[:, k, :], ra[:, k, :], ACT.Exp, scale=softp[:, 1, c:c + 1])
                last.then_inc(decay, 1)
                for g in range(4):
                    copy(vml[:, :, g * 256:(g + 1) * 256], lambda b: b[:, :].rearrange("p (m c) -> p m c", m=TT),
                         "mlv", l, g)
                act.wait_ge(rg_s, l + 1)
                act.activation(pages[17], pages[17], ACT.Sqrt, scale=2.0).then_inc(rg_root, 1)
                for j in range(12):
                    if j == 0:
                        act.wait_ge(a_ready, l + 1)
                    if j == 8:
                        act.wait_ge(rg_done, l + 1)
                    g, q = j // 4, j % 4
                    two_biased(lambda m: gates[g][:, 2 * q + m, :], ("gt", l, j), ACT.Sigmoid,
                               lambda m: vec("b_merge", l, 24)[:, 2 * j + m:2 * j + m + 1])
                    if ML_FIRST + 2 <= j < ML_FIRST + 2 + HEADS:
                        ml_den(l, j - ML_FIRST - 2)
                    if ML_FIRST <= j < ML_FIRST + HEADS:
                        ml_exps(l, j - ML_FIRST)
                act.wait_ge(ml_head, HEADS * (l + 1))
                act.wait_ge(rg_done, l + 1)
                act.activation(sq, hn, ACT.Square).then_inc(ml_sq, 1)
                for j in range(2):
                    b = filled(act, "mlsum", l, j)
                    act.activation(ml_root[:, j * 512:(j + 1) * 512], b[:, :], ACT.Sqrt, bias=eps_t[:, :],
                                   scale=1.0 / 256).then_inc(freed("mlsum", l, j), 1)
                square(2 * l + 1)
                root_mean(2 * l + 1)

            act.wait_ge(first_loaded, 16 * len(FIRST_LOADS))
            act.wait_ge(init_done, 1)
            for q in range(4):
                act.activation(sq_mem[:, 2 * q:2 * q + 2, :], memT[:, 2 * q:2 * q + 2, :], ACT.Square)\
                   .then_inc(memsq, 1)
            for to, of in SMALL_LOADS:
                act.dma_start(to, of).then_inc(small_loaded, 16)
            b = filled(act, "msum")
            act.activation(mem_rstd[:, :], b[:, 0:T], ACT.Sqrt, bias=eps_t[:, :], scale=1.0 / D)\
               .then_inc(freed("msum"), 1)
            act.wait_ge(lam_abs, 1)
            act.activation(softp[:, 1, :], softp[:, 0, :], ACT.Exp, scale=-1.0).then_inc(lam_exp, 1)
            mixer(0)
            hidden("a", FF1)
            mixer(1)

            act.wait_ge(gate_arg, 1)
            act.activation(gv[:, :, 1:2], gv[:, :, 0:1], ACT.Exp).then_inc(gate_exp, 1)
            for j in range(4):
                copy(htok[:, j // 2, (j % 2) * 512:(j % 2 + 1) * 512], None, "htok", j)

            def experts(x):
                def gathered_half(count):
                    act.wait_ge(x.gathered, count)
                    act.activation(xg[:, 0:4, :], S[:, 2, :].rearrange("p (k t) -> p k t", k=4), ACT.Copy)\
                       .then_inc(x.xg_ready, 1)

                gathered_half(1)
                with act.Fori(0, EXPERTS) as e:
                    for j in range(FF1):
                        if j >= 4:
                            o = x.w(1, j - 4)
                            act.wait_ge(x.bank_free[o % NB], e * (MOE_OUTS // NB) + o // NB + 1)
                        o = x.w(0, j)
                        act.wait_ge(x.bank_full, e * MOE_OUTS + o + 1)
                        act.activation(silu_tmp[:, j % 4, 0:2 * CAP], O[o % NB][:, 0:2 * CAP], ACT.Silu)\
                           .then_inc(x.bank_free[o % NB], 1)
                    gathered_half(e + 2)
                    act.wait_ge(x.acc_units, e * FF1 + x.acc + FF1)
                    act.activation(y_tok[:, 0:512], S[:, 0, :], ACT.Copy).then_inc(x.y_ready, 1)

            experts(main)
            act.wait_ge(routed, 1)
            with act.If(act.value_load(flag[0:1, 0:1], min_val=0, max_val=1) != 0):
                experts(again)

            square(N_FINAL1)
            act.dma_start(onehot, a["onehot"]).then_inc(table_loaded, 16)
            root_mean(N_FINAL1)
            square(N_FFN1B)
            root_mean(N_FFN1B)
            for g in range(GROUPS):
                copy(brow[:, g, :], lambda b: b[0:HA, :], "brow", g)
            for g in range(GROUPS):
                evacuated(act, "brow", g)
            act.dma_start(brow_dram.rearrange("(g h) m -> h g m", g=GROUPS), brow).then_inc(rows_stored, 16)
            act.wait_ge(rows_stored, 16)
            for g in range(GROUPS):
                shifted = bass.AP(tensor=brow_dram.tensor, offset=g * HA * 512, ap=[[1, P], [512, HA], [1, 384]])
                act.dma_start(brevs[g], shifted).then_inc(rows_loaded[g], 16)
            hidden(1, FF2)
            square(N_MIXB)
            for h in range(GROUPS * HA):
                if h == BIAS_NORM:
                    root_mean(N_MIXB)
                copy(bias[:, h, :], lambda b: b[:, 0:384], "bias", h)
            for kind, to in (("qd", qd), ("kd", kd)):
                for j in range(6):
                    copy(to[:, 2 * j:2 * j + 2, :], None, kind, j)
            for halves, summed, _turned, s, t, v in slots_b():
                kind, j = next((unit for unit, m in halves if m == 1), (None, None))
                if kind in ("qb", "kb"):
                    c = j if kind == "qb" else 4
                    copy(qk[:, c * 512:(c + 1) * 512], None, kind, j)
                    evacuated(act, kind, j)
                    act.activation(scr[:, c * 512:(c + 1) * 512], qk[:, c * 512:(c + 1) * 512], ACT.Square)\
                       .then_inc(qk_sq, 1)
                if kind == "vb":
                    copy(vb, lambda b: b[:, :].rearrange("p (m c) -> p m c", m=TT), kind, j)
                if kind == "gate":
                    b = filled(act, kind, j)
                    for m in range(2):
                        c = 2 * j + m
                        last = act.activation(gate2[:, c * T:(c + 1) * T], b[:, m * T:(m + 1) * T], ACT.Sigmoid,
                                              bias=vec("b_gate_2", None, 16)[:, c:c + 1])
                    last.then_inc(freed(kind, j), 1)
                if summed is not None:
                    c, b = summed, filled(act, "qksum", summed)
                    act.activation(scr[:, c * 512:(c + 1) * 512], b[:, :], ACT.Sqrt, bias=eps_t[:, :],
                                   scale=1.0 / P).then_inc(freed("qksum", c), 1)
                if t:
                    take_over(t)
                if s:
                    exps(s)
            square(N_FFN2B)
            root_mean(N_FFN2B)
            hidden(2, FF2)
            square(N_FINALB)
            root_mean(N_FINALB)
            for q in range(4):
                act.wait_ge(h_ready, 8 * N_FINALB + 2 * q + 2)
                act.dma_start(out[:, 2 * q:2 * q + 2, :], hT[:, 2 * q:2 * q + 2, :]).then_inc(stored, 16)
            act.wait_ge(stored, 64)

        @block.gpsimd
        def _(pool):
            for l in range(2):
                for h in range(HEADS):
                    n = HEADS * l + h
                    e = probs[:, n % 2, 0:3 * P].rearrange("p (b j) -> p b j", b=3)[:, 0:3:2, :]
                    pool.wait_ge(ml_exp, n + 1)
                    pool.affine_select(out=e, in_=e, pattern=[[0, 2], [1, P]], compare_op=ALU.is_ge, fill=0.0,
                                       base=0, channel_multiplier=-1).then_inc(ml_mask, 1)

        @block.vector
        def _(dve):
            steps = [0]

            def step(ins):
                steps[0] += 1
                ins.then_inc(dve_step, 1)
                dve.wait_ge(dve_step, steps[0])

            def log1p_half(q, e, z, z2):
                step(dve.tensor_scalar(z, e, 2.0, None, ALU.add))
                step(dve.reciprocal(z, z))
                step(dve.tensor_tensor(z, z, e, ALU.mult))
                step(dve.tensor_tensor(z2, z, z, ALU.mult))
                step(dve.tensor_scalar(q, z2, 1.0 / (2 * SERIES + 1), None, ALU.mult))
                for k in range(SERIES - 1, 0, -1):
                    step(dve.scalar_tensor_tensor(q, q, 1.0 / (2 * k + 1), z2, ALU.add, ALU.mult))
                step(dve.scalar_tensor_tensor(q, q, 1.0, z, ALU.add, ALU.mult))

            def norm(n, to):
                evacuated(dve, "nsum", n)
                step(dve.reciprocal(root[:, :], root[:, :]))
                g = vec(*NORM_G[n])
                for k in range(KD):
                    dve.scalar_tensor_tensor(to[:, k, :], xT[:, k, :], g[:, k:k + 1], root[:, :], ALU.mult, ALU.mult)\
                       .then_inc(h_ready, 1)

            def sum_squares(n):
                assert n in SUMMED
                s = (sq if n <= N_FINAL1 else sq_b)
                first, second_, third = [s[:, 2 * q:2 * q + 2, :] for q in range(3)]
                dve.wait_ge(squares, 4 * n + 2)
                step(dve.tensor_tensor(first, first, second_, ALU.add))
                dve.wait_ge(squares, 4 * n + 3)
                dve.tensor_tensor(first, first, third, ALU.add).then_inc(sq_sum, 1)

            def norm_memory(l):
                g = vec("mem_norm_g", l)
                for k in range(KD):
                    dve.scalar_tensor_tensor(memn[:, k, :], memT[:, k, :], g[:, k:k + 1], mem_rstd[:, :], ALU.mult,
                                             ALU.mult).then_inc(memn_ready, 1)

            def quarter(q):
                return xT[:, 2 * q:2 * q + 2, :].rearrange("p k t -> p (k t)")

            def hidden(f, ff, h):
                for j in range(ff):
                    evacuated(dve, "w1", f, j)
                    b = filled(dve, "w3", f, j)
                    dve.tensor_tensor(h[:, 2 * j:2 * j + 2, :].rearrange("p k t -> p (k t)"), silu_tmp[:, j % 4, :],
                                      b[:, :], ALU.mult).then_inc(freed("w3", f, j), 1)

            def second(ffn, count, weight, n):
                for q in range(4):
                    if q < 3:
                        dve.wait_ge(acc_quarter, 3 * ffn + q + 1)
                    else:
                        sum_squares(n)
                        dve.wait_ge(acc_units, count)
                    dve.scalar_tensor_tensor(quarter(q), S[:, q, :], weight, quarter(q), ALU.mult, ALU.add)\
                       .then_inc(x_added, 1)

            def mixed(l, n):
                for q in range(4):
                    if q == 3:
                        sum_squares(n)
                    b = filled(dve, "wout", l, q)
                    dve.tensor_tensor(quarter(q), quarter(q), b[:, :], ALU.add).then_inc(freed("wout", l, q), 1)

            def convolve(x, to, w, bias_, done):
                for k in range(KD):
                    last = dve.tensor_scalar(to[:, k, :], x[:, k, 0:T], w[:, k:k + 1], bias_[:, k:k + 1], ALU.mult,
                                             ALU.add)
                step(last)
                for tap in range(1, PAD + 1):
                    for k in range(KD):
                        last = dve.scalar_tensor_tensor(to[:, k, :], x[:, k, tap:tap + T],
                                                        w[:, tap * KD + k:tap * KD + k + 1], to[:, k, :], ALU.mult,
                                                        ALU.add)
                    if tap < PAD:
                        step(last)
                last.then_inc(done, 1)

            def maxima(s):
                n = STEP[s]
                par = n % 2
                dve.wait_ge(scores, n + 1)
                if s[0] == "dil":
                    h, m = s[1:]
                    dve.wait_ge(exped, n)
                    shifts = bias.rearrange("p (g h) m -> p g h m", g=GROUPS)[:, :, h, P * (1 - m):P * (1 - m) + T]
                    dve.scalar_tensor_tensor(work[:, :].rearrange("p (g t) -> p g t", g=GROUPS),
                                             S2[:, 0:768].rearrange("p (g t) -> p g t", g=GROUPS), DA ** -0.5,
                                             shifts, ALU.mult, ALU.add).then_inc(scores_free, 1)
                    dve.wait_ge(scores_free, n + 1)
                    step(dve.reduce_max(smax[:, par, 0, 0:1], work[:, :], AXX))
                    dve.tensor_scalar(smax[:, par, 1, 0:1], smax[:, par, 0, 0:1], -1.0, None, ALU.mult)\
                       .then_inc(maxed, 1)
                    return
                scale = 256 ** -0.5 if s[0] == "mem" else P ** -0.5
                step(dve.reduce_max(smax[:, par, 0, :], S[:, 0, :].rearrange("p (m t) -> p m t", m=TT), AXX))
                dve.tensor_scalar(smax[:, par, 1, :], smax[:, par, 0, :], -scale, None, ALU.mult).then_inc(maxed, 1)

            def normalise(s):
                n = STEP[s]
                par = n % 2
                dve.wait_ge(exped, n + 1)
                if s[0] == "dil":
                    step(dve.reciprocal(ssum[:, par, 1, 0:1], ssum[:, par, 0, 0:1]))
                    dve.tensor_scalar(probs[:, par, :], probs[:, par, :], ssum[:, par, 1, 0:1], None, ALU.mult)\
                       .then_inc(probs_ready, 1)
                    return
                dve.reciprocal(ssum[:, par, 1, :], ssum[:, par, 0, :]).then_inc(scores_free, 1)
                dve.wait_ge(scores_free, n + 1)
                for m in range(TT):
                    c = slice(m * T, (m + 1) * T)
                    last = dve.tensor_scalar(probs[:, par, c], probs[:, par, c], ssum[:, par, 1, m:m + 1], None,
                                             ALU.mult)
                last.then_inc(probs_ready, 1)

            def values(s):
                n = STEP[s]
                b = filled(dve, "pv", n)
                if s[0] == "mem":
                    h = s[2]
                    ins = dve.tensor_copy(yxa[:, 2 * h:2 * h + 2, :].rearrange("p k t -> p (k t)"), b[:, :])
                elif s[0] == "dil":
                    h, m = s[1:]
                    r = DA * (h % 2)
                    ins = dve.tensor_copy(o_a[r:r + DA, h // 2, m * P:(m + 1) * P], b[r:r + DA, 0:P])
                else:
                    ins = dve.tensor_copy(o_b[:, s[1], :], b[:, 0:T])
                ins.then_inc(freed("pv", n), 1)

            def gate_rows(l):
                b = filled(dve, "if", l)
                bi, bf = vec("ml_b_i", l, 1)[0:4, :], vec("ml_b_f", l, 1)[0:4, :]
                i_, f_, af, e_, z, z2, q, u = rows
                dve.tensor_scalar(i_, b[0:4, 0:T], bi, None, ALU.add)
                dve.tensor_scalar(f_, b[0:4, T:2 * T], bf, None, ALU.add).then_inc(freed("if", l), 1)
                evacuated(dve, "if", l)
                dve.scalar_tensor_tensor(af, f_, -1.0, f_, ALU.mult, ALU.max).then_inc(abs_f, 1)
                dve.wait_ge(exp_f, l + 1)
                log1p_half(q, e_, z, z2)
                step(dve.tensor_scalar(u, f_, 0.0, None, ALU.min))
                step(dve.scalar_tensor_tensor(u, q, -2.0, u, ALU.mult, ALU.add))
                step(dve.tensor_tensor_scan(z, ones_row[0:4, :], u, 0.0, ALU.mult, ALU.add))
                step(dve.tensor_tensor(arow, i_, z, ALU.subtract))
                step(dve.tensor_tensor_scan(mrow[:, 0, :], arow, arow, 0.0, ALU.max, ALU.max))
                dve.tensor_tensor(mrow[:, 1, :], mrow[:, 0, :], z, ALU.add).then_inc(a_ready, 1)

            def ml_args(l, h):
                n = HEADS * l + h
                dve.wait_ge(ml_scores, n + 1)
                if n >= 2:
                    dve.wait_ge(ml_num, n - 1)
                w = probs[:, n % 2, :]
                for s in range(TT):
                    last = dve.tensor_scalar(w[:, s * T:s * T + T - s * P], S[:, 1, s * P:T], acol[:, s, h:h + 1], 0.0,
                                             ALU.subtract, ALU.max)
                last.then_inc(ml_arg, 1)

            def ml_weights(l, h):
                n = HEADS * l + h
                dve.wait_ge(ml_mask, n + 1)
                w = probs[:, n % 2, 0:3 * P]
                dve.tensor_tensor(w, w, S[:, 0, 0:3 * P], ALU.mult).then_inc(ml_w, 1)

            def ml_out(l, h):
                n = HEADS * l + h
                dve.wait_ge(ml_em, n + 1)
                dve.wait_ge(ml_abs, n + 1)
                r = work[:, (n % 2) * T:(n % 2 + 1) * T]
                step(dve.tensor_tensor(r, r, work[:, 2 * T:3 * T], ALU.max))
                step(dve.reciprocal(r, r))
                for m in range(2):
                    last = dve.tensor_tensor(hn[:, 2 * h + m, :], S[:, 2, m * T:(m + 1) * T], r, ALU.mult)
                step(last)
                dve.tensor_tensor(hn[:, 2 * h:2 * h + 2, :], hn[:, 2 * h:2 * h + 2, :], ogate[:, 2 * h:2 * h + 2, :],
                                  ALU.mult).then_inc(ml_head, 1)

            def merge(l, branch):
                for j in range(4):
                    c = slice(2 * j, 2 * j + 2)
                    g = gates[branch][:, c, :].rearrange("p k t -> p (k t)")
                    to = merged[:, c, :].rearrange("p k t -> p (k t)")
                    name = ("br", l, 4 * branch + j)
                    evacuated(dve, "gt", l, 4 * branch + j)
                    b = filled(dve, *name)
                    if branch == 0:
                        dve.tensor_tensor(to, g, b[:, :], ALU.mult).then_inc(freed(*name), 1)
                        evacuated(dve, *name)
                        continue
                    dve.tensor_tensor(g, g, b[:, :], ALU.mult).then_inc(freed(*name), 1)
                    evacuated(dve, *name)
                    if branch == 2:
                        step(dve.tensor_tensor(to, to, g, ALU.add))
                    else:
                        dve.tensor_tensor(to, to, g, ALU.add).then_inc(merged_ready, 1)

            def mixer(l):
                if l == 0:
                    sum_squares(N_MIX0)
                for j in range(4, 8):
                    if j == KV_NORM:
                        norm(2 * l, hT)
                    b = filled(dve, "kv", l, j)
                    h = j - 4
                    dve.tensor_copy(vmem[:, :, h * 256:(h + 1) * 256], b[:, :].rearrange("p (m c) -> p m c", m=TT))\
                       .then_inc(freed("kv", l, j), 1)
                dve.memset(ax_pad[:, :, 0:PAD], 0.0)
                step(dve.memset(mu_pad[:, :, 0:PAD], 0.0))
                for j in range(4):
                    b = filled(dve, "mu", l, j)
                    dve.tensor_copy(mu_pad[:, 2 * j:2 * j + 2, PAD:PAD + T],
                                    b[:, :].rearrange("p (k t) -> p k t", k=2)).then_inc(freed("mu", l, j), 1)
                gate_rows(l)
                for j in range(4):
                    evacuated(dve, "ax", l, j)
                convolve(ax_pad, xc, vec("conv_rg_w", l, 32), vec("conv_rg_b", l), conv_rg)
                for j in range(4):
                    evacuated(dve, "mu", l, j)
                convolve(mu_pad, cml, vec("conv_ml_w", l, 32), vec("conv_ml_b", l), conv_ml)
                for n in range(HEADS + 2):
                    if n < HEADS:
                        maxima(("mem", l, n))
                        normalise(("mem", l, n))
                    if n >= 2:
                        values(("mem", l, n - 2))
                for g in range(4):
                    b = filled(dve, "mlq", l, g)
                    dve.tensor_copy(qml[:, 2 * g:2 * g + 2, :].rearrange("p k t -> p (k t)"), b[:, :])\
                       .then_inc(freed("mlq", l, g), 1)
                for g in range(4):
                    b = filled(dve, "mlk", l, g)
                    dve.tensor_scalar(kml[:, 2 * g:2 * g + 2, :].rearrange("p k t -> p (k t)"), b[:, :], 256 ** -0.5,
                                      None, ALU.mult).then_inc(freed("mlk", l, g), 1)
                b = filled(dve, "acol", l)
                dve.tensor_copy(acol[:, :, :], b[:, 0:8].rearrange("p (m h) -> p m h", m=TT))\
                   .then_inc(freed("acol", l), 1)
                i_flat, t_flat, s_flat = pages[14], tanh_v, pages[17]
                dve.wait_ge(decay, l + 1)
                step(dve.tensor_scalar(s_flat, t_flat, 1.0, None, ALU.add))
                step(dve.reciprocal(s_flat, s_flat))
                dve.scalar_tensor_tensor(s_flat, t_flat, 1e-34, s_flat, ALU.max, ALU.mult).then_inc(rg_s, 1)
                evacuated(dve, "rgx", l, 3)
                step(dve.tensor_tensor(i_flat, i_flat, pages[11], ALU.mult))
                dve.wait_ge(rg_root, l + 1)
                step(dve.tensor_tensor(i_flat, i_flat, s_flat, ALU.mult))
                for k in range(KD):
                    last = dve.tensor_tensor_scan(tanh_t[:, k, :], ra[:, k, :], ib[:, k, :], 0.0, ALU.mult, ALU.add)
                step(last)
                evacuated(dve, "ay", l, 3)
                dve.tensor_tensor(pages[10], pages[10], t_flat, ALU.mult).then_inc(rg_done, 1)
                evacuated(dve, "acol", l)
                evacuated(dve, "o", l, 3)
                for h in range(HEADS + 2):
                    if h < HEADS:
                        ml_args(l, h)
                        ml_weights(l, h)
                    if h >= 2:
                        ml_out(l, h - 2)
                merge(l, 0)
                for j in range(2):
                    evacuated(dve, "mlsum", l, j)
                step(dve.reciprocal(ml_root, ml_root))
                g = vec("ml_norm_g", l)
                for k in range(KD):
                    last = dve.scalar_tensor_tensor(hn[:, k, :], hn[:, k, :], g[:, k:k + 1],
                                                    ml_root[:, (k // 2) * T:(k // 2 + 1) * T], ALU.mult, ALU.mult)
                last.then_inc(ml_done, 1)
                merge(l, 2)
                merge(l, 1)
                mixed(l, 2 * l + 1)
                for q in range(4):
                    evacuated(dve, "wout", l, q)
                norm(2 * l + 1, hT)

            dve.memset(ones_row[:, :], 1.0)
            dve.memset(eps_t[:, :], EPS).then_inc(init_done, 1)
            dve.wait_ge(first_loaded, 16 * len(FIRST_LOADS))
            for l in range(2):
                lam = vec("rg_lambda", l)
                last = dve.scalar_tensor_tensor(softp[:, 0, 8 * l:8 * l + 8], lam, -1.0, lam, ALU.mult, ALU.max)
            last.then_inc(lam_abs, 1)
            evacuated(dve, "msum")
            step(dve.reciprocal(mem_rstd[:, :], mem_rstd[:, :]))
            norm_memory(0)
            dve.wait_ge(lam_exp, 1)
            log1p_half(softp[:, 0, :], softp[:, 1, :], softp[:, 2, :], softp[:, 3, :])
            for l in range(2):
                last = dve.tensor_scalar(softp[:, 2, 8 * l:8 * l + 8], vec("rg_lambda", l), -1.0, 0.0, ALU.mult, ALU.max)
            step(last)
            step(dve.scalar_tensor_tensor(softp[:, 0, :], softp[:, 0, :], 2.0, softp[:, 2, :], ALU.mult, ALU.add))
            step(dve.tensor_scalar(softp[:, 1, :], softp[:, 0, :], -RG_C, None, ALU.mult))
            dve.tensor_scalar(softp[:, 0, :], softp[:, 0, :], RG_C, None, ALU.mult).then_inc(lam_done, 1)
            mixer(0)
            norm_memory(1)
            hidden("a", FF1, hid)
            second(0, FF1, 1.0, N_MIX1)
            mixer(1)

            L, top, m_, c_, f1, f2, picked, gate, rank, left = [lg[:, n, :, :] for n in range(10)]
            b = filled(dve, "logit")
            dve.tensor_tensor(L[:, 0, :], b[:, 0:8], vec("router_b"), ALU.add)
            dve.tensor_tensor(L[:, 1, :], b[:, 8:16], vec("router_b"), ALU.add).then_inc(freed("logit"), 1)
            evacuated(dve, "logit")
            for m in range(TT):
                last = dve.max(top[:, m, :], L[:, m, :])
            step(last)
            dve.tensor_tensor(gv[:, :, 0:1], top[:, :, 1:2], top[:, :, 0:1], ALU.subtract).then_inc(gate_arg, 1)

            def first_of(f):
                for m in range(TT):
                    last = dve.tensor_tensor_scan(c_[:, m, :], ones_row[:, 0:8], m_[:, m, :], 0.0, ALU.mult, ALU.add)
                step(last)
                step(dve.tensor_tensor(c_, c_, m_, ALU.mult))
                step(dve.tensor_scalar(f, c_, 1.0, None, ALU.is_equal))

            for m in range(TT):
                last = dve.tensor_scalar(m_[:, m, :], L[:, m, :], top[:, m, 0:1], None, ALU.is_equal)
            step(last)
            first_of(f1)
            step(dve.tensor_scalar(left, f1, -1.0, 1.0, ALU.mult, ALU.add))
            for m in range(TT):
                last = dve.scalar_tensor_tensor(m_[:, m, :], L[:, m, :], top[:, m, 1:2], left[:, m, :], ALU.is_equal,
                                                ALU.mult)
            step(last)
            first_of(f2)
            dve.tensor_tensor(picked, f1, f2, ALU.add).then_inc(sel_ready, 1)
            dve.wait_ge(gate_exp, 1)
            step(dve.tensor_scalar(gv[:, :, 2:3], gv[:, :, 1:2], 1.0, None, ALU.add))
            step(dve.reciprocal(gv[:, :, 3:4], gv[:, :, 2:3]))
            step(dve.tensor_tensor(gv[:, :, 4:5], gv[:, :, 1:2], gv[:, :, 3:4], ALU.mult))
            for m in range(TT):
                last = dve.tensor_scalar(gate[:, m, :], f1[:, m, :], gv[:, m, 3:4], None, ALU.mult)
            step(last)
            for m in range(TT):
                last = dve.scalar_tensor_tensor(gate[:, m, :], f2[:, m, :], gv[:, m, 4:5], gate[:, m, :], ALU.mult,
                                                ALU.add)
            step(last)
            b = filled(dve, "rank")
            step(dve.scalar_tensor_tensor(rank, b[:, 0:16].rearrange("p (m e) -> p m e", m=TT), 1.0, picked, ALU.add,
                                          ALU.mult))
            dve.reduce_max(cnt[:, 0:1], b[:, 16:24], AXX).then_inc(freed("rank"), 1)
            evacuated(dve, "rank")
            dve.tensor_scalar(flag[:, :], cnt[:, 0:1], float(CAP), None, ALU.is_gt).then_inc(routed, 1)
            step(dve.tensor_scalar(rank, rank, -1.0, None, ALU.add))

            def pick(x):
                dve.memset(GT[:, 0:T], 0.0)
                for half in range(2):
                    dve.memset(y_tok[:, half * 512:(half + 1) * 512], 0.0).then_inc(x.y_ready, 1)
                dve.memset(Pall[:, :, EXPERTS * CAP:(EXPERTS + 1) * CAP], 0.0)
                slots_of(0).then_inc(picks, 1)
                for m in range(TT):
                    for e in range(EXPERTS):
                        last = dve.tensor_scalar(Pg[:, m, e, :], iota, rank[:, m, e:e + 1], gate[:, m, e:e + 1],
                                                 ALU.is_equal, ALU.mult)
                last.then_inc(picks, 1)

            def slots_of(e):
                for m in range(TT):
                    last = dve.tensor_scalar(Pall[:, m, e * CAP:(e + 1) * CAP], iota, rank[:, m, e:e + 1], None,
                                             ALU.is_equal)
                return last

            def gathered_half(x, count):
                dve.wait_ge(x.gathered, count)
                dve.tensor_copy(xg[:, 4:8, :], S[:, 3, :].rearrange("p (k t) -> p k t", k=4))\
                   .then_inc(x.xg_ready, 1)

            def gate_columns(x, o):
                gathered_half(x, 1)
                for j in range(4):
                    dve.wait_ge(x.bank_full, o + j + 1)
                    dve.tensor_copy(GT[:, T * (1 + 2 * j):T * (3 + 2 * j)], O[(o + j) % NB][:, :])\
                       .then_inc(x.bank_free[(o + j) % NB], 1)
                for e in range(1, EXPERTS):
                    last = slots_of(e)
                last.then_inc(picks, 1)

            def experts(x):
                with dve.Fori(0, EXPERTS) as e:
                    for j in range(FF1):
                        o1, o = x.w(0, j), x.w(1, j)
                        dve.wait_ge(x.bank_free[o1 % NB], e * (MOE_OUTS // NB) + o1 // NB + 1)
                        dve.wait_ge(x.bank_full, e * MOE_OUTS + o + 1)
                        dve.tensor_tensor(hid_e[:, 2 * j:2 * j + 2, :].rearrange("p k t -> p (k t)"),
                                          silu_tmp[:, j % 4, 0:2 * CAP], O[o % NB][:, 0:2 * CAP], ALU.mult)\
                           .then_inc(x.bank_free[o % NB], 1)
                        if j == 0:
                            for q in range(4):
                                o = x.comb(q)
                                dve.wait_ge(x.bank_full, e * MOE_OUTS + o + 1)
                                dve.tensor_tensor(quarter(q), quarter(q), O[o % NB][:, :], ALU.add)\
                                   .then_inc(x.bank_free[o % NB], 1)
                            for q in range(4):
                                o = x.comb(q)
                                dve.wait_ge(x.bank_free[o % NB], e * (MOE_OUTS // NB) + o // NB + 1)
                    gathered_half(x, e + 2)
                    dve.wait_ge(x.acc_units, e * FF1 + x.acc + FF1)
                    dve.tensor_copy(y_tok[:, 512:1024], S[:, 1, :]).then_inc(x.y_ready, 1)
                o = x.o + EXPERTS * MOE_OUTS
                for q in range(4):
                    dve.wait_ge(x.bank_full, o + q + 1)
                    dve.tensor_tensor(quarter(q), quarter(q), O[(o + q) % NB][:, :], ALU.add)\
                       .then_inc(x.bank_free[(o + q) % NB], 1)
                for q in range(4):
                    dve.wait_ge(x.bank_free[(o + q) % NB], (o + q) // NB + 1)

            pick(main)
            gate_columns(main, plan.o["gtr", 0])
            experts(main)
            dve.wait_ge(routed, 1)
            with dve.If(dve.value_load(flag[0:1, 0:1], min_val=0, max_val=1) != 0):
                dve.tensor_scalar(rank, rank, -float(CAP), None, ALU.add).then_inc(ranks_moved, 1)
                dve.wait_ge(ranks_moved, 1)
                pick(again)
                gate_columns(again, 0)
                experts(again)
            dve.memset(cnt[:, 1:2], 0.0).then_inc(moe_done, 1)

            norm(N_FINAL1, xT)
            dve.wait_ge(h_ready, 8 * N_FINAL1 + 8)
            norm(N_FFN1B, hT)
            hidden(1, FF2, hid2)
            acc = FF1 + EXPERTS * FF1 + FF2
            second(1, acc, 0.5, N_MIXB)
            dve.wait_ge(x_added, 8)
            norm(N_MIXB, hT)
            for j in range(6):
                b = filled(dve, "vd", j)
                dve.tensor_copy(vd[:, :, j * 256:(j + 1) * 256], b[:, :].rearrange("p (m c) -> p m c", m=TT))\
                   .then_inc(freed("vd", j), 1)
            for h in range(4):
                evacuated(dve, "bias", GROUPS * HA - 1 - h)
            for _halves, summed, turned, s, t, v in slots_b():
                if turned is not None:
                    c = turned
                    dve.wait_ge(qk_norm, c + 1)
                    b = filled(dve, "rot", c)
                    for m in range(2):
                        w = slice((2 * c + m) * T, (2 * c + m + 1) * T)
                        dve.tensor_tensor(qk[:, w], qk[:, w], rope[:, 0, :], ALU.mult)
                        last = dve.tensor_tensor(scr[:, w], b[:, m * T:(m + 1) * T], rope[:, 1, :], ALU.mult)
                    last.then_inc(freed("rot", c), 1)
                    evacuated(dve, "rot", c)
                    w = slice(c * 512, (c + 1) * 512)
                    dve.tensor_tensor(qk[:, w], qk[:, w], scr[:, w], ALU.add).then_inc(qk_ready, 1)
                if s:
                    maxima(s)
                    normalise(s)
                if v:
                    values(v)
                if summed is not None:
                    c = summed
                    w = slice(c * 512, (c + 1) * 512)
                    evacuated(dve, "qksum", c)
                    step(dve.reciprocal(scr[:, w], scr[:, w]))
                    g = vec("k_norm_2" if c == 4 else "q_norm_2", None, 1)
                    dve.scalar_tensor_tensor(qk[:, w], qk[:, w], g, scr[:, w], ALU.mult, ALU.mult)\
                       .then_inc(qk_norm, 1)
            acc += 2
            for j in range(4):
                evacuated(dve, "gate", j)
            dve.wait_ge(acc_units, acc)
            for q in range(4):
                w = slice(q * 512, (q + 1) * 512)
                last = dve.tensor_tensor(gate2[:, w], gate2[:, w], S[:, q, :], ALU.mult)
            last.then_inc(bra_free, 1)
            dve.wait_ge(bra_free, 1)
            for j in range(4):
                w, w1 = slice(j * 512, (j + 1) * 512), slice(2048 + j * 512, 2048 + (j + 1) * 512)
                evacuated(dve, "gate", 4 + j)
                b = filled(dve, "brb", j)
                dve.tensor_tensor(gate2[:, w1], gate2[:, w1], b[:, :], ALU.mult).then_inc(freed("brb", j), 1)
                evacuated(dve, "brb", j)
                dve.tensor_tensor(gate2[:, w], gate2[:, w], gate2[:, w1], ALU.add).then_inc(merged_ready, 1)
            mixed(2, N_FFN2B)
            for q in range(4):
                evacuated(dve, "wout", 2, q)
            norm(N_FFN2B, hT)
            hidden(2, FF2, hid2)
            acc += FF2
            second(2, acc, 0.5, N_FINALB)
            dve.wait_ge(x_added, 12)
            norm(N_FINALB, hT)



def _buckets(rel):
    n, exact = 16, 8
    a = np.abs(rel)
    af = np.maximum(a, 1).astype(np.float32)
    large = exact + (np.log(af / np.float32(exact)) / np.float32(math.log(1024 / exact))
                     * np.float32(n - exact)).astype(np.int32)
    large = np.minimum(large, n - 1)
    return np.where(rel > 0, n, 0) + np.where(a < exact, a, large)


def _constants():
    eye = np.eye(P, dtype=np.float32)
    n = np.arange(P)
    rot = np.zeros((P, P), np.float32)
    rot[n[1::2], n[0::2]] = -1.0
    rot[n[0::2], n[1::2]] = 1.0
    mats = np.concatenate([eye, np.ones((P, P), np.float32), eye[::-1], rot,
                           (n[:, None] < n[None, :]).astype(np.float32),
                           np.broadcast_to(n.astype(np.float32), (P, P))], axis=1)
    sel = np.kron(np.eye(HEADS, dtype=np.float32), np.ones((1, P), np.float32))
    t = np.arange(T)
    freq = np.float32(10000.0) ** (-np.arange(32, dtype=np.float32) / np.float32(32))
    ang = np.concatenate([(t // 64).astype(np.float32)[:, None] * freq, (t % 64).astype(np.float32)[:, None] * freq],
                         axis=-1)
    rope = np.stack([np.repeat(f(ang), 2, axis=1).T for f in (np.cos, np.sin)], axis=1).astype(np.float32)
    rel = np.arange(512) - 255
    onehot = np.zeros((33, GROUPS, 512), np.float32)
    for g, d in enumerate(DIL):
        seen = (rel % d == 0) & (np.abs(rel) <= 64 * d)
        for c in np.flatnonzero(seen):
            onehot[_buckets(rel[c:c + 1])[0], g, c] = 1.0
        onehot[32, g, ~seen] = NEG
    return {"mats": mats, "sel": sel, "rope": rope, "onehot": onehot}


def _features(v):
    v = np.asarray(v).reshape(-1, P)
    return v.T


def _columns_of(w):
    *lead, k, n = w.shape
    w = w.reshape(*lead, k // P, P, n // UC, UC)
    at = len(lead)
    w = np.moveaxis(w, (at + 2, at + 1, at), (at, at + 1, at + 2))
    return np.ascontiguousarray(w).reshape(*lead, n // UC, P, -1)


def _rows_of(w):
    *lead, f, n = w.shape
    w = w.reshape(*lead, f // 256, 2, P, n)
    w = np.swapaxes(w, len(lead) + 1, len(lead) + 2)
    return np.ascontiguousarray(w).reshape(*lead, f // 256, P, 2 * n)


def _lay_out(i):
    g = {n: np.asarray(v) for n, v in i.items()}
    cols = []
    for l in range(2):
        for name in ("norm_mix_g", "mem_norm_g", "norm_ffn_g", "conv_rg_w", "conv_rg_b", "rg_b_a", "rg_b_x",
                     "rg_lambda", "conv_ml_w", "conv_ml_b", "ml_norm_g", "b_merge"):
            cols.append(_features(g[name][l]))
        for name in ("ml_b_i", "ml_b_f"):
            cols.append(np.pad(g[name][l], (0, P - HEADS))[:, None])
    for name in ("final_norm_g", "ffn1_norm_2", "mix_norm_2", "b_gate_2", "q_norm_2", "k_norm_2", "ffn2_norm_2",
                 "final_norm_2"):
        cols.append(_features(g[name]))
    cols.append(np.broadcast_to(g["router_b"][0], (P, EXPERTS)))
    w_in = g["w_in"]
    a = {
        "xT": g["x"][0].T.reshape(KD, P, T).transpose(1, 0, 2),
        "memT": g["mem"][0].T.reshape(KD, P, T).transpose(1, 0, 2),
        "vecs": np.concatenate(cols, axis=1),
        "wif": w_in[:, :, 4096:4104].reshape(2, KD, P, 8).transpose(2, 0, 1, 3),
        "wr": g["router_w"][0].reshape(KD, P, EXPERTS).transpose(1, 0, 2),
        "btab": np.concatenate([g["rel_bias_2"], np.ones((1, 24), np.float32)]),
        "w_in": _columns_of(np.concatenate([w_in[:, :, :4096], w_in[:, :, 4104:]], axis=2)).reshape(64, P, 2048),
        "w_kv": _columns_of(g["w_kv"]).reshape(16, P, 2048),
        "moe_w1": _columns_of(g["moe_w1"][0]), "moe_w3": _columns_of(g["moe_w3"][0]),
        "moe_w2": _rows_of(g["moe_w2"][0]),
        "ffn_w1": _columns_of(g["ffn_w1"][0]), "ffn_w3": _columns_of(g["ffn_w3"][0]),
        "ffn_w2": _rows_of(g["ffn_w2"][0]),
        "w_in_2": _columns_of(g["w_in_2"][0]), "w_branch_a": _rows_of(g["w_branch_a_2"][0]),
        "w_branch_b": _columns_of(g["w_branch_b_2"][0]), "w_out_2": _columns_of(g["w_out_2"][0]),
    }
    for name in ("w_br_rg", "w_br_ml", "w_br_xa", "w_out"):
        a[name] = _columns_of(g[name]).reshape(8, P, 2048)
    for name, key in (("rga", "rg_w_a"), ("rgx", "rg_w_x"), ("mlq", "ml_w_q"), ("mlk", "ml_w_k"), ("mlv", "ml_w_v")):
        a[name] = _columns_of(g[key].reshape(2, D, UC)).reshape(2, P, 2048)
    for f in (1, 2):
        a[f"ffn{f}_w1_2"] = _columns_of(g[f"ffn{f}_w1_2"][0])
        a[f"ffn{f}_w3_2"] = _columns_of(g[f"ffn{f}_w3_2"][0])
        a[f"ffn{f}_w2_2"] = _rows_of(g[f"ffn{f}_w2_2"][0])
    a.update(_constants())
    return {n: np.ascontiguousarray(v) for n, v in a.items()}


def kernel(**inputs):
    import concourse.bacc as bacc
    from concourse.bass_utils import run_bass_kernel_spmd

    nc = bacc.Bacc("TRN2", target_bir_lowering=False, num_devices=1, dynamic_dma_scratch_size=1024)
    arrays = {}
    handles = {}
    for name, v in _lay_out(inputs).items():
        arrays[f"in_{name}"] = v
        handles[name] = nc.dram_tensor(f"in_{name}", v.shape, mybir.dt.from_np(v.dtype), kind="ExternalInput").ap()
    out = nc.dram_tensor("out", (P, KD, T), F32, kind="ExternalOutput").ap()
    build(nc, handles, out)
    r = run_bass_kernel_spmd(nc, [arrays], core_ids=[0])
    return r.results[0]["out"].transpose(1, 0, 2).reshape(D, T).T.reshape(1, T, D)
```

```python
import concourse.bass as bass
from concourse import mybir
from concourse.alu_op_type import AluOpType as ALU
from contextlib import ExitStack
import math
import numpy as np

F32 = mybir.dt.float32
I32 = mybir.dt.int32
F32R = mybir.dt.float32r
ACT = mybir.ActivationFunctionType
AXX = mybir.AxisListType.X

P = 128
T = 256
TT = T // P
D = 1024
KD = D // P
HEADS = 4
UC = 256
NS = 6
NB = 4
NW = 3
EPS = 1e-6
FF1 = 3584 // UC
FF2 = 2816 // UC
EXPERTS = 8
CAP = P
PAD = 3
SERIES = 8
GROUPS = 3
DIL = (1, 4, 16)
HA = 8
DA = 64
HB = 8
NEG = -1e30
RG_C = 8.0

PARTS = [(2048, 4096), (4096, 6144), (6144, 7168), (6144, 8192), (8192, 9216), (9216, 10240),
         (10240, 11264), (11264, 12288), (12288, 13312), (13312, 14336), (13312, 18944), (14336, 15360),
         (14336, 21504), (18480, 20528), (18944, 19968), (19968, 20992), (20528, 22576), (20992, 22016),
         (21504, 23552), (22576, 24624), (23552, 24576), (24576, 25600), (25600, 26624), (26624, 27648),
         (26672, 27696), (27648, 28672), (27696, 28720), (28672, 30720), (28720, 34352), (28720, 35888),
         (30720, 32768), (32768, 33792), (32816, 34864), (33792, 34816), (34352, 35376), (34816, 35840),
         (35376, 36400), (35888, 36912)]

VEC = {}


def _columns():
    at = 0
    for l in range(2):
        for name, n in (("norm_mix_g", 8), ("mem_norm_g", 8), ("norm_ffn_g", 8), ("conv_rg_w", 32),
                        ("conv_rg_b", 8), ("rg_b_a", 8), ("rg_b_x", 8), ("rg_lambda", 8), ("conv_ml_w", 32),
                        ("conv_ml_b", 8), ("ml_norm_g", 8), ("b_merge", 24), ("ml_b_i", 1), ("ml_b_f", 1)):
            VEC[name, l] = at
            at += n
    for name, n in (("final_norm_g", 8), ("ffn1_norm_2", 8), ("mix_norm_2", 8), ("b_gate_2", 16),
                    ("q_norm_2", 1), ("k_norm_2", 1), ("ffn2_norm_2", 8), ("final_norm_2", 8), ("router_b", 8)):
        VEC[name] = at
        at += n
    return at


NV = _columns()


class Plan:

    def __init__(self):
        self.units = []
        self.u = {}
        self.o = {}
        self.released = []
        self.n_o = 0
        self.n_acc = 0
        self.halves = []
        self.consumed = []
        self.half_of = {}

    def out(self, *name):
        self.o[name] = self.n_o
        self.n_o += 1

    def unit(self, array, index, *name, outs=1):
        self.u[name] = len(self.units)
        self.units.append((array, index))
        if outs == 1:
            self.out(*name)
        else:
            for g in range(outs):
                self.out(*name, g)
        self.released.append(("bank", self.n_o))

    def acc(self, array, index, *name):
        self.u[name] = len(self.units)
        self.units.append((array, index))
        self.n_acc += 1
        self.released.append(("acc", self.n_acc))

    def split(self, name):
        self.half_of[name] = len(self.halves)
        self.halves += [(self.u[name], name, m) for m in range(2)]
        self.consumed += [("used", len(self.halves) // 2), self.released[-1]]
        self.released[-1] = ("split", len(self.halves))

    def ffn(self, f, names, ff):
        for j in range(ff):
            for w in ("w1", "w3"):
                self.unit(names[w], j, w, f, j)
                self.split((w, f, j))
        for j in range(ff):
            self.acc(names["w2"], j, "w2", f, j)
            self.split(("w2", f, j))


N_MIX0, N_FFN0, N_MIX1, N_MOE, N_FINAL1, N_FFN1B, N_MIXB, N_FFN2B, N_FINALB = range(9)

X_MEM, X_MIX, X_RG, X_XA, X_FFN, X_DIL = (0, 5), (1, 6), (2, 7), (3, 8), (4, 9, 11), 10

SUMMED = (N_MIX0, N_FFN0, N_MIX1, N_MOE, N_MIXB, N_FFN2B, N_FINALB)

BIAS_NORM = 10
KV_NORM = 6
ML_FIRST = 3
MEM_SLOTS = [("o", j) for j in range(4)] + [("ay", j) for j in range(4)]
MIX_UNITS = [("kv", j) for j in range(8)] + [("ax", j) for j in range(4)] + [("mu", j) for j in range(4)]
DIL_UNITS = [(kind, j) for kind in ("qd", "kd", "vd") for j in range(6)]
DIL_STEPS = [("dil", h, tt) for h in range(HA) for tt in range(TT)]
GQA_STEPS = [("gqa", h) for h in range(HB)]
SLOTS_B = [("qb", 0), ("qb", 1), ("qb", 2), ("qb", 3), ("kb", 0), ("vb", 0)] + [("gate", j) for j in range(8)]


def attention_steps():
    steps = [("mem", 0, h) for h in range(HEADS)] + [("mem", 1, h) for h in range(HEADS)]
    return steps + DIL_STEPS + GQA_STEPS


STEP = {s: n for n, s in enumerate(attention_steps())}


def slots_b():
    halves = [(unit, m) for unit in SLOTS_B for m in range(2)]
    steps = DIL_STEPS + GQA_STEPS
    out = []
    for n in range(len(steps) + 2):
        count = 2 if n in (18, 21) else 1
        out.append(([halves.pop(0) for _ in range(count)],
                    n // 2 - 1 if n in (2, 4, 6, 8, 10) else None,
                    n // 2 - 2 if n in (5, 7, 9, 11, 13) else None,
                    steps[n] if n < len(steps) else None,
                    steps[n - 1] if 1 <= n <= len(steps) else None,
                    steps[n - 2] if n >= 2 else None))
    assert not halves
    return out


def make_plan():
    p = Plan()
    p.out("msum")
    for l in range(2):
        for j in range(8):
            if j == KV_NORM:
                p.out("nsum", 2 * l)
            p.unit("w_kv", l * 8 + j, "kv", l, j)
            p.split(("kv", l, j))
        for j in range(4):
            p.unit("w_in", l * 32 + j, "ax", l, j)
            p.split(("ax", l, j))
        for j in range(4):
            p.unit("w_in", l * 32 + 8 + j, "mu", l, j)
            p.split(("mu", l, j))
        p.out("if", l)
        for j in range(4):
            p.unit("w_in", l * 32 + 16 + j, "qa", l, j)
        for n, (kind, j) in enumerate(MEM_SLOTS):
            p.unit("w_in", l * 32 + {"o": 12, "ay": 4}[kind] + j, kind, l, j)
            if 2 <= n < 2 + HEADS:
                p.out("pv", STEP["mem", l, n - 2])
        for w in ("rga", "rgx", "mlq", "mlk", "mlv"):
            p.unit(w, l, w, l, outs=4)
        p.out("acol", l)
        for j in range(12):
            p.unit("w_in", l * 32 + 20 + j, "gt", l, j)
        for j in range(4):
            p.unit("w_br_rg", l * 4 + j, "br", l, j)
            p.split(("br", l, j))
        for j in range(2):
            p.out("mlsum", l, j)
        for j in range(4):
            p.unit("w_br_xa", l * 4 + j, "br", l, 8 + j)
            p.split(("br", l, 8 + j))
        for j in range(4):
            p.unit("w_br_ml", l * 4 + j, "br", l, 4 + j)
        for j in range(4):
            p.unit("w_out", l * 4 + j, "wout", l, j)
        p.out("nsum", 2 * l + 1)
        if l == 0:
            p.ffn(0, {w: f"ffn_{w}" for w in ("w1", "w3", "w2")}, FF1)
    p.out("logit")
    for j in range(4):
        p.out("htok", j)
    p.out("rank")
    for j in range(4):
        p.out("gtr", j)
    p.moe_u, p.moe_o, p.moe_acc = len(p.units), p.n_o, p.n_acc
    for _ in range(EXPERTS):
        p.units += [None] * (3 * FF1)
        p.released += [None] * (3 * FF1)
    for j in range(FF1):
        p.released[len(p.units) - FF1 + j] = ("acc", p.moe_acc + (EXPERTS - 1) * FF1 + j + 1)
    p.n_o += EXPERTS * MOE_OUTS
    p.n_acc += EXPERTS * FF1
    for j in range(4):
        p.out("comb", j)
    p.out("nsum", N_FINAL1)
    p.out("nsum", N_FFN1B)
    for g in range(GROUPS):
        p.out("brow", g)

    def ffn_b(f):
        p.ffn(f, {w: f"ffn{f}_{w}_2" for w in ("w1", "w3", "w2")}, FF2)

    ffn_b(1)
    for h in range(GROUPS * HA):
        if h == BIAS_NORM:
            p.out("nsum", N_MIXB)
        p.out("bias", h)
    for kind, n, at in (("qd", 6, 0), ("kd", 6, 6), ("vd", 6, 12)):
        for j in range(n):
            p.unit("w_in_2", at + j, kind, j)
            p.split((kind, j))
    col = {"qb": 18, "kb": 22, "vb": 23, "gate": 24}
    for halves, normed, turned, score, trans, value in slots_b():
        for unit, m in halves:
            if m == 1:
                p.unit("w_in_2", col[unit[0]] + unit[1], *unit)
        if normed is not None:
            p.out("qksum", normed)
        if turned is not None:
            p.out("rot", turned)
        if value:
            p.out("pv", STEP[value])
    for j in range(2):
        p.acc("w_branch_a", j, "bra", j)
    for j in range(4):
        p.unit("w_branch_b", j, "brb", j)
    for j in range(4):
        p.unit("w_out_2", j, "wout", 2, j)
    p.out("nsum", N_FFN2B)
    ffn_b(2)
    p.out("nsum", N_FINALB)
    return p


MOE_OUTS = 2 * FF1 + 4


class Experts:

    def __init__(self, sem, tag, loaded, bank_full, bank_free, acc_units, u, o, acc):
        self.loaded, self.bank_full, self.bank_free, self.acc_units = loaded, bank_full, bank_free, acc_units
        self.u, self.o, self.acc = u, o, acc
        self.gathered = sem(f"gathered{tag}")
        self.xg_ready = sem(f"xg_ready{tag}")
        self.y_ready = sem(f"y_ready{tag}")

    def comb(self, j):
        return self.o + 2 + j

    def w(self, which, j):
        return self.o + (which if j == 0 else 4 + 2 * j + which)


def build(nc, a, out):
    with ExitStack() as ctx:
        def sb(name, shape, dt=F32):
            return ctx.enter_context(nc.sbuf_tensor(name, shape, dt))

        def sem(name):
            return ctx.enter_context(nc.semaphore(name))

        plan = make_plan()

        ring = sb("ring", [P, NS, 2048])
        second_names = {}

        def name_parts(first, end):
            with nc.sbuf_tensor(f"before_parts_{first}_{end}", [P, first], F32):
                with nc.sbuf_tensor(f"parts_{first}_{end}", [P, end - first], F32R) as t:
                    second_names[first, end] = t

        for stretch in PARTS:
            name_parts(*stretch)
        arena = sb("arena", [P, 18 * 2048 + 48])
        at = [0]

        def page(n):
            at[0] += n
            return arena[:, at[0] - n:at[0]]

        def tiles(v, k=KD):
            return v.rearrange("p (k t) -> p k t", k=k)

        pages = [page(2048) for _ in range(6)]
        ax_pad = tiles(page(KD * (T + PAD)))
        mu_pad = tiles(page(KD * (T + PAD)))
        pages += [None, None] + [page(2048) for _ in range(10)]
        xT, hT, memT, memn = [tiles(pages[n]) for n in range(4)]
        yxa = memn
        kmem, vmem = tiles(pages[4]), pages[5].rearrange("p (m c) -> p m c", m=TT)
        qml, kml = tiles(pages[4]), tiles(pages[5])
        qxa, vml = tiles(pages[8]), pages[8].rearrange("p (m c) -> p m c", m=TT)
        ogate, ygelu, xc, cml = [tiles(pages[n]) for n in (9, 10, 11, 12)]
        hn = cml
        ml_root = arena[:, 6 * 2048:6 * 2048 + HEADS * T]
        ra, ib, g0, g1, g2 = [tiles(pages[n]) for n in (13, 14, 15, 16, 17)]
        gates = (g0, g1, g2)
        tanh_v = arena[:, 6 * 2048:7 * 2048]
        tanh_t = tiles(tanh_v)
        sq = ib
        sq_mem = g0
        merged = ra
        hid = arena[:, at[0] - 8192:at[0] - 8192 + 2 * FF1 * T].rearrange("p (f t) -> p f t", f=2 * FF1)
        silu_tmp = pages[13].rearrange("p (b c) -> p b c", b=4)
        hid_e = arena[:, at[0] - 8192:at[0] - 8192 + 2 * FF1 * CAP].rearrange("p (f t) -> p f t", f=2 * FF1)
        xg = pages[12][:, 0:KD * CAP].rearrange("p (k t) -> p k t", k=KD)
        y_tok = pages[12][:, 1024:2048]
        htok = pages[5].rearrange("p (m c) -> p m c", m=TT)
        Pg = pages[4].rearrange("p (m e s) -> p m e s", m=TT, e=EXPERTS)
        blk = arena[:, 6 * 2048:6 * 2048 + 4144 + 2048]
        Pall = blk[:, 0:TT * (EXPERTS + 1) * CAP].rearrange("p (m s) -> p m s", m=TT)
        GT = blk[:, 2304:2304 + (EXPERTS + 1) * T]
        b0 = 2 * 2048

        def area(n):
            nonlocal b0
            b0 += n
            return arena[:, b0 - n:b0]

        qd, kd = tiles(area(12 * T), 12), tiles(area(12 * T), 12)
        vd = area(TT * 12 * P).rearrange("p (m c) -> p m c", m=TT)
        bias = area(24 * 384).rearrange("p (h m) -> p h m", h=24)
        b_qk = b0
        qk = area(10 * T)
        scr = area(10 * T)
        vb = area(TT * 256).rearrange("p (m c) -> p m c", m=TT)
        gate2 = area(16 * T)
        o_a, o_b = tiles(area(4 * T), 4), tiles(area(8 * T))
        onehot = vd.rearrange("p m c -> p (m c)")[0:33, 0:GROUPS * 512].rearrange("p (g m) -> p g m", g=GROUPS)
        brow = scr[0:HA, 0:GROUPS * 512].rearrange("p (g m) -> p g m", g=GROUPS)
        brevs = [v.rearrange("p (h m) -> p h m", h=HA)
                 for v in (kd.rearrange("p k t -> p (k t)"), vd.rearrange("p m c -> p (m c)"),
                           arena[:, b_qk:b_qk + HA * 384])]
        sq_b = qd[:, 0:KD, :]
        assert b0 <= 18 * 2048 + 48, b0
        hid2 = arena[:, at[0] - 8192:at[0] - 8192 + 2 * FF2 * T].rearrange("p (f t) -> p f t", f=2 * FF2)

        def part_at(first, end):
            return second_names[first, end][:, :]

        def split_memory(ff, h_at, h, w_at):
            return {"ff": ff, "x_hi": tiles(part_at(h_at, h_at + 2048)), "x_lo": tiles(part_at(2048, 4096)),
                    "hid": h,
                    "hid_hi": part_at(w_at[0], w_at[0] + 2 * ff * T).rearrange("p (f t) -> p f t", f=2 * ff),
                    "hid_lo": part_at(at[0] - 8192, at[0] - 8192 + 2 * ff * T)
                    .rearrange("p (f t) -> p f t", f=2 * ff),
                    "w_hi": [part_at(n, n + 1024) for n in w_at[1:1 + NW]],
                    "w_lo": [part_at(n, n + 1024) for n in w_at[1 + NW:]]}

        mix_w = {"w_hi": [part_at(n, n + 1024) for n in (23552, 24576, 25600)],
                 "w_lo": [part_at(n, n + 1024) for n in (26672, 27696, 35888)]}
        mem_parts = {"x_hi": tiles(part_at(21504, 23552)), "x_lo": tiles(part_at(6144, 8192))}
        mix_parts = {"x_hi": tiles(part_at(18480, 20528)), "x_lo": tiles(part_at(32816, 34864))}
        br_w = {"w_hi": [part_at(n, n + 1024) for n in (8192, 9216, 10240)],
                "w_lo": [part_at(n, n + 1024) for n in (11264, 13312, 14336)]}
        rg_parts = {"x_hi": tiles(part_at(22576, 24624)), "x_lo": tiles(part_at(20528, 22576))}
        xa_parts = {"x_hi": tiles(part_at(18480, 20528)), "x_lo": tiles(part_at(6144, 8192))}
        dil = {"x_hi": tiles(part_at(28672, 30720)), "x_lo": tiles(part_at(30720, 32768)),
               "w_hi": [part_at(n, n + 1024) for n in (25600, 26624, 27648)],
               "w_lo": [part_at(n, n + 1024) for n in (32768, 33792, 34816)]}
        mix_1 = (14336, 8192, 9216, 10240, 11264, 12288, 13312)
        mix_2 = (13312, 6144, 34352, 35376, 18944, 19968, 20992)
        FFN = [split_memory(FF1, 21504, hid, mix_1), split_memory(FF2, 4096, hid2, mix_2),
               split_memory(FF2, 4096, hid2, mix_2)]

        ones_row = sb("ones_row", [P, T])
        vecs = sb("vecs", [P, NV])
        mats = sb("mats", [P, 6 * P])
        ident, ones, flip, rotm, tri, iota = [mats[:, n * P:(n + 1) * P] for n in range(6)]
        sel = sb("sel", [4, HEADS * P])
        wif = sb("wif", [P, 2, KD, 8])
        wr = sb("wr", [P, KD, 8])
        rope = sb("rope", [P, 2, T])
        btab = sb("btab", [33, 24])
        softp = sb("softp", [P, 4, 16])
        eps_t = sb("eps_t", [P, 1])
        warm = sb("warm", [P, 1])
        root = sb("root", [P, T])
        mem_rstd = sb("mem_rstd", [P, T])
        probs = sb("probs", [P, 2, 768])
        probsT = sb("probsT", [P, 2, 768])
        work = sb("work", [P, 768])
        smax = sb("smax", [P, 2, 2, 2])
        ssum = sb("ssum", [P, 2, 2, 2])
        mrow = probs[0:4, :, 512:768]
        arow = probsT[0:4, 0, 512:768]
        acol = sb("acol", [P, TT, HEADS])
        lg = sb("lg", [P, 14, TT, EXPERTS])
        gv = sb("gv", [P, TT, 8])
        flag = sb("flag", [P, 1], I32)
        cnt = sb("cnt", [P, 2])
        rows = [pages[15][0:4, n * T:(n + 1) * T] for n in range(8)]

        O = [ctx.enter_context(nc.psum_tensor(f"O{n}", [P, 512], F32)) for n in range(NB)]
        S = ctx.enter_context(nc.psum_tensor("S", [P, 4, 512], F32))
        S2 = S[:, :, :].rearrange("p b c -> p (b c)")
        brow_dram = nc.dram_tensor("bias_rows", [GROUPS * HA, 512], F32, kind="Internal").ap()

        loaded = [sem(f"slot{n}_loaded") for n in range(NS)]
        first_loaded = sem("first_loaded")
        small_loaded = sem("small_loaded")
        bank_full = sem("bank_full")
        bank_free = [sem(f"bank{n}_free") for n in range(NB)]
        acc_units = sem("acc_units")
        acc_quarter = sem("acc_quarter")
        w_hi = sem("w_hi")
        w_lo = sem("w_lo")
        w_used = sem("w_used")
        h_hi = sem("h_hi")
        h_lo = sem("h_lo")
        hid_split = sem("hid_split")
        squares = sem("squares")
        sq_sum = sem("sq_sum")
        memsq = sem("memsq")
        h_ready = sem("h_ready")
        memn_ready = sem("memn_ready")
        x_added = sem("x_added")
        dve_step = sem("dve_step")
        act_step = sem("act_step")
        init_done = sem("init_done")
        conv_rg = sem("conv_rg")
        conv_ml = sem("conv_ml")
        silu_ml = sem("silu_ml")
        exp_f = sem("exp_f")
        abs_f = sem("abs_f")
        a_ready = sem("a_ready")
        decay = sem("decay")
        rg_s = sem("rg_s")
        rg_root = sem("rg_root")
        rg_done = sem("rg_done")
        lam_abs = sem("lam_abs")
        lam_exp = sem("lam_exp")
        lam_done = sem("lam_done")
        scores = sem("scores")
        scores_free = sem("scores_free")
        maxed = sem("maxed")
        exped = sem("exped")
        probs_ready = sem("probs_ready")
        transposed = sem("transposed")
        probsT_ready = sem("probsT_ready")
        ml_scores = sem("ml_scores")
        ml_arg = sem("ml_arg")
        ml_exp = sem("ml_exp")
        ml_em = sem("ml_em")
        ml_mask = sem("ml_mask")
        ml_w = sem("ml_w")
        ml_num = sem("ml_num")
        ml_abs = sem("ml_abs")
        ml_head = sem("ml_head")
        ml_sq = sem("ml_sq")
        ml_done = sem("ml_done")
        merged_ready = sem("merged_ready")
        routed = sem("routed")
        gate_exp = sem("gate_exp")
        gate_arg = sem("gate_arg")
        sel_ready = sem("sel_ready")
        picks = sem("picks")
        ranks_moved = sem("ranks_moved")
        moe_done = sem("moe_done")
        table_loaded = sem("table_loaded")
        rows_stored = sem("rows_stored")
        rows_loaded = [sem(f"rows_loaded{g}") for g in range(GROUPS)]
        qk_sq = sem("qk_sq")
        qk_norm = sem("qk_norm")
        qk_ready = sem("qk_ready")
        bra_free = sem("bra_free")
        stored = sem("stored")

        main = Experts(sem, "", loaded, bank_full, bank_free, acc_units, plan.moe_u, plan.moe_o, plan.moe_acc)
        again = Experts(sem, "_again", [sem(f"slot{n}_loaded_again") for n in range(NS)], sem("bank_full_again"),
                        [sem(f"bank{n}_free_again") for n in range(NB)], sem("acc_units_again"), 0, 4, 0)

        def vec(name, l=None, n=8):
            c = VEC[name] if l is None else VEC[name, l]
            return vecs[:, c:c + n]

        def filled(eng, *name):
            o = plan.o[name]
            eng.wait_ge(bank_full, o + 1)
            return O[o % NB]

        def freed(*name):
            return bank_free[plan.o[name] % NB]

        def evacuated(eng, *name):
            o = plan.o[name]
            eng.wait_ge(bank_free[o % NB], o // NB + 1)

        def by_rows(name):
            return name[0] in ("w2", "vd") or name[0] == "kv" and name[2] >= 4

        def half_of_unit(h):
            u, name, m = plan.halves[h]
            w = ring[:, u % NS, :]
            if by_rows(name):
                return w[:, m * 1024:(m + 1) * 1024]
            return w.rearrange("p (k c) -> p k c", k=KD)[:, :, m * P:(m + 1) * P]

        def part(h, which):
            _, name, _ = plan.halves[h]
            at = FFN[name[1]] if name[0] in ("w1", "w3", "w2") else {"kv": mix_w, "ax": mix_w, "mu": mix_w}.get(name[0], dil)
            if name[0] == "br":
                at = br_w
            w = at[which][h % NW]
            return w if by_rows(name) else w.rearrange("p (k c) -> p k c", k=KD)

        def half_range(f):
            first = plan.half_of["w1", f, 0]
            return first, plan.half_of["w2", f, FFN[f]["ff"] - 1] + 2

        def mix_halves(l):
            return plan.half_of["kv", l, 0], plan.half_of["mu", l, 3] + 2

        def branch_halves(l):
            return plan.half_of["br", l, 0], plan.half_of["br", l, 11] + 2

        HID_BEFORE = [0, FF1, FF1 + FF2]

        MIXER_BEFORE = {N_FFN0: 0, N_MOE: 1, N_FFN2B: 2}
        FFN_BEFORE = {N_MIX1: 0, N_MIXB: 1, N_FINALB: 2}

        def x_ready(eng, n, quarter):
            if n == N_MIX0:
                eng.wait_ge(small_loaded, SMALL * 16)
            elif n == N_FINAL1:
                eng.wait_ge(moe_done, 1)
            elif n == N_FFN1B:
                eng.wait_ge(h_ready, 8 * N_FINAL1 + 2 * quarter + 2)
            elif n in MIXER_BEFORE:
                evacuated(eng, "wout", MIXER_BEFORE[n], quarter)
            else:
                eng.wait_ge(x_added, 4 * FFN_BEFORE[n] + quarter + 1)

        FFN_OF = {N_FFN0: 0, N_FFN2B: 2}
        NORM_G = {N_MIX0: ("norm_mix_g", 0), N_FFN0: ("norm_ffn_g", 0), N_MIX1: ("norm_mix_g", 1),
                  N_MOE: ("norm_ffn_g", 1), N_FINAL1: ("final_norm_g",), N_FFN1B: ("ffn1_norm_2",),
                  N_MIXB: ("mix_norm_2",), N_FFN2B: ("ffn2_norm_2",), N_FINALB: ("final_norm_2",)}

        FIRST_LOADS = [(memT, a["memT"]), (mats[:, :], a["mats"]), (vecs[:, :], a["vecs"])]
        SMALL_LOADS = [(xT, a["xT"]), (sel[:, :], a["sel"]), (wif[:, :, :, :], a["wif"]), (wr[:, :, :], a["wr"]),
                       (rope[:, :, :], a["rope"]), (btab[:, :], a["btab"])]
        SMALL = len(SMALL_LOADS)

        block = ctx.enter_context(nc.Block())

        @block.sync
        def _(sp):
            RELEASES = {"bank": bank_full, "acc": acc_units, "split": w_lo}

            def bring(first, last):
                for u in range(first, last):
                    array, index = plan.units[u]
                    if u >= NS:
                        how, count = plan.released[u - NS]
                        sp.wait_ge(RELEASES[how], count)
                    sp.dma_start(ring[:, u % NS, :], a[array][index]).then_inc(loaded[u % NS], 16)

            def expert_unit(x, e, i):
                slot = (x.u + i) % NS
                array, index = (("moe_w1", "moe_w3")[i % 2], i // 2) if i < 2 * FF1 else ("moe_w2", i - 2 * FF1)
                sp.dma_start(ring[:, slot, :], a[array][e, index]).then_inc(x.loaded[slot], 16)

            def used(x, e, i):
                if i < 2 * FF1:
                    sp.wait_ge(x.bank_full, e * MOE_OUTS + x.w(i % 2, i // 2) + 1)
                else:
                    sp.wait_ge(x.acc_units, e * FF1 + x.acc + i - 2 * FF1 + 1)

            def experts(x):
                with sp.Fori(0, EXPERTS - 1) as e:
                    for i in range(NS, 3 * FF1):
                        if i == 2 * FF1 - 1:
                            used(x, e, i + 1 - NS)
                        elif i != 2 * FF1:
                            used(x, e, i - NS)
                        expert_unit(x, e, i)
                    for i in range(NS):
                        used(x, e, 3 * FF1 - NS + i)
                        expert_unit(x, e + 1, i)
                for i in range(NS, 3 * FF1):
                    used(x, EXPERTS - 1, i - NS)
                    expert_unit(x, EXPERTS - 1, i)

            for to, of in FIRST_LOADS:
                sp.dma_start(to, of).then_inc(first_loaded, 16)
            bring(0, plan.moe_u)
            for i in range(NS):
                how, count = plan.released[plan.moe_u - NS + i]
                sp.wait_ge(RELEASES[how], count)
                expert_unit(main, 0, i)
            experts(main)
            sp.wait_ge(routed, 1)
            with sp.If(sp.value_load(flag[0:1, 0:1], min_val=0, max_val=1) != 0):
                sp.wait_ge(acc_units, plan.moe_acc + EXPERTS * FF1)
                for i in range(NS):
                    expert_unit(again, 0, i)
                experts(again)
                sp.wait_ge(again.acc_units, EXPERTS * FF1)
            bring(plan.moe_u + EXPERTS * 3 * FF1, len(plan.units))

        @block.tensor
        def _(pe):
            seen = [0]

            def take(*name):
                u = plan.u[name]
                pe.wait_ge(loaded[u % NS], 16 * (u // NS + 1))
                return ring[:, u % NS, :]

            def bank(*name):
                o = plan.o[name]
                assert o == seen[0], (name, o, seen[0])
                seen[0] += 1
                if o >= NB:
                    pe.wait_ge(bank_free[o % NB], o // NB)
                return O[o % NB]

            def columns(w, rhs, name, kt=KD, tile_ready=None):
                b = bank(*name)
                w = w.rearrange("p (k c) -> p k c", k=kt)
                for m in range(2):
                    for k in range(kt):
                        if m == 0 and tile_ready:
                            tile_ready(k)
                        mm = pe.matmul(b[:, m * T:(m + 1) * T], w[:, k, m * P:(m + 1) * P], rhs(k),
                                       start=(k == 0), stop=(k == kt - 1))
                mm.then_inc(bank_full, 1)

            def normed(n):
                return lambda k: pe.wait_ge(h_ready, 8 * n + k + 1)

            def merged_tiles(n):
                return lambda k: pe.wait_ge(merged_ready, 4 * n + k // 2 + 1)

            def half(unit, m):
                w = take(*unit).rearrange("p (k c) -> p k c", k=KD)
                if m == 1:
                    b = bank(*unit)
                else:
                    o = plan.o[unit]
                    pe.wait_ge(bank_free[o % NB], o // NB)
                    b = O[o % NB]
                for k in range(KD):
                    if unit[0] == "vb":
                        lhs, rhs = hT[:, k, m * P:(m + 1) * P], w[:, k, :]
                    else:
                        lhs, rhs = w[:, k, m * P:(m + 1) * P], hT[:, k, :]
                    mm = pe.matmul(b[:, m * 256:(m + 1) * 256], lhs, rhs, start=(k == 0), stop=(k == KD - 1))
                if m == 1:
                    mm.then_inc(bank_full, 1)

            def norm_sum(n):
                b = bank("nsum", n)
                s = sq if n <= N_FINAL1 else sq_b
                if n in SUMMED:
                    pe.wait_ge(sq_sum, SUMMED.index(n) + 1)
                for k in (0, 1, 6, 7) if n in SUMMED else range(KD):
                    if k == 6 or k % 2 == 0 and n not in SUMMED:
                        pe.wait_ge(squares, 4 * n + k // 2 + 1)
                    mm = pe.matmul(b[:, 0:T], ones, s[:, k, :], start=(k == 0), stop=(k == 7))
                mm.then_inc(bank_full, 1)

            def three(out, w_part, x_hi, x_lo, start, stop):
                hi, lo = w_part
                pe.matmul(out, hi, x_hi, start=start, stop=False, skip_group_check=True)
                pe.matmul(out, hi, x_lo, start=False, stop=False, skip_group_check=True)
                return pe.matmul(out, lo, x_hi, start=False, stop=stop, skip_group_check=True)

            def from_parts(name, x, wait_for=None):
                b = bank(*name)
                for n in range(2):
                    h = plan.half_of[name] + n
                    pe.wait_ge(w_lo, h + 1)
                    hi, lo = part(h, "w_hi"), part(h, "w_lo")
                    if by_rows(name):
                        hi, lo = [w.rearrange("p (k c) -> p k c", k=KD // 2) for w in (hi, lo)]
                        for k in range(KD // 2):
                            for m in range(TT):
                                t = slice(m * P, (m + 1) * P)
                                mm = three(b[:, m * UC:(m + 1) * UC],
                                           (x["x_hi"][:, 4 * n + k, t], x["x_lo"][:, 4 * n + k, t]),
                                           hi[:, k, :], lo[:, k, :], n == 0 and k == 0 and m == 0,
                                           n == 1 and k == KD // 2 - 1)
                    else:
                        for k in range(KD):
                            if n == 0 and wait_for is not None:
                                pe.wait_ge(h_lo, 8 * wait_for + k + 1)
                            mm = three(b[:, n * T:(n + 1) * T], (hi[:, k, :], lo[:, k, :]), x["x_hi"][:, k, :],
                                       x["x_lo"][:, k, :], k == 0, k == KD - 1)
                    mm.then_inc(bank_full if n else w_used, 1)

            def hidden(f):
                x = FFN[f]
                for j in range(x["ff"]):
                    for which in ("w1", "w3"):
                        b = bank(which, f, j)
                        for m in range(2):
                            h = plan.half_of[which, f, j] + m
                            pe.wait_ge(w_lo, h + 1)
                            hi, lo = part(h, "w_hi"), part(h, "w_lo")
                            for k in range(KD):
                                if (which, j, m) == ("w1", 0, 0):
                                    pe.wait_ge(h_lo, 8 * X_FFN[f] + k + 1)
                                mm = three(b[:, m * T:(m + 1) * T], (hi[:, k, :], lo[:, k, :]), x["x_hi"][:, k, :],
                                           x["x_lo"][:, k, :], k == 0, k == KD - 1)
                            mm.then_inc(bank_full if m else w_used, 1)

            def second(f):
                x = FFN[f]
                for j in range(x["ff"]):
                    pe.wait_ge(hid_split, HID_BEFORE[f] + j + 1)
                    h = plan.half_of["w2", f, j]
                    last = j == x["ff"] - 1
                    order = [(k, m) for k in range(2) for m in range(KD)]
                    if last:
                        order.sort(key=lambda km: (km[1] // 2, km[0]))
                    pe.wait_ge(w_lo, h + 1)
                    for n, (k, m) in enumerate(order):
                        if n == (2 if last else 8):
                            pe.wait_ge(w_lo, h + 2)
                        c = slice(m * P, (m + 1) * P)
                        mm = three(S[:, m // 2, (m % 2) * T:(m % 2 + 1) * T],
                                   (part(h + k, "w_hi")[:, c], part(h + k, "w_lo")[:, c]),
                                   x["hid_hi"][:, 2 * j + k, :], x["hid_lo"][:, 2 * j + k, :],
                                   j == 0 and k == 0 and m % 2 == 0, last and k == 1)
                        if last and n in (3, 7, 11):
                            mm.then_inc(acc_quarter, 1)
                        if n == (13 if last else 7):
                            mm.then_inc(w_used, 1)
                    mm.then_inc(acc_units, 1)

            def score(step):
                n = STEP[step]
                if n == 0:
                    pass
                else:
                    pe.wait_ge(scores_free, n)
                if step[0] == "mem":
                    h = step[2]
                    if h == 0:
                        evacuated(pe, "kv", step[1], 3)
                    evacuated(pe, "qa", step[1], h)
                    for m in range(TT):
                        for k in range(2):
                            mm = pe.matmul(S[:, 0, m * T:(m + 1) * T], qxa[:, 2 * h + k, m * P:(m + 1) * P],
                                           kmem[:, 2 * h + k, :], start=(k == 0), stop=(k == 1))
                elif step[0] == "dil":
                    h, m = step[1:]
                    if (h, m) == (0, 0):
                        evacuated(pe, "kd", 5)
                        evacuated(pe, "qd", 5)
                    r = DA * (h % 2)
                    for g in range(GROUPS):
                        t = (g * HA + h) // 2
                        mm = pe.matmul(S2[:, g * T:(g + 1) * T], qd[r:r + DA, t, m * P:(m + 1) * P],
                                       kd[r:r + DA, t, :], start=True, stop=True)
                else:
                    h = step[1]
                    if h == 0:
                        pe.wait_ge(qk_ready, 5)
                    q4 = qk.rearrange("p (k t) -> p k t", k=10)
                    for m in range(TT):
                        mm = pe.matmul(S[:, 0, m * T:(m + 1) * T], q4[:, h, m * P:(m + 1) * P],
                                       q4[:, HB + h // 4, :], start=True, stop=True)
                mm.then_inc(scores, 1)

            def transpose(step):
                n = STEP[step]
                pe.wait_ge(probs_ready, n + 1)
                if n:
                    pe.wait_ge(probsT_ready, n)
                p = probs[:, n % 2, :]
                if step[0] == "dil":
                    for c in range(6):
                        mm = pe.transpose(S2[:, 1024 + c * P:1024 + (c + 1) * P], p[:, c * P:(c + 1) * P], ident)
                else:
                    for m in range(TT):
                        for c in range(2):
                            mm = pe.transpose(S2[:, 1024 + c * T + m * P:1024 + c * T + (m + 1) * P],
                                              p[:, m * T + c * P:m * T + (c + 1) * P], ident)
                mm.then_inc(transposed, 1)

            def value(step):
                n = STEP[step]
                b = bank("pv", n)
                pe.wait_ge(probsT_ready, n + 1)
                p = probsT[:, n % 2, :]
                if step[0] == "mem":
                    h = step[2]
                    evacuated(pe, "kv", step[1], 4 + h)
                    for m in range(2):
                        for c in range(2):
                            mm = pe.matmul(b[:, m * T:(m + 1) * T], vmem[:, c, h * 256 + m * P:h * 256 + (m + 1) * P],
                                           p[:, c * T:(c + 1) * T], start=(c == 0), stop=(c == 1))
                elif step[0] == "dil":
                    h, m = step[1:]
                    if (h, m) == (0, 0):
                        evacuated(pe, "vd", 5)
                    r = DA * (h % 2)
                    for c in range(6):
                        g, t = c // 2, c % 2
                        mm = pe.matmul(b[r:r + DA, 0:P], vd[:, t, g * 512 + h * DA:g * 512 + (h + 1) * DA],
                                       p[:, c * P:(c + 1) * P], start=(c == 0), stop=(c == 5))
                else:
                    h = step[1]
                    if h == 0:
                        evacuated(pe, "vb", 0)
                    for c in range(2):
                        mm = pe.matmul(b[:, 0:T], vb[:, c, (h // 4) * P:(h // 4 + 1) * P], p[:, c * T:(c + 1) * T],
                                       start=(c == 0), stop=(c == 1))
                mm.then_inc(bank_full, 1)

            def blocks(w, rhs, name):
                w = w.rearrange("p (k c) -> p k c", k=KD)
                for g in range(4):
                    b = bank(*name, g)
                    for m in range(2):
                        for k in range(2):
                            mm = pe.matmul(b[:, m * T:(m + 1) * T], w[:, 2 * g + k, m * P:(m + 1) * P],
                                           rhs(2 * g + k), start=(k == 0), stop=(k == 1))
                    mm.then_inc(bank_full, 1)

            def ml_score(l, h):
                n = HEADS * l + h
                if n:
                    pe.wait_ge(ml_w, n)
                    pe.wait_ge(ml_em, n)
                if h == 0:
                    pe.wait_ge(scores_free, STEP["mem", l, 3] + 1)
                    pe.wait_ge(a_ready, l + 1)
                    evacuated(pe, "mlq", l, 3)
                    evacuated(pe, "mlk", l, 3)
                for s in range(TT):
                    to = S[:, 0, 0:T] if s == 0 else S[:, 0, T:T + P]
                    for k in range(2):
                        pe.matmul(to, kml[:, 2 * h + k, s * P:(s + 1) * P], qml[:, 2 * h + k, s * P:T],
                                  start=(k == 0), stop=(k == 1))
                pe.matmul(S[:, 1, :], sel[:, h * P:(h + 1) * P], mrow, start=True, stop=True)\
                  .then_inc(ml_scores, 1)

            def ml_value(l, h):
                n = HEADS * l + h
                pe.wait_ge(ml_w, n + 1)
                if n:
                    pe.wait_ge(ml_head, n)
                if h == 0:
                    pe.wait_ge(probsT_ready, STEP["mem", l, 3] + 1)
                    evacuated(pe, "mlv", l, 3)
                w = probs[:, n % 2, :]
                pe.matmul(S[:, 3, 0:T], ones, w[:, 0:T], start=True, stop=False, skip_group_check=True)
                pe.matmul(S[:, 3, P:T], ones, w[:, T:T + P], start=False, stop=True, skip_group_check=True)
                for m in range(2):
                    c = h * 256 + m * P
                    pe.matmul(S[:, 2, m * T:(m + 1) * T], vml[:, 0, c:c + P], w[:, 0:T], start=True, stop=False,
                              skip_group_check=True)
                    mm = pe.matmul(S[:, 2, m * T + P:(m + 1) * T], vml[:, 1, c:c + P], w[:, T:T + P], start=False,
                                   stop=True, skip_group_check=True)
                mm.then_inc(ml_num, 1)

            def mixer(l):
                for j in range(8):
                    if j == KV_NORM:
                        norm_sum(2 * l)
                    from_parts(("kv", l, j), mem_parts, X_MEM[l] if j == 0 else None)
                for kind in ("ax", "mu"):
                    for j in range(4):
                        from_parts((kind, l, j), mix_parts, X_MIX[l] if (kind, j) == ("ax", 0) else None)
                b = bank("if", l)
                for m in range(2):
                    for k in range(KD):
                        mm = pe.matmul(b[0:4, m * T:(m + 1) * T], wif[:, l, k, 4 * m:4 * m + 4], hT[:, k, :],
                                       start=(k == 0), stop=(k == KD - 1))
                mm.then_inc(bank_full, 1)
                for j in range(4):
                    columns(take("qa", l, j), lambda k: hT[:, k, :], ("qa", l, j))
                for n, (kind, j) in enumerate(MEM_SLOTS):
                    columns(take(kind, l, j), lambda k: hT[:, k, :], (kind, l, j))
                    if n < HEADS:
                        score(("mem", l, n))
                    if 1 <= n < 1 + HEADS:
                        transpose(("mem", l, n - 1))
                    if 2 <= n < 2 + HEADS:
                        value(("mem", l, n - 2))
                for name in ("rga", "rgx"):
                    w = take(name, l)
                    pe.wait_ge(conv_rg, l + 1)
                    blocks(w, lambda k: xc[:, k, :], (name, l))
                for name in ("mlq", "mlk"):
                    w = take(name, l)
                    pe.wait_ge(silu_ml, l + 1)
                    blocks(w, lambda k: cml[:, k, :], (name, l))
                w = take("mlv", l).rearrange("p (k c) -> p k c", k=KD)
                evacuated(pe, "mu", l, 3)
                for g in range(4):
                    b = bank("mlv", l, g)
                    for m in range(TT):
                        for k in range(2):
                            mm = pe.matmul(b[:, m * UC:(m + 1) * UC],
                                           mu_pad[:, 2 * g + k, PAD + m * P:PAD + (m + 1) * P], w[:, 2 * g + k, :],
                                           start=(k == 0), stop=(k == 1))
                    mm.then_inc(bank_full, 1)
                b = bank("acol", l)
                pe.wait_ge(a_ready, l + 1)
                for m in range(TT):
                    mm = pe.matmul(b[:, 4 * m:4 * m + 4], arow[:, m * P:(m + 1) * P], ident[0:4, 0:4],
                                   start=True, stop=True)
                mm.then_inc(bank_full, 1)
                for j in range(12):
                    columns(take("gt", l, j), lambda k: hT[:, k, :], ("gt", l, j))
                    if ML_FIRST <= j < ML_FIRST + HEADS:
                        ml_score(l, j - ML_FIRST)
                    if ML_FIRST + 2 <= j < ML_FIRST + 2 + HEADS:
                        ml_value(l, j - ML_FIRST - 2)
                for j in range(4):
                    from_parts(("br", l, j), rg_parts, X_RG[l] if j == 0 else None)
                pe.wait_ge(ml_sq, l + 1)
                for j in range(2):
                    b = bank("mlsum", l, j)
                    for h in range(2):
                        for k in range(2):
                            mm = pe.matmul(b[:, h * T:(h + 1) * T], ones, sq[:, 4 * j + 2 * h + k, :],
                                           start=(k == 0), stop=(k == 1))
                    mm.then_inc(bank_full, 1)
                for j in range(8, 12):
                    from_parts(("br", l, j), xa_parts, X_XA[l] if j == 8 else None)
                for j in range(4, 8):
                    w = take("br", l, j)
                    if j == 4:
                        pe.wait_ge(ml_done, l + 1)
                    columns(w, lambda k: hn[:, k, :], ("br", l, j))
                for j in range(4):
                    columns(take("wout", l, j), lambda k: merged[:, k, :], ("wout", l, j),
                            tile_ready=merged_tiles(l) if j == 0 else None)
                norm_sum(2 * l + 1)

            b = bank("msum")
            pe.wait_ge(first_loaded, 16 * len(FIRST_LOADS))
            for k in range(KD):
                if k % 2 == 0:
                    pe.wait_ge(memsq, k // 2 + 1)
                mm = pe.matmul(b[:, 0:T], ones, sq_mem[:, k, :], start=(k == 0), stop=(k == KD - 1))
            mm.then_inc(bank_full, 1)
            mixer(0)
            hidden(0)
            second(0)
            mixer(1)

            b = bank("logit")
            for m in range(TT):
                for k in range(KD):
                    if m == 0:
                        normed(N_MOE)(k)
                    mm = pe.matmul(b[:, 8 * m:8 * m + 8], hT[:, k, m * P:(m + 1) * P], wr[:, k, :],
                                   start=(k == 0), stop=(k == KD - 1))
            mm.then_inc(bank_full, 1)
            for j in range(4):
                b = bank("htok", j)
                for c in range(4):
                    m, k = j // 2, 4 * (j % 2) + c
                    mm = pe.transpose(b[:, c * P:(c + 1) * P], hT[:, k, m * P:(m + 1) * P], ident)
                mm.then_inc(bank_full, 1)
            b = bank("rank")
            pe.wait_ge(sel_ready, 1)
            picked = lg[:, 6, :, :]
            pe.matmul(b[:, 0:8], tri, picked[:, 0, :], start=True, stop=True)
            pe.matmul(b[:, 8:16], tri, picked[:, 1, :], start=True, stop=False)
            pe.matmul(b[:, 8:16], ones, picked[:, 0, :], start=False, stop=True)
            pe.matmul(b[:, 16:24], ones, picked[:, 0, :], start=True, stop=False)
            pe.matmul(b[:, 16:24], ones, picked[:, 1, :], start=False, stop=True).then_inc(bank_full, 1)

            def gate_rows(x, o, n_pass):
                pe.wait_ge(picks, 3 * n_pass - 1)
                for j in range(4):
                    if o + j >= NB:
                        pe.wait_ge(x.bank_free[(o + j) % NB], (o + j) // NB)
                    b = O[(o + j) % NB]
                    for c in range(4):
                        e, m = 2 * j + c // 2, c % 2
                        mm = pe.transpose(b[:, c * P:(c + 1) * P], Pg[:, m, e, :], ident)
                    mm.then_inc(x.bank_full, 1)

            def gather(x, e):
                for k in range(KD):
                    for m in range(TT):
                        mm = pe.matmul(S2[:, 1024 + k * CAP:1024 + (k + 1) * CAP], htok[:, m, k * P:(k + 1) * P],
                                       Pall[:, m, bass.ts(e, CAP)], start=(m == 0), stop=(m == 1))
                mm.then_inc(x.gathered, 1)

            def combine(x, o, e):
                for j in range(4):
                    pe.wait_ge(x.bank_free[(o + j) % NB], (o + j) // NB + e * (MOE_OUTS // NB))
                    b = O[(o + j) % NB]
                    for m in range(2):
                        c = (2 * j + m) * P
                        mm = pe.matmul(b[:, m * T:(m + 1) * T], y_tok[:, c:c + P], GT[:, bass.ts(e, T)],
                                       start=True, stop=True)
                    mm.then_inc(x.bank_full, 1)

            def first_gather(x, n_pass):
                pe.wait_ge(picks, 3 * n_pass - 2)
                gather(x, 0)

            def experts(x, n_pass):
                with pe.Fori(0, EXPERTS) as e:
                    pe.wait_ge(x.xg_ready, e * 2 + 2)
                    for i in range(2 * FF1):
                        o = x.w(i % 2, i // 2)
                        slot = (x.u + i) % NS
                        pe.wait_ge(x.loaded[slot], e * (16 * 3 * FF1 // NS) + 16 * ((x.u + i) // NS + 1))
                        pe.wait_ge(x.bank_free[o % NB], e * (MOE_OUTS // NB) + o // NB)
                        b = O[o % NB]
                        w = ring[:, slot, :].rearrange("p (k c) -> p k c", k=KD)
                        for m in range(2):
                            for k in range(KD):
                                mm = pe.matmul(b[:, m * CAP:(m + 1) * CAP], w[:, k, m * P:(m + 1) * P], xg[:, k, :],
                                               start=(k == 0), stop=(k == KD - 1))
                        mm.then_inc(x.bank_full, 1)
                        if i == 1:
                            pe.wait_ge(x.y_ready, e * 2 + 2)
                            combine(x, x.comb(0), e)
                    pe.wait_ge(picks, 3 * n_pass)
                    gather(x, e + 1)
                    for j in range(FF1):
                        slot = (x.u + 2 * FF1 + j) % NS
                        pe.wait_ge(x.loaded[slot], e * (16 * 3 * FF1 // NS) + 16 * ((x.u + 2 * FF1 + j) // NS + 1))
                        o = x.w(1, j)
                        pe.wait_ge(x.bank_free[o % NB], e * (MOE_OUTS // NB) + o // NB + 1)
                        w = ring[:, slot, :].rearrange("p (k c) -> p k c", k=2)
                        for k in range(2):
                            for c in range(2):
                                mm = pe.matmul(S[:, c, :], hid_e[:, 2 * j + k, :], w[:, k, c * 512:(c + 1) * 512],
                                               start=(j == 0 and k == 0), stop=(j == FF1 - 1 and k == 1))
                        mm.then_inc(x.acc_units, 1)
                pe.wait_ge(x.y_ready, 2 * EXPERTS + 2)
                last_combine(x)

            def last_combine(x):
                o = x.o + EXPERTS * MOE_OUTS
                for j in range(4):
                    pe.wait_ge(x.bank_free[(o + j) % NB], (o + j) // NB)
                    b = O[(o + j) % NB]
                    for m in range(2):
                        c = (2 * j + m) * P
                        mm = pe.matmul(b[:, m * T:(m + 1) * T], y_tok[:, c:c + P], GT[:, EXPERTS * T:(EXPERTS + 1) * T],
                                       start=True, stop=True)
                    mm.then_inc(x.bank_full, 1)

            def combined(x):
                o = x.o + EXPERTS * MOE_OUTS
                for q in range(4):
                    pe.wait_ge(x.bank_free[(o + q) % NB], (o + q) // NB + 1)

            for j in range(4):
                evacuated(pe, "htok", j)
            first_gather(main, 1)
            gate_rows(main, plan.o["gtr", 0], 1)
            seen[0] = plan.moe_o
            experts(main, 1)
            seen[0] = plan.o["comb", 3] + 1
            pe.wait_ge(routed, 1)
            with pe.If(pe.value_load(flag[0:1, 0:1], min_val=0, max_val=1) != 0):
                combined(main)
                first_gather(again, 2)
                gate_rows(again, 0, 2)
                experts(again, 2)
                combined(again)
            norm_sum(N_FINAL1)
            norm_sum(N_FFN1B)

            pe.wait_ge(table_loaded, 16)
            for g in range(GROUPS):
                bank("brow", g)
                pe.matmul(O[plan.o["brow", g] % NB][0:HA, :], btab[:, g * HA:(g + 1) * HA], onehot[:, g, :],
                          start=True, stop=True).then_inc(bank_full, 1)
            hidden(1)
            second(1)
            for h in range(GROUPS * HA):
                if h == BIAS_NORM:
                    norm_sum(N_MIXB)
                b = bank("bias", h)
                if h % HA == 0:
                    pe.wait_ge(rows_loaded[h // HA], 16)
                pe.matmul(b[:, 0:384], flip, brevs[h // HA][:, h % HA, :], start=True, stop=True).then_inc(bank_full, 1)
            for kind in ("qd", "kd", "vd"):
                for j in range(6):
                    from_parts((kind, j), dil, X_DIL if (kind, j) == ("qd", 0) else None)
            for halves, summed, turned, s, t, v in slots_b():
                for unit, m in halves:
                    half(unit, m)
                if summed is not None:
                    b = bank("qksum", summed)
                    pe.wait_ge(qk_sq, summed + 1)
                    pe.matmul(b[:, :], ones, scr[:, summed * 512:(summed + 1) * 512], start=True, stop=True)\
                      .then_inc(bank_full, 1)
                if turned is not None:
                    b = bank("rot", turned)
                    pe.wait_ge(qk_norm, turned + 1)
                    pe.matmul(b[:, :], rotm, qk[:, turned * 512:(turned + 1) * 512], start=True, stop=True)\
                      .then_inc(bank_full, 1)
                if s:
                    score(s)
                if t:
                    transpose(t)
                if v:
                    value(v)
            pe.wait_ge(scores_free, len(STEP))
            pe.wait_ge(probsT_ready, len(STEP))
            for j in range(2):
                w = take("bra", j).rearrange("p (k c) -> p k c", k=2)
                if j == 0:
                    evacuated(pe, "pv", STEP["dil", HA - 1, 1])
                for k in range(2):
                    for m in range(KD):
                        mm = pe.matmul(S[:, m // 2, (m % 2) * T:(m % 2 + 1) * T], w[:, k, m * P:(m + 1) * P],
                                       o_a[:, 2 * j + k, :], start=(j == 0 and k == 0 and m % 2 == 0),
                                       stop=(j == 1 and k == 1), skip_group_check=True)
                mm.then_inc(acc_units, 1)
            for j in range(4):
                w = take("brb", j)
                if j == 0:
                    evacuated(pe, "pv", STEP["gqa", HB - 1])
                columns(w, lambda k: o_b[:, k, :], ("brb", j))
            for j in range(4):
                columns(take("wout", 2, j), lambda k: tiles(gate2[:, 0:2048])[:, k, :], ("wout", 2, j),
                        tile_ready=merged_tiles(2) if j == 0 else None)
            norm_sum(N_FFN2B)
            hidden(2)
            second(2)
            norm_sum(N_FINALB)
            assert seen[0] == plan.n_o

        @block.scalar
        def _(act):
            steps = [0]

            def step(ins):
                steps[0] += 1
                ins.then_inc(act_step, 1)
                act.wait_ge(act_step, steps[0])

            def copy(to, of, *name):
                b = filled(act, *name)
                act.activation(to, b[:, :] if of is None else of(b), ACT.Copy).then_inc(freed(*name), 1)

            def split_high(h):
                u = plan.halves[h][0]
                act.wait_ge(loaded[u % NS], 16 * (u // NS + 1))
                if h >= NW:
                    how, count = plan.consumed[h - NW]
                    act.wait_ge({"used": w_used, "bank": bank_full, "acc": acc_units}[how], count)
                act.activation(part(h, "w_hi"), half_of_unit(h), ACT.Copy).then_inc(w_hi, 1)

            def split_ahead(first):
                for h in range(first, first + NW):
                    split_high(h)

            def square(n):
                s = sq if n <= N_FINAL1 else sq_b
                act.activation(warm[:, :], eps_t[:, :], ACT.Sqrt)
                for q in range(4):
                    if q == 3 and n in FFN_OF:
                        split_ahead(half_range(FFN_OF[n])[0])
                    x_ready(act, n, q)
                    act.activation(s[:, 2 * q:2 * q + 2, :], xT[:, 2 * q:2 * q + 2, :], ACT.Square)\
                       .then_inc(squares, 1)

            def root_mean(n):
                b = filled(act, "nsum", n)
                if n:
                    act.wait_ge(h_ready, 8 * n)
                act.activation(root[:, :], b[:, 0:T], ACT.Sqrt, bias=eps_t[:, :], scale=1.0 / D)\
                   .then_inc(freed("nsum", n), 1)

            def high_parts(ready, count, of, x):
                for k in range(KD):
                    act.wait_ge(ready, count + k + 1)
                    act.activation(x["x_hi"][:, k, :], of[:, k, :], ACT.Copy).then_inc(h_hi, 1)

            def hidden(f, n):
                x = FFN[f]
                high_parts(h_ready, 8 * n, hT, x)
                first, end = half_range(f)
                for i in range(3 * x["ff"]):
                    for h in (first + 2 * i + NW, first + 2 * i + NW + 1):
                        if h < end:
                            split_high(h)
                    j = i // 2
                    if i < 2 * x["ff"] and i % 2 == 0:
                        if j >= 4:
                            evacuated(act, "w3", f, j - 4)
                        b = filled(act, "w1", f, j)
                        act.activation(silu_tmp[:, j % 4, :], b[:, :], ACT.Silu).then_inc(freed("w1", f, j), 1)

            def exps(s):
                n = STEP[s]
                par = n % 2
                act.wait_ge(maxed, n + 1)
                if n >= 2:
                    act.wait_ge(transposed, n - 1)
                if s[0] == "dil":
                    act.activation(probs[:, par, :], work[:, :], ACT.Exp, bias=smax[:, par, 1, 0:1],
                                   accum_out=ssum[:, par, 0, 0:1]).then_inc(exped, 1)
                    return
                scale = 256 ** -0.5 if s[0] == "mem" else P ** -0.5
                for m in range(TT):
                    last = act.activation(probs[:, par, m * T:(m + 1) * T], S[:, 0, m * T:(m + 1) * T], ACT.Exp,
                                          bias=smax[:, par, 1, m:m + 1], scale=scale,
                                          accum_out=ssum[:, par, 0, m:m + 1])
                last.then_inc(exped, 1)

            def take_over(s):
                n = STEP[s]
                act.wait_ge(transposed, n + 1)
                if n >= 2:
                    act.wait_ge(bank_full, plan.o["pv", n - 2] + 1)
                w = 768 if s[0] == "dil" else 512
                act.activation(probsT[:, n % 2, 0:w], S2[:, 1024:1024 + w], ACT.Copy).then_inc(probsT_ready, 1)

            def gated(l, kind, j, func, to):
                b = filled(act, kind, l, j)
                act.activation(to, b[:, :], func).then_inc(freed(kind, l, j), 1)

            def two_biased(to, name, func, bias_of):
                b = filled(act, *name)
                act.activation(to(0), b[:, 0:T], func, bias=bias_of(0))
                act.activation(to(1), b[:, T:2 * T], func, bias=bias_of(1)).then_inc(freed(*name), 1)

            def ml_exps(l, h):
                n = HEADS * l + h
                e = probs[:, n % 2, 0:3 * P]
                act.wait_ge(ml_arg, n + 1)
                act.activation(e, e, ACT.Exp, scale=-1.0).then_inc(ml_exp, 1)
                if n >= 2:
                    act.wait_ge(ml_head, n - 1)
                act.activation(work[:, (n % 2) * T:(n % 2 + 1) * T], S[:, 1, T:2 * T], ACT.Exp, scale=-1.0)\
                   .then_inc(ml_em, 1)

            def ml_den(l, h):
                n = HEADS * l + h
                act.wait_ge(ml_num, n + 1)
                act.activation(work[:, 2 * T:3 * T], S[:, 3, 0:T], ACT.Abs).then_inc(ml_abs, 1)

            def mixer(l):
                for i, (kind, j) in enumerate(MIX_UNITS):
                    if i == KV_NORM:
                        root_mean(2 * l)
                    for h in (mix_halves(l)[0] + 2 * i + NW, mix_halves(l)[0] + 2 * i + NW + 1):
                        if h < mix_halves(l)[1]:
                            split_high(h)
                    if i == 2:
                        square(2 * l)
                    if i == KV_NORM:
                        high_parts(h_ready, 8 * (2 * l), hT, mix_parts)
                    if kind == "kv" and j < 4:
                        copy(kmem[:, 2 * j:2 * j + 2, :], None, "kv", l, j)
                    if kind == "ax":
                        copy(ax_pad[:, 2 * j:2 * j + 2, PAD:PAD + T],
                             lambda b: b[:, :].rearrange("p (k t) -> p k t", k=2), "ax", l, j)
                act.wait_ge(abs_f, l + 1)
                act.activation(rows[3], rows[2], ACT.Exp, scale=-1.0).then_inc(exp_f, 1)
                for j in range(4):
                    copy(qxa[:, 2 * j:2 * j + 2, :], None, "qa", l, j)
                for n, (kind, j) in enumerate(MEM_SLOTS):
                    if kind == "o":
                        gated(l, kind, j, ACT.Sigmoid, ogate[:, 2 * j:2 * j + 2, :])
                    else:
                        gated(l, kind, j, ACT.Gelu_apprx_tanh, ygelu[:, 2 * j:2 * j + 2, :])
                    if 1 <= n < 1 + HEADS:
                        take_over(("mem", l, n - 1))
                    if n < HEADS:
                        exps(("mem", l, n))
                act.wait_ge(conv_ml, l + 1)
                act.activation(cml, cml, ACT.Silu).then_inc(silu_ml, 1)
                for name, to, bias_name in (("rga", ra, "rg_b_a"), ("rgx", ib, "rg_b_x")):
                    for g in range(4):
                        two_biased(lambda m: to[:, 2 * g + m, :], (name, l, g), ACT.Sigmoid,
                                   lambda m: vec(bias_name, l)[:, 2 * g + m:2 * g + m + 1])
                if l == 0:
                    act.wait_ge(lam_done, 1)
                evacuated(act, "rga", l, 3)
                act.wait_ge(conv_rg, l + 1)
                for k in range(KD):
                    c = 8 * l + k
                    act.activation(tanh_t[:, k, :], ra[:, k, :], ACT.Tanh, scale=softp[:, 0, c:c + 1])
                for k in range(KD):
                    c = 8 * l + k
                    last = act.activation(ra[:, k, :], ra[:, k, :], ACT.Exp, scale=softp[:, 1, c:c + 1])
                last.then_inc(decay, 1)
                for g in range(4):
                    copy(vml[:, :, g * 256:(g + 1) * 256], lambda b: b[:, :].rearrange("p (m c) -> p m c", m=TT),
                         "mlv", l, g)
                act.wait_ge(rg_s, l + 1)
                act.activation(pages[17], pages[17], ACT.Sqrt, scale=2.0).then_inc(rg_root, 1)
                for j in range(12):
                    if j == 0:
                        act.wait_ge(a_ready, l + 1)
                    if j == 8:
                        act.wait_ge(rg_done, l + 1)
                    g, q = j // 4, j % 4
                    two_biased(lambda m: gates[g][:, 2 * q + m, :], ("gt", l, j), ACT.Sigmoid,
                               lambda m: vec("b_merge", l, 24)[:, 2 * j + m:2 * j + m + 1])
                    if ML_FIRST + 2 <= j < ML_FIRST + 2 + HEADS:
                        ml_den(l, j - ML_FIRST - 2)
                    if ML_FIRST <= j < ML_FIRST + HEADS:
                        ml_exps(l, j - ML_FIRST)
                    if j == 9:
                        for k in range(KD):
                            act.activation(rg_parts["x_hi"][:, k, :], ygelu[:, k, :], ACT.Copy).then_inc(h_hi, 1)
                    if j == 10:
                        split_ahead(branch_halves(l)[0])
                act.wait_ge(ml_head, HEADS * (l + 1))
                act.wait_ge(rg_done, l + 1)
                act.activation(sq, hn, ACT.Square).then_inc(ml_sq, 1)
                evacuated(act, "pv", STEP["mem", l, 3])
                for k in range(KD):
                    act.activation(xa_parts["x_hi"][:, k, :], yxa[:, k, :], ACT.Copy).then_inc(h_hi, 1)

                def branch_split(i):
                    for h in (branch_halves(l)[0] + 2 * i + NW, branch_halves(l)[0] + 2 * i + NW + 1):
                        if h < branch_halves(l)[1]:
                            split_high(h)

                for i in range(4):
                    branch_split(i)
                for j in range(2):
                    b = filled(act, "mlsum", l, j)
                    act.activation(ml_root[:, j * 512:(j + 1) * 512], b[:, :], ACT.Sqrt, bias=eps_t[:, :],
                                   scale=1.0 / 256).then_inc(freed("mlsum", l, j), 1)
                for i in range(4, 8):
                    branch_split(i)
                square(2 * l + 1)
                root_mean(2 * l + 1)

            act.wait_ge(first_loaded, 16 * len(FIRST_LOADS))
            act.wait_ge(init_done, 1)
            for q in range(4):
                act.activation(sq_mem[:, 2 * q:2 * q + 2, :], memT[:, 2 * q:2 * q + 2, :], ACT.Square)\
                   .then_inc(memsq, 1)
            for to, of in SMALL_LOADS:
                act.dma_start(to, of).then_inc(small_loaded, 16)
            b = filled(act, "msum")
            act.activation(mem_rstd[:, :], b[:, 0:T], ACT.Sqrt, bias=eps_t[:, :], scale=1.0 / D)\
               .then_inc(freed("msum"), 1)
            act.wait_ge(lam_abs, 1)
            act.activation(softp[:, 1, :], softp[:, 0, :], ACT.Exp, scale=-1.0).then_inc(lam_exp, 1)
            split_high(mix_halves(0)[0])
            split_high(mix_halves(0)[0] + 1)
            high_parts(memn_ready, 0, memn, mem_parts)
            split_high(mix_halves(0)[0] + 2)
            mixer(0)
            hidden(0, N_FFN0)
            act.wait_ge(hid_split, FF1)
            split_ahead(mix_halves(1)[0])
            high_parts(memn_ready, 8, memn, mem_parts)
            mixer(1)

            act.wait_ge(gate_arg, 1)
            act.activation(gv[:, :, 1:2], gv[:, :, 0:1], ACT.Exp).then_inc(gate_exp, 1)
            for j in range(4):
                copy(htok[:, j // 2, (j % 2) * 512:(j % 2 + 1) * 512], None, "htok", j)

            def experts(x):
                def gathered_half(count):
                    act.wait_ge(x.gathered, count)
                    act.activation(xg[:, 0:4, :], S[:, 2, :].rearrange("p (k t) -> p k t", k=4), ACT.Copy)\
                       .then_inc(x.xg_ready, 1)

                gathered_half(1)
                with act.Fori(0, EXPERTS) as e:
                    for j in range(FF1):
                        if j >= 4:
                            o = x.w(1, j - 4)
                            act.wait_ge(x.bank_free[o % NB], e * (MOE_OUTS // NB) + o // NB + 1)
                        o = x.w(0, j)
                        act.wait_ge(x.bank_full, e * MOE_OUTS + o + 1)
                        act.activation(silu_tmp[:, j % 4, 0:2 * CAP], O[o % NB][:, 0:2 * CAP], ACT.Silu)\
                           .then_inc(x.bank_free[o % NB], 1)
                    gathered_half(e + 2)
                    act.wait_ge(x.acc_units, e * FF1 + x.acc + FF1)
                    act.activation(y_tok[:, 0:512], S[:, 0, :], ACT.Copy).then_inc(x.y_ready, 1)

            experts(main)
            act.wait_ge(routed, 1)
            with act.If(act.value_load(flag[0:1, 0:1], min_val=0, max_val=1) != 0):
                experts(again)

            split_ahead(half_range(1)[0])
            square(N_FINAL1)
            act.dma_start(onehot, a["onehot"]).then_inc(table_loaded, 16)
            root_mean(N_FINAL1)
            square(N_FFN1B)
            root_mean(N_FFN1B)
            for g in range(GROUPS):
                copy(brow[:, g, :], lambda b: b[0:HA, :], "brow", g)
            for g in range(GROUPS):
                evacuated(act, "brow", g)
            act.dma_start(brow_dram.rearrange("(g h) m -> h g m", g=GROUPS), brow).then_inc(rows_stored, 16)
            act.wait_ge(rows_stored, 16)
            for g in range(GROUPS):
                shifted = bass.AP(tensor=brow_dram.tensor, offset=g * HA * 512, ap=[[1, P], [512, HA], [1, 384]])
                act.dma_start(brevs[g], shifted).then_inc(rows_loaded[g], 16)
            hidden(1, N_FFN1B)
            square(N_MIXB)
            split_ahead(plan.half_of["qd", 0])
            for h in range(GROUPS * HA):
                if h == BIAS_NORM:
                    root_mean(N_MIXB)
                copy(bias[:, h, :], lambda b: b[:, 0:384], "bias", h)
            high_parts(h_ready, 8 * N_MIXB, hT, dil)
            for i, (kind, j) in enumerate(DIL_UNITS):
                for h in (plan.half_of[kind, j] + NW, plan.half_of[kind, j] + NW + 1):
                    if h < plan.half_of[DIL_UNITS[-1]] + 2:
                        split_high(h)
                if kind != "vd":
                    copy({"qd": qd, "kd": kd}[kind][:, 2 * j:2 * j + 2, :], None, kind, j)
            for halves, summed, _turned, s, t, v in slots_b():
                kind, j = next((unit for unit, m in halves if m == 1), (None, None))
                if kind in ("qb", "kb"):
                    c = j if kind == "qb" else 4
                    copy(qk[:, c * 512:(c + 1) * 512], None, kind, j)
                    evacuated(act, kind, j)
                    act.activation(scr[:, c * 512:(c + 1) * 512], qk[:, c * 512:(c + 1) * 512], ACT.Square)\
                       .then_inc(qk_sq, 1)
                if kind == "vb":
                    copy(vb, lambda b: b[:, :].rearrange("p (m c) -> p m c", m=TT), kind, j)
                if kind == "gate":
                    b = filled(act, kind, j)
                    for m in range(2):
                        c = 2 * j + m
                        last = act.activation(gate2[:, c * T:(c + 1) * T], b[:, m * T:(m + 1) * T], ACT.Sigmoid,
                                              bias=vec("b_gate_2", None, 16)[:, c:c + 1])
                    last.then_inc(freed(kind, j), 1)
                if summed is not None:
                    c, b = summed, filled(act, "qksum", summed)
                    act.activation(scr[:, c * 512:(c + 1) * 512], b[:, :], ACT.Sqrt, bias=eps_t[:, :],
                                   scale=1.0 / P).then_inc(freed("qksum", c), 1)
                if t:
                    take_over(t)
                if s:
                    exps(s)
            square(N_FFN2B)
            root_mean(N_FFN2B)
            hidden(2, N_FFN2B)
            square(N_FINALB)
            root_mean(N_FINALB)
            for q in range(4):
                act.wait_ge(h_ready, 8 * N_FINALB + 2 * q + 2)
                act.dma_start(out[:, 2 * q:2 * q + 2, :], hT[:, 2 * q:2 * q + 2, :]).then_inc(stored, 16)
            act.wait_ge(stored, 64)

        @block.gpsimd
        def _(pool):
            def masks(l):
                for h in range(HEADS):
                    n = HEADS * l + h
                    e = probs[:, n % 2, 0:3 * P].rearrange("p (b j) -> p b j", b=3)[:, 0:3:2, :]
                    pool.wait_ge(ml_exp, n + 1)
                    pool.affine_select(out=e, in_=e, pattern=[[0, 2], [1, P]], compare_op=ALU.is_ge, fill=0.0,
                                       base=0, channel_multiplier=-1).then_inc(ml_mask, 1)

            def low_parts(n, of, x):
                for k in range(KD):
                    pool.wait_ge(h_hi, 8 * n + k + 1)
                    pool.tensor_tensor(x["x_lo"][:, k, :], of[:, k, :], x["x_hi"][:, k, :], ALU.subtract)\
                        .then_inc(h_lo, 1)

            for l in range(2):
                low_parts(X_MEM[l], memn, mem_parts)
                low_parts(X_MIX[l], hT, mix_parts)
                masks(l)
                low_parts(X_RG[l], ygelu, rg_parts)
                low_parts(X_XA[l], yxa, xa_parts)
                low_parts(X_FFN[l], hT, FFN[l])
            low_parts(X_DIL, hT, dil)
            low_parts(X_FFN[2], hT, FFN[2])

        @block.vector
        def _(dve):
            steps = [0]

            def step(ins):
                steps[0] += 1
                ins.then_inc(dve_step, 1)
                dve.wait_ge(dve_step, steps[0])

            def log1p_half(q, e, z, z2):
                step(dve.tensor_scalar(z, e, 2.0, None, ALU.add))
                step(dve.reciprocal(z, z))
                step(dve.tensor_tensor(z, z, e, ALU.mult))
                step(dve.tensor_tensor(z2, z, z, ALU.mult))
                step(dve.tensor_scalar(q, z2, 1.0 / (2 * SERIES + 1), None, ALU.mult))
                for k in range(SERIES - 1, 0, -1):
                    step(dve.scalar_tensor_tensor(q, q, 1.0 / (2 * k + 1), z2, ALU.add, ALU.mult))
                step(dve.scalar_tensor_tensor(q, q, 1.0, z, ALU.add, ALU.mult))

            def norm(n, to):
                evacuated(dve, "nsum", n)
                step(dve.reciprocal(root[:, :], root[:, :]))
                g = vec(*NORM_G[n])
                for k in range(KD):
                    dve.scalar_tensor_tensor(to[:, k, :], xT[:, k, :], g[:, k:k + 1], root[:, :], ALU.mult, ALU.mult)\
                       .then_inc(h_ready, 1)

            def sum_squares(n):
                assert n in SUMMED
                s = (sq if n <= N_FINAL1 else sq_b)
                first, second_, third = [s[:, 2 * q:2 * q + 2, :] for q in range(3)]
                dve.wait_ge(squares, 4 * n + 2)
                step(dve.tensor_tensor(first, first, second_, ALU.add))
                dve.wait_ge(squares, 4 * n + 3)
                dve.tensor_tensor(first, first, third, ALU.add).then_inc(sq_sum, 1)

            def norm_memory(l, *only):
                g = vec("mem_norm_g", l)
                for k in only or range(KD):
                    dve.scalar_tensor_tensor(memn[:, k, :], memT[:, k, :], g[:, k:k + 1], mem_rstd[:, :], ALU.mult,
                                             ALU.mult).then_inc(memn_ready, 1)

            def quarter(q):
                return xT[:, 2 * q:2 * q + 2, :].rearrange("p k t -> p (k t)")

            def split_low(h):
                dve.wait_ge(w_hi, h + 1)
                dve.tensor_tensor(part(h, "w_lo"), half_of_unit(h), part(h, "w_hi"), ALU.subtract).then_inc(w_lo, 1)

            def split_ahead(first):
                for h in range(first, first + NW):
                    split_low(h)

            def hidden(f):
                x = FFN[f]
                first, end = half_range(f)
                for i in range(3 * x["ff"]):
                    for h in (first + 2 * i + NW, first + 2 * i + NW + 1):
                        if h < end:
                            split_low(h)
                    if f == 0 and 0 <= i - 2 * x["ff"] < KD:
                        norm_memory(1, i - 2 * x["ff"])
                    if i < 2 * x["ff"] and i % 2 == 1:
                        j = i // 2
                        hid_, hi, lo = [x[n][:, 2 * j:2 * j + 2, :].rearrange("p k t -> p (k t)")
                                        for n in ("hid", "hid_hi", "hid_lo")]
                        evacuated(dve, "w1", f, j)
                        b = filled(dve, "w3", f, j)
                        dve.tensor_tensor(hid_, silu_tmp[:, j % 4, :], b[:, :], ALU.mult).then_inc(freed("w3", f, j), 1)
                        evacuated(dve, "w3", f, j)
                        step(dve.tensor_copy(hi, hid_))
                        dve.tensor_tensor(lo, hid_, hi, ALU.subtract).then_inc(hid_split, 1)

            def second(ffn, count, weight, n):
                for q in range(4):
                    if q < 3:
                        dve.wait_ge(acc_quarter, 3 * ffn + q + 1)
                    else:
                        if n == N_MIX1:
                            split_ahead(mix_halves(1)[0])
                        else:
                            sum_squares(n)
                        dve.wait_ge(acc_units, count)
                    dve.scalar_tensor_tensor(quarter(q), S[:, q, :], weight, quarter(q), ALU.mult, ALU.add)\
                       .then_inc(x_added, 1)

            def mixed(l, n):
                for q in range(4):
                    if q == 3:
                        if n in FFN_OF:
                            split_ahead(half_range(FFN_OF[n])[0])
                        sum_squares(n)
                    b = filled(dve, "wout", l, q)
                    dve.tensor_tensor(quarter(q), quarter(q), b[:, :], ALU.add).then_inc(freed("wout", l, q), 1)

            def convolve(x, to, w, bias_, done):
                for k in range(KD):
                    last = dve.tensor_scalar(to[:, k, :], x[:, k, 0:T], w[:, k:k + 1], bias_[:, k:k + 1], ALU.mult,
                                             ALU.add)
                step(last)
                for tap in range(1, PAD + 1):
                    for k in range(KD):
                        last = dve.scalar_tensor_tensor(to[:, k, :], x[:, k, tap:tap + T],
                                                        w[:, tap * KD + k:tap * KD + k + 1], to[:, k, :], ALU.mult,
                                                        ALU.add)
                    if tap < PAD:
                        step(last)
                last.then_inc(done, 1)

            def maxima(s):
                n = STEP[s]
                par = n % 2
                dve.wait_ge(scores, n + 1)
                if s[0] == "dil":
                    h, m = s[1:]
                    dve.wait_ge(exped, n)
                    shifts = bias.rearrange("p (g h) m -> p g h m", g=GROUPS)[:, :, h, P * (1 - m):P * (1 - m) + T]
                    dve.scalar_tensor_tensor(work[:, :].rearrange("p (g t) -> p g t", g=GROUPS),
                                             S2[:, 0:768].rearrange("p (g t) -> p g t", g=GROUPS), DA ** -0.5,
                                             shifts, ALU.mult, ALU.add).then_inc(scores_free, 1)
                    dve.wait_ge(scores_free, n + 1)
                    step(dve.reduce_max(smax[:, par, 0, 0:1], work[:, :], AXX))
                    dve.tensor_scalar(smax[:, par, 1, 0:1], smax[:, par, 0, 0:1], -1.0, None, ALU.mult)\
                       .then_inc(maxed, 1)
                    return
                scale = 256 ** -0.5 if s[0] == "mem" else P ** -0.5
                step(dve.reduce_max(smax[:, par, 0, :], S[:, 0, :].rearrange("p (m t) -> p m t", m=TT), AXX))
                dve.tensor_scalar(smax[:, par, 1, :], smax[:, par, 0, :], -scale, None, ALU.mult).then_inc(maxed, 1)

            def normalise(s):
                n = STEP[s]
                par = n % 2
                dve.wait_ge(exped, n + 1)
                if s[0] == "dil":
                    step(dve.reciprocal(ssum[:, par, 1, 0:1], ssum[:, par, 0, 0:1]))
                    dve.tensor_scalar(probs[:, par, :], probs[:, par, :], ssum[:, par, 1, 0:1], None, ALU.mult)\
                       .then_inc(probs_ready, 1)
                    return
                dve.reciprocal(ssum[:, par, 1, :], ssum[:, par, 0, :]).then_inc(scores_free, 1)
                dve.wait_ge(scores_free, n + 1)
                for m in range(TT):
                    c = slice(m * T, (m + 1) * T)
                    last = dve.tensor_scalar(probs[:, par, c], probs[:, par, c], ssum[:, par, 1, m:m + 1], None,
                                             ALU.mult)
                last.then_inc(probs_ready, 1)

            def values(s):
                n = STEP[s]
                b = filled(dve, "pv", n)
                if s[0] == "mem":
                    h = s[2]
                    ins = dve.tensor_copy(yxa[:, 2 * h:2 * h + 2, :].rearrange("p k t -> p (k t)"), b[:, :])
                elif s[0] == "dil":
                    h, m = s[1:]
                    r = DA * (h % 2)
                    ins = dve.tensor_copy(o_a[r:r + DA, h // 2, m * P:(m + 1) * P], b[r:r + DA, 0:P])
                else:
                    ins = dve.tensor_copy(o_b[:, s[1], :], b[:, 0:T])
                ins.then_inc(freed("pv", n), 1)

            def gate_rows(l):
                b = filled(dve, "if", l)
                bi, bf = vec("ml_b_i", l, 1)[0:4, :], vec("ml_b_f", l, 1)[0:4, :]
                i_, f_, af, e_, z, z2, q, u = rows
                dve.tensor_scalar(i_, b[0:4, 0:T], bi, None, ALU.add)
                dve.tensor_scalar(f_, b[0:4, T:2 * T], bf, None, ALU.add).then_inc(freed("if", l), 1)
                evacuated(dve, "if", l)
                dve.scalar_tensor_tensor(af, f_, -1.0, f_, ALU.mult, ALU.max).then_inc(abs_f, 1)
                dve.wait_ge(exp_f, l + 1)
                log1p_half(q, e_, z, z2)
                step(dve.tensor_scalar(u, f_, 0.0, None, ALU.min))
                step(dve.scalar_tensor_tensor(u, q, -2.0, u, ALU.mult, ALU.add))
                step(dve.tensor_tensor_scan(z, ones_row[0:4, :], u, 0.0, ALU.mult, ALU.add))
                step(dve.tensor_tensor(arow, i_, z, ALU.subtract))
                step(dve.tensor_tensor_scan(mrow[:, 0, :], arow, arow, 0.0, ALU.max, ALU.max))
                dve.tensor_tensor(mrow[:, 1, :], mrow[:, 0, :], z, ALU.add).then_inc(a_ready, 1)

            def ml_args(l, h):
                n = HEADS * l + h
                dve.wait_ge(ml_scores, n + 1)
                if n >= 2:
                    dve.wait_ge(ml_num, n - 1)
                w = probs[:, n % 2, :]
                for s in range(TT):
                    last = dve.tensor_scalar(w[:, s * T:s * T + T - s * P], S[:, 1, s * P:T], acol[:, s, h:h + 1], 0.0,
                                             ALU.subtract, ALU.max)
                last.then_inc(ml_arg, 1)

            def ml_weights(l, h):
                n = HEADS * l + h
                dve.wait_ge(ml_mask, n + 1)
                w = probs[:, n % 2, 0:3 * P]
                dve.tensor_tensor(w, w, S[:, 0, 0:3 * P], ALU.mult).then_inc(ml_w, 1)

            def ml_out(l, h):
                n = HEADS * l + h
                dve.wait_ge(ml_em, n + 1)
                dve.wait_ge(ml_abs, n + 1)
                r = work[:, (n % 2) * T:(n % 2 + 1) * T]
                step(dve.tensor_tensor(r, r, work[:, 2 * T:3 * T], ALU.max))
                step(dve.reciprocal(r, r))
                for m in range(2):
                    last = dve.tensor_tensor(hn[:, 2 * h + m, :], S[:, 2, m * T:(m + 1) * T], r, ALU.mult)
                step(last)
                dve.tensor_tensor(hn[:, 2 * h:2 * h + 2, :], hn[:, 2 * h:2 * h + 2, :], ogate[:, 2 * h:2 * h + 2, :],
                                  ALU.mult).then_inc(ml_head, 1)

            def branch_split(l, i):
                for h in (branch_halves(l)[0] + 2 * i + NW, branch_halves(l)[0] + 2 * i + NW + 1):
                    if h < branch_halves(l)[1]:
                        split_low(h)

            def merge(l, branch):
                for j in range(4):
                    c = slice(2 * j, 2 * j + 2)
                    g = gates[branch][:, c, :].rearrange("p k t -> p (k t)")
                    to = merged[:, c, :].rearrange("p k t -> p (k t)")
                    name = ("br", l, 4 * branch + j)
                    if branch == 0:
                        branch_split(l, j)
                    if branch == 2 and j < 3:
                        branch_split(l, 5 + j)
                    evacuated(dve, "gt", l, 4 * branch + j)
                    b = filled(dve, *name)
                    if branch == 0:
                        dve.tensor_tensor(to, g, b[:, :], ALU.mult).then_inc(freed(*name), 1)
                        evacuated(dve, *name)
                        continue
                    dve.tensor_tensor(g, g, b[:, :], ALU.mult).then_inc(freed(*name), 1)
                    evacuated(dve, *name)
                    if branch == 2:
                        step(dve.tensor_tensor(to, to, g, ALU.add))
                    else:
                        dve.tensor_tensor(to, to, g, ALU.add).then_inc(merged_ready, 1)

            def mixer(l):
                for i, (kind, j) in enumerate(MIX_UNITS):
                    if i == KV_NORM:
                        norm(2 * l, hT)
                    for h in (mix_halves(l)[0] + 2 * i + NW, mix_halves(l)[0] + 2 * i + NW + 1):
                        if h < mix_halves(l)[1]:
                            split_low(h)
                    if i == 4:
                        sum_squares(2 * l)
                    if kind == "kv" and j >= 4:
                        b = filled(dve, "kv", l, j)
                        h = j - 4
                        dve.tensor_copy(vmem[:, :, h * 256:(h + 1) * 256],
                                        b[:, :].rearrange("p (m c) -> p m c", m=TT)).then_inc(freed("kv", l, j), 1)
                    if kind == "mu":
                        b = filled(dve, "mu", l, j)
                        dve.tensor_copy(mu_pad[:, 2 * j:2 * j + 2, PAD:PAD + T],
                                        b[:, :].rearrange("p (k t) -> p k t", k=2)).then_inc(freed("mu", l, j), 1)
                dve.memset(ax_pad[:, :, 0:PAD], 0.0)
                step(dve.memset(mu_pad[:, :, 0:PAD], 0.0))
                gate_rows(l)
                for j in range(4):
                    evacuated(dve, "ax", l, j)
                convolve(ax_pad, xc, vec("conv_rg_w", l, 32), vec("conv_rg_b", l), conv_rg)
                for j in range(4):
                    evacuated(dve, "mu", l, j)
                convolve(mu_pad, cml, vec("conv_ml_w", l, 32), vec("conv_ml_b", l), conv_ml)
                for n in range(HEADS + 2):
                    if n < HEADS:
                        maxima(("mem", l, n))
                        normalise(("mem", l, n))
                    if n >= 2:
                        values(("mem", l, n - 2))
                for g in range(4):
                    b = filled(dve, "mlq", l, g)
                    dve.tensor_copy(qml[:, 2 * g:2 * g + 2, :].rearrange("p k t -> p (k t)"), b[:, :])\
                       .then_inc(freed("mlq", l, g), 1)
                for g in range(4):
                    b = filled(dve, "mlk", l, g)
                    dve.tensor_scalar(kml[:, 2 * g:2 * g + 2, :].rearrange("p k t -> p (k t)"), b[:, :], 256 ** -0.5,
                                      None, ALU.mult).then_inc(freed("mlk", l, g), 1)
                b = filled(dve, "acol", l)
                dve.tensor_copy(acol[:, :, :], b[:, 0:8].rearrange("p (m h) -> p m h", m=TT))\
                   .then_inc(freed("acol", l), 1)
                i_flat, t_flat, s_flat = pages[14], tanh_v, pages[17]
                dve.wait_ge(decay, l + 1)
                step(dve.tensor_scalar(s_flat, t_flat, 1.0, None, ALU.add))
                step(dve.reciprocal(s_flat, s_flat))
                dve.scalar_tensor_tensor(s_flat, t_flat, 1e-34, s_flat, ALU.max, ALU.mult).then_inc(rg_s, 1)
                evacuated(dve, "rgx", l, 3)
                step(dve.tensor_tensor(i_flat, i_flat, pages[11], ALU.mult))
                dve.wait_ge(rg_root, l + 1)
                step(dve.tensor_tensor(i_flat, i_flat, s_flat, ALU.mult))
                for k in range(KD):
                    last = dve.tensor_tensor_scan(tanh_t[:, k, :], ra[:, k, :], ib[:, k, :], 0.0, ALU.mult, ALU.add)
                step(last)
                evacuated(dve, "ay", l, 3)
                dve.tensor_tensor(pages[10], pages[10], t_flat, ALU.mult).then_inc(rg_done, 1)
                evacuated(dve, "acol", l)
                evacuated(dve, "o", l, 3)
                for h in range(HEADS + 2):
                    if h < HEADS:
                        ml_args(l, h)
                        ml_weights(l, h)
                    if h >= 2:
                        ml_out(l, h - 2)
                split_ahead(branch_halves(l)[0])
                merge(l, 0)
                for j in range(2):
                    evacuated(dve, "mlsum", l, j)
                dve.reciprocal(ml_root[:, 0:512], ml_root[:, 0:512])
                branch_split(l, 4)
                step(dve.reciprocal(ml_root[:, 512:1024], ml_root[:, 512:1024]))
                g = vec("ml_norm_g", l)
                for k in range(KD):
                    last = dve.scalar_tensor_tensor(hn[:, k, :], hn[:, k, :], g[:, k:k + 1],
                                                    ml_root[:, (k // 2) * T:(k // 2 + 1) * T], ALU.mult, ALU.mult)
                last.then_inc(ml_done, 1)
                merge(l, 2)
                merge(l, 1)
                mixed(l, 2 * l + 1)
                for q in range(4):
                    evacuated(dve, "wout", l, q)
                norm(2 * l + 1, hT)

            dve.memset(ones_row[:, :], 1.0)
            dve.memset(eps_t[:, :], EPS).then_inc(init_done, 1)
            dve.wait_ge(first_loaded, 16 * len(FIRST_LOADS))
            for l in range(2):
                lam = vec("rg_lambda", l)
                last = dve.scalar_tensor_tensor(softp[:, 0, 8 * l:8 * l + 8], lam, -1.0, lam, ALU.mult, ALU.max)
            last.then_inc(lam_abs, 1)
            evacuated(dve, "msum")
            step(dve.reciprocal(mem_rstd[:, :], mem_rstd[:, :]))
            norm_memory(0, 0, 1, 2, 3)
            split_low(mix_halves(0)[0])
            norm_memory(0, 4, 5, 6, 7)
            split_low(mix_halves(0)[0] + 1)
            split_low(mix_halves(0)[0] + 2)
            dve.wait_ge(lam_exp, 1)
            log1p_half(softp[:, 0, :], softp[:, 1, :], softp[:, 2, :], softp[:, 3, :])
            for l in range(2):
                last = dve.tensor_scalar(softp[:, 2, 8 * l:8 * l + 8], vec("rg_lambda", l), -1.0, 0.0, ALU.mult, ALU.max)
            step(last)
            step(dve.scalar_tensor_tensor(softp[:, 0, :], softp[:, 0, :], 2.0, softp[:, 2, :], ALU.mult, ALU.add))
            step(dve.tensor_scalar(softp[:, 1, :], softp[:, 0, :], -RG_C, None, ALU.mult))
            dve.tensor_scalar(softp[:, 0, :], softp[:, 0, :], RG_C, None, ALU.mult).then_inc(lam_done, 1)
            mixer(0)
            hidden(0)
            second(0, FF1, 1.0, N_MIX1)
            mixer(1)

            L, top, m_, c_, f1, f2, picked, gate, rank, left = [lg[:, n, :, :] for n in range(10)]
            b = filled(dve, "logit")
            dve.tensor_tensor(L[:, 0, :], b[:, 0:8], vec("router_b"), ALU.add)
            dve.tensor_tensor(L[:, 1, :], b[:, 8:16], vec("router_b"), ALU.add).then_inc(freed("logit"), 1)
            evacuated(dve, "logit")
            for m in range(TT):
                last = dve.max(top[:, m, :], L[:, m, :])
            step(last)
            dve.tensor_tensor(gv[:, :, 0:1], top[:, :, 1:2], top[:, :, 0:1], ALU.subtract).then_inc(gate_arg, 1)

            def first_of(f):
                for m in range(TT):
                    last = dve.tensor_tensor_scan(c_[:, m, :], ones_row[:, 0:8], m_[:, m, :], 0.0, ALU.mult, ALU.add)
                step(last)
                step(dve.tensor_tensor(c_, c_, m_, ALU.mult))
                step(dve.tensor_scalar(f, c_, 1.0, None, ALU.is_equal))

            for m in range(TT):
                last = dve.tensor_scalar(m_[:, m, :], L[:, m, :], top[:, m, 0:1], None, ALU.is_equal)
            step(last)
            first_of(f1)
            step(dve.tensor_scalar(left, f1, -1.0, 1.0, ALU.mult, ALU.add))
            for m in range(TT):
                last = dve.scalar_tensor_tensor(m_[:, m, :], L[:, m, :], top[:, m, 1:2], left[:, m, :], ALU.is_equal,
                                                ALU.mult)
            step(last)
            first_of(f2)
            dve.tensor_tensor(picked, f1, f2, ALU.add).then_inc(sel_ready, 1)
            dve.wait_ge(gate_exp, 1)
            step(dve.tensor_scalar(gv[:, :, 2:3], gv[:, :, 1:2], 1.0, None, ALU.add))
            step(dve.reciprocal(gv[:, :, 3:4], gv[:, :, 2:3]))
            step(dve.tensor_tensor(gv[:, :, 4:5], gv[:, :, 1:2], gv[:, :, 3:4], ALU.mult))
            for m in range(TT):
                last = dve.tensor_scalar(gate[:, m, :], f1[:, m, :], gv[:, m, 3:4], None, ALU.mult)
            step(last)
            for m in range(TT):
                last = dve.scalar_tensor_tensor(gate[:, m, :], f2[:, m, :], gv[:, m, 4:5], gate[:, m, :], ALU.mult,
                                                ALU.add)
            step(last)
            b = filled(dve, "rank")
            step(dve.scalar_tensor_tensor(rank, b[:, 0:16].rearrange("p (m e) -> p m e", m=TT), 1.0, picked, ALU.add,
                                          ALU.mult))
            dve.reduce_max(cnt[:, 0:1], b[:, 16:24], AXX).then_inc(freed("rank"), 1)
            evacuated(dve, "rank")
            dve.tensor_scalar(flag[:, :], cnt[:, 0:1], float(CAP), None, ALU.is_gt).then_inc(routed, 1)
            step(dve.tensor_scalar(rank, rank, -1.0, None, ALU.add))

            def pick(x):
                dve.memset(GT[:, 0:T], 0.0)
                for half in range(2):
                    dve.memset(y_tok[:, half * 512:(half + 1) * 512], 0.0).then_inc(x.y_ready, 1)
                dve.memset(Pall[:, :, EXPERTS * CAP:(EXPERTS + 1) * CAP], 0.0)
                slots_of(0).then_inc(picks, 1)
                for m in range(TT):
                    for e in range(EXPERTS):
                        last = dve.tensor_scalar(Pg[:, m, e, :], iota, rank[:, m, e:e + 1], gate[:, m, e:e + 1],
                                                 ALU.is_equal, ALU.mult)
                last.then_inc(picks, 1)

            def slots_of(e):
                for m in range(TT):
                    last = dve.tensor_scalar(Pall[:, m, e * CAP:(e + 1) * CAP], iota, rank[:, m, e:e + 1], None,
                                             ALU.is_equal)
                return last

            def gathered_half(x, count):
                dve.wait_ge(x.gathered, count)
                dve.tensor_copy(xg[:, 4:8, :], S[:, 3, :].rearrange("p (k t) -> p k t", k=4))\
                   .then_inc(x.xg_ready, 1)

            def gate_columns(x, o):
                gathered_half(x, 1)
                for j in range(4):
                    dve.wait_ge(x.bank_full, o + j + 1)
                    dve.tensor_copy(GT[:, T * (1 + 2 * j):T * (3 + 2 * j)], O[(o + j) % NB][:, :])\
                       .then_inc(x.bank_free[(o + j) % NB], 1)
                for e in range(1, EXPERTS):
                    last = slots_of(e)
                last.then_inc(picks, 1)

            def experts(x):
                with dve.Fori(0, EXPERTS) as e:
                    for j in range(FF1):
                        o1, o = x.w(0, j), x.w(1, j)
                        dve.wait_ge(x.bank_free[o1 % NB], e * (MOE_OUTS // NB) + o1 // NB + 1)
                        dve.wait_ge(x.bank_full, e * MOE_OUTS + o + 1)
                        dve.tensor_tensor(hid_e[:, 2 * j:2 * j + 2, :].rearrange("p k t -> p (k t)"),
                                          silu_tmp[:, j % 4, 0:2 * CAP], O[o % NB][:, 0:2 * CAP], ALU.mult)\
                           .then_inc(x.bank_free[o % NB], 1)
                        if j == 0:
                            for q in range(4):
                                o = x.comb(q)
                                dve.wait_ge(x.bank_full, e * MOE_OUTS + o + 1)
                                dve.tensor_tensor(quarter(q), quarter(q), O[o % NB][:, :], ALU.add)\
                                   .then_inc(x.bank_free[o % NB], 1)
                            for q in range(4):
                                o = x.comb(q)
                                dve.wait_ge(x.bank_free[o % NB], e * (MOE_OUTS // NB) + o // NB + 1)
                    gathered_half(x, e + 2)
                    dve.wait_ge(x.acc_units, e * FF1 + x.acc + FF1)
                    dve.tensor_copy(y_tok[:, 512:1024], S[:, 1, :]).then_inc(x.y_ready, 1)
                o = x.o + EXPERTS * MOE_OUTS
                for q in range(4):
                    dve.wait_ge(x.bank_full, o + q + 1)
                    dve.tensor_tensor(quarter(q), quarter(q), O[(o + q) % NB][:, :], ALU.add)\
                       .then_inc(x.bank_free[(o + q) % NB], 1)
                for q in range(4):
                    dve.wait_ge(x.bank_free[(o + q) % NB], (o + q) // NB + 1)

            pick(main)
            gate_columns(main, plan.o["gtr", 0])
            experts(main)
            dve.wait_ge(routed, 1)
            with dve.If(dve.value_load(flag[0:1, 0:1], min_val=0, max_val=1) != 0):
                dve.tensor_scalar(rank, rank, -float(CAP), None, ALU.add).then_inc(ranks_moved, 1)
                dve.wait_ge(ranks_moved, 1)
                pick(again)
                gate_columns(again, 0)
                experts(again)
            dve.memset(cnt[:, 1:2], 0.0).then_inc(moe_done, 1)

            split_ahead(half_range(1)[0])
            norm(N_FINAL1, xT)
            dve.wait_ge(h_ready, 8 * N_FINAL1 + 8)
            norm(N_FFN1B, hT)
            hidden(1)
            acc = FF1 + EXPERTS * FF1 + FF2
            second(1, acc, 0.5, N_MIXB)
            dve.wait_ge(x_added, 8)
            split_ahead(plan.half_of["qd", 0])
            norm(N_MIXB, hT)
            for i, (kind, j) in enumerate(DIL_UNITS):
                for h in (plan.half_of[kind, j] + NW, plan.half_of[kind, j] + NW + 1):
                    if h < plan.half_of[DIL_UNITS[-1]] + 2:
                        split_low(h)
                if kind == "vd":
                    b = filled(dve, "vd", j)
                    dve.tensor_copy(vd[:, :, j * 256:(j + 1) * 256], b[:, :].rearrange("p (m c) -> p m c", m=TT))\
                       .then_inc(freed("vd", j), 1)
            for h in range(4):
                evacuated(dve, "bias", GROUPS * HA - 1 - h)
            for _halves, summed, turned, s, t, v in slots_b():
                if turned is not None:
                    c = turned
                    dve.wait_ge(qk_norm, c + 1)
                    b = filled(dve, "rot", c)
                    for m in range(2):
                        w = slice((2 * c + m) * T, (2 * c + m + 1) * T)
                        dve.tensor_tensor(qk[:, w], qk[:, w], rope[:, 0, :], ALU.mult)
                        last = dve.tensor_tensor(scr[:, w], b[:, m * T:(m + 1) * T], rope[:, 1, :], ALU.mult)
                    last.then_inc(freed("rot", c), 1)
                    evacuated(dve, "rot", c)
                    w = slice(c * 512, (c + 1) * 512)
                    dve.tensor_tensor(qk[:, w], qk[:, w], scr[:, w], ALU.add).then_inc(qk_ready, 1)
                if s:
                    maxima(s)
                    normalise(s)
                if v:
                    values(v)
                if summed is not None:
                    c = summed
                    w = slice(c * 512, (c + 1) * 512)
                    evacuated(dve, "qksum", c)
                    step(dve.reciprocal(scr[:, w], scr[:, w]))
                    g = vec("k_norm_2" if c == 4 else "q_norm_2", None, 1)
                    dve.scalar_tensor_tensor(qk[:, w], qk[:, w], g, scr[:, w], ALU.mult, ALU.mult)\
                       .then_inc(qk_norm, 1)
            acc += 2
            for j in range(4):
                evacuated(dve, "gate", j)
            dve.wait_ge(acc_units, acc)
            for q in range(4):
                w = slice(q * 512, (q + 1) * 512)
                last = dve.tensor_tensor(gate2[:, w], gate2[:, w], S[:, q, :], ALU.mult)
            last.then_inc(bra_free, 1)
            dve.wait_ge(bra_free, 1)
            for j in range(4):
                w, w1 = slice(j * 512, (j + 1) * 512), slice(2048 + j * 512, 2048 + (j + 1) * 512)
                evacuated(dve, "gate", 4 + j)
                b = filled(dve, "brb", j)
                dve.tensor_tensor(gate2[:, w1], gate2[:, w1], b[:, :], ALU.mult).then_inc(freed("brb", j), 1)
                evacuated(dve, "brb", j)
                dve.tensor_tensor(gate2[:, w], gate2[:, w], gate2[:, w1], ALU.add).then_inc(merged_ready, 1)
            mixed(2, N_FFN2B)
            for q in range(4):
                evacuated(dve, "wout", 2, q)
            norm(N_FFN2B, hT)
            hidden(2)
            acc += FF2
            second(2, acc, 0.5, N_FINALB)
            dve.wait_ge(x_added, 12)
            norm(N_FINALB, hT)



def _buckets(rel):
    n, exact = 16, 8
    a = np.abs(rel)
    af = np.maximum(a, 1).astype(np.float32)
    large = exact + (np.log(af / np.float32(exact)) / np.float32(math.log(1024 / exact))
                     * np.float32(n - exact)).astype(np.int32)
    large = np.minimum(large, n - 1)
    return np.where(rel > 0, n, 0) + np.where(a < exact, a, large)


def _constants():
    eye = np.eye(P, dtype=np.float32)
    n = np.arange(P)
    rot = np.zeros((P, P), np.float32)
    rot[n[1::2], n[0::2]] = -1.0
    rot[n[0::2], n[1::2]] = 1.0
    mats = np.concatenate([eye, np.ones((P, P), np.float32), eye[::-1], rot,
                           (n[:, None] < n[None, :]).astype(np.float32),
                           np.broadcast_to(n.astype(np.float32), (P, P))], axis=1)
    sel = np.kron(np.eye(HEADS, dtype=np.float32), np.ones((1, P), np.float32))
    t = np.arange(T)
    freq = np.float32(10000.0) ** (-np.arange(32, dtype=np.float32) / np.float32(32))
    ang = np.concatenate([(t // 64).astype(np.float32)[:, None] * freq, (t % 64).astype(np.float32)[:, None] * freq],
                         axis=-1)
    rope = np.stack([np.repeat(f(ang), 2, axis=1).T for f in (np.cos, np.sin)], axis=1).astype(np.float32)
    rel = np.arange(512) - 255
    onehot = np.zeros((33, GROUPS, 512), np.float32)
    for g, d in enumerate(DIL):
        seen = (rel % d == 0) & (np.abs(rel) <= 64 * d)
        for c in np.flatnonzero(seen):
            onehot[_buckets(rel[c:c + 1])[0], g, c] = 1.0
        onehot[32, g, ~seen] = NEG
    return {"mats": mats, "sel": sel, "rope": rope, "onehot": onehot}


def _features(v):
    v = np.asarray(v).reshape(-1, P)
    return v.T


def _columns_of(w):
    *lead, k, n = w.shape
    w = w.reshape(*lead, k // P, P, n // UC, UC)
    at = len(lead)
    w = np.moveaxis(w, (at + 2, at + 1, at), (at, at + 1, at + 2))
    return np.ascontiguousarray(w).reshape(*lead, n // UC, P, -1)


def _rows_of(w):
    *lead, f, n = w.shape
    w = w.reshape(*lead, f // 256, 2, P, n)
    w = np.swapaxes(w, len(lead) + 1, len(lead) + 2)
    return np.ascontiguousarray(w).reshape(*lead, f // 256, P, 2 * n)


def _lay_out(i):
    g = {n: np.asarray(v) for n, v in i.items()}
    cols = []
    for l in range(2):
        for name in ("norm_mix_g", "mem_norm_g", "norm_ffn_g", "conv_rg_w", "conv_rg_b", "rg_b_a", "rg_b_x",
                     "rg_lambda", "conv_ml_w", "conv_ml_b", "ml_norm_g", "b_merge"):
            cols.append(_features(g[name][l]))
        for name in ("ml_b_i", "ml_b_f"):
            cols.append(np.pad(g[name][l], (0, P - HEADS))[:, None])
    for name in ("final_norm_g", "ffn1_norm_2", "mix_norm_2", "b_gate_2", "q_norm_2", "k_norm_2", "ffn2_norm_2",
                 "final_norm_2"):
        cols.append(_features(g[name]))
    cols.append(np.broadcast_to(g["router_b"][0], (P, EXPERTS)))
    w_in = g["w_in"]
    a = {
        "xT": g["x"][0].T.reshape(KD, P, T).transpose(1, 0, 2),
        "memT": g["mem"][0].T.reshape(KD, P, T).transpose(1, 0, 2),
        "vecs": np.concatenate(cols, axis=1),
        "wif": w_in[:, :, 4096:4104].reshape(2, KD, P, 8).transpose(2, 0, 1, 3),
        "wr": g["router_w"][0].reshape(KD, P, EXPERTS).transpose(1, 0, 2),
        "btab": np.concatenate([g["rel_bias_2"], np.ones((1, 24), np.float32)]),
        "w_in": _columns_of(np.concatenate([w_in[:, :, :4096], w_in[:, :, 4104:]], axis=2)).reshape(64, P, 2048),
        "w_kv": _columns_of(g["w_kv"]).reshape(16, P, 2048),
        "moe_w1": _columns_of(g["moe_w1"][0]), "moe_w3": _columns_of(g["moe_w3"][0]),
        "moe_w2": _rows_of(g["moe_w2"][0]),
        "ffn_w1": _columns_of(g["ffn_w1"][0]), "ffn_w3": _columns_of(g["ffn_w3"][0]),
        "ffn_w2": _rows_of(g["ffn_w2"][0]),
        "w_in_2": _columns_of(g["w_in_2"][0]), "w_branch_a": _rows_of(g["w_branch_a_2"][0]),
        "w_branch_b": _columns_of(g["w_branch_b_2"][0]), "w_out_2": _columns_of(g["w_out_2"][0]),
    }
    for name in ("w_br_rg", "w_br_ml", "w_br_xa", "w_out"):
        a[name] = _columns_of(g[name]).reshape(8, P, 2048)
    for name, key in (("rga", "rg_w_a"), ("rgx", "rg_w_x"), ("mlq", "ml_w_q"), ("mlk", "ml_w_k"), ("mlv", "ml_w_v")):
        a[name] = _columns_of(g[key].reshape(2, D, UC)).reshape(2, P, 2048)
    for f in (1, 2):
        a[f"ffn{f}_w1_2"] = _columns_of(g[f"ffn{f}_w1_2"][0])
        a[f"ffn{f}_w3_2"] = _columns_of(g[f"ffn{f}_w3_2"][0])
        a[f"ffn{f}_w2_2"] = _rows_of(g[f"ffn{f}_w2_2"][0])
    a.update(_constants())
    return {n: np.ascontiguousarray(v) for n, v in a.items()}


def kernel(**inputs):
    import concourse.bacc as bacc
    from concourse.bass_utils import run_bass_kernel_spmd

    nc = bacc.Bacc("TRN2", target_bir_lowering=False, num_devices=1, dynamic_dma_scratch_size=1024)
    arrays = {}
    handles = {}
    for name, v in _lay_out(inputs).items():
        arrays[f"in_{name}"] = v
        handles[name] = nc.dram_tensor(f"in_{name}", v.shape, mybir.dt.from_np(v.dtype), kind="ExternalInput").ap()
    out = nc.dram_tensor("out", (P, KD, T), F32, kind="ExternalOutput").ap()
    build(nc, handles, out)
    r = run_bass_kernel_spmd(nc, [arrays], core_ids=[0])
    return r.results[0]["out"].transpose(1, 0, 2).reshape(D, T).T.reshape(1, T, D)
```
